# Optimizing a Trainium2 kernel written in Bass

```python
import math
import jax, jax.numpy as jnp
from jax import lax
import numpy as np

D_MODEL = 1024
BATCH = 1
SEQ = 512
DEPTH = 2

N_META = 16
GRID_W = 64
HEAD_DIM = 64
NA_WIDTH = D_MODEL // 2
NA_HEADS = NA_WIDTH // HEAD_DIM
NA_WIN_ROWS = 8
NA_WIN_COLS = 16
RWKV_WIDTH = D_MODEL // 2
RWKV_HEADS = RWKV_WIDTH // HEAD_DIM
RWKV_W_RANK = 64
RWKV_A_RANK = 64
RWKV_G_RANK = 128
MIX_WIDTH = NA_WIDTH + RWKV_WIDTH
SHIFT_COLS = 3 * RWKV_WIDTH + RWKV_W_RANK + RWKV_A_RANK + RWKV_G_RANK
IN_COLS = 3 * NA_WIDTH + SHIFT_COLS
S5_GROUP_CH = 16
S5_GROUPS = D_MODEL // S5_GROUP_CH
S5_STATE = 64
MOE_GROUPS = 4
MOE_PER_GROUP = 8
MOE_EXPERTS = MOE_GROUPS * MOE_PER_GROUP
MOE_TOP_K = 2
MOE_D_FF = D_MODEL // 2
MOE_BLOCK = 128
NORM_EPS = 1e-6
RWKV_GN_EPS = 64e-5
NEG_INF = -1e30

kernel_name = 'hybrid_na_rwkv7_s5_hmoe_encoder'

def rms_norm(x, gain):
    xf = x.astype(jnp.float32)
    y = xf * lax.rsqrt(jnp.mean(xf * xf, axis=-1, keepdims=True) + NORM_EPS)
    return (y * gain.astype(jnp.float32)).astype(x.dtype)

def centred_token_shift(p, mu):
    pad = jnp.pad(p, ((0, 0), (1, 1), (0, 0)))
    nb = 0.5 * (pad[:, :-2] + pad[:, 2:])
    return p + mu.astype(p.dtype) * (nb - p)

def neighbourhood_attention(q, k, v, rpb):
    Bsz, L, H, Dh = q.shape
    T = L - N_META
    rows = T // GRID_W
    wr = min(NA_WIN_ROWS, rows)
    scale = Dh ** -0.5
    f32 = jnp.float32
    grid = lambda t: t[:, N_META:].reshape(Bsz, rows, GRID_W, H, Dh)
    qm, km, vm = q[:, :N_META], k[:, :N_META], v[:, :N_META]
    qg, kg, vg = grid(q), grid(k), grid(v)
    r_ids = jnp.arange(rows)
    row_idx = jnp.clip(r_ids - wr // 2, 0, rows - wr)[:, None] + jnp.arange(wr)[None, :]
    kb = kg[:, row_idx].reshape(Bsz, rows, wr * GRID_W, H, Dh)
    vb = vg[:, row_idx].reshape(Bsz, rows, wr * GRID_W, H, Dh)
    c_ids = jnp.arange(GRID_W)
    c_start = jnp.clip(c_ids - NA_WIN_COLS // 2, 0, GRID_W - NA_WIN_COLS)
    in_band = (c_ids[None, :] >= c_start[:, None]) & (c_ids[None, :] < c_start[:, None] + NA_WIN_COLS)
    dr = row_idx - r_ids[:, None] + NA_WIN_ROWS - 1
    dc = jnp.clip(c_ids[None, :] - c_ids[:, None] + NA_WIN_COLS - 1, 0, 2 * NA_WIN_COLS - 2)
    bias = rpb.astype(f32)[:, dr[:, None, :, None], dc[None, :, None, :]]
    bias = jnp.where(in_band[None, None, :, None, :], bias, NEG_INF).reshape(H, rows, GRID_W, wr * GRID_W)
    s_grid = jnp.einsum('brqhd,brkhd->bhrqk', qg, kb).astype(f32) * scale + bias[None]
    s_meta = jnp.einsum('brqhd,bmhd->bhrqm', qg, km).astype(f32) * scale
    p = jax.nn.softmax(jnp.concatenate([s_meta, s_grid], axis=-1), axis=-1).astype(v.dtype)
    o_grid = (jnp.einsum('bhrqm,bmhd->brqhd', p[..., :N_META], vm)
              + jnp.einsum('bhrqk,brkhd->brqhd', p[..., N_META:], vb))
    s_mm = jnp.einsum('bqhd,bkhd->bhqk', qm, km).astype(f32) * scale
    o_meta = jnp.einsum('bhqk,bkhd->bqhd', jax.nn.softmax(s_mm, axis=-1).astype(v.dtype), vm)
    return jnp.concatenate([o_meta, o_grid.reshape(Bsz, T, H, Dh)], axis=1)

def _rwkv7_step(S, inp):
    w_t, kk_t, a_t, k_t, v_t, r_t = inp
    sa = jnp.einsum('dbhvk,dbhk->dbhv', S, -kk_t)
    S = (S * w_t[..., None, :] + sa[..., :, None] * (kk_t * a_t)[..., None, :]
         + v_t[..., :, None] * k_t[..., None, :])
    y = jnp.einsum('dbhvk,dbhk->dbhv', S, r_t)
    return S, y

def rwkv7_bidir(r, k, v, w_lo, a_lo, g_lo, w0, w_up, a0, a_up, g_up, k_k, k_a, r_k, lnx_g, lnx_b):
    Bsz, L, C = r.shape
    out_dtype = r.dtype
    f = lambda t: t.astype(jnp.float32)
    r, k, v, w_lo, a_lo, g_lo = f(r), f(k), f(v), f(w_lo), f(a_lo), f(g_lo)
    w_log = -jax.nn.softplus(-(f(w0)[:, None, None, :]
                               + jnp.einsum('blr,drc->dblc', jnp.tanh(w_lo), f(w_up)))) - 0.5
    decay = jnp.exp(-jnp.exp(w_log))
    a = jax.nn.sigmoid(f(a0)[:, None, None, :] + jnp.einsum('blr,drc->dblc', a_lo, f(a_up)))
    g = jax.nn.sigmoid(g_lo) @ f(g_up)
    hd = lambda t: t.reshape(t.shape[:-1] + (RWKV_HEADS, HEAD_DIM))
    kk = hd(k * f(k_k))
    kk = kk / jnp.maximum(jnp.sqrt(jnp.sum(kk * kk, axis=-1, keepdims=True)), 1e-12)
    k_dir = hd(k[None] * (1.0 + (a - 1.0) * f(k_a)))
    rh, vh = hd(r), hd(v)

    def both(t):
        return jnp.stack([t, jnp.flip(t, axis=1)])

    def per(t):
        return jnp.stack([t[0], jnp.flip(t[1], axis=1)])

    xs = (per(hd(decay)), both(kk), per(hd(a)), per(k_dir), both(vh), both(rh))
    xs = tuple(jnp.moveaxis(t, 2, 0) for t in xs)
    S0 = jnp.zeros((2, Bsz, RWKV_HEADS, HEAD_DIM, HEAD_DIM), jnp.float32)
    _, ys = lax.scan(_rwkv7_step, S0, xs)
    y = per(jnp.moveaxis(ys, 0, 2)).sum(axis=0)
    mean = jnp.mean(y, axis=-1, keepdims=True)
    var = jnp.mean(jnp.square(y - mean), axis=-1, keepdims=True)
    y = ((y - mean) * lax.rsqrt(var + RWKV_GN_EPS)).reshape(Bsz, L, C) * f(lnx_g) + f(lnx_b)
    bonus = (jnp.sum(rh[None] * k_dir * f(r_k), axis=-1, keepdims=True) * vh[None]).sum(axis=0)
    return ((y + bonus.reshape(Bsz, L, C)) * g).astype(out_dtype)

def na_rwkv_mixer(hn, w_in, w_out, rpb, mu, w0, w_up, a0, a_up, g_up, k_k, k_a, r_k, lnx_g, lnx_b):
    Bsz, L, _ = hn.shape
    proj = hn @ w_in
    q, k, v, rest = jnp.split(proj, [NA_WIDTH, 2 * NA_WIDTH, 3 * NA_WIDTH], axis=-1)
    rest = centred_token_shift(rest, mu)
    C = RWKV_WIDTH
    r, kr, vr, w_lo, a_lo, g_lo = jnp.split(
        rest, [C, 2 * C, 3 * C, 3 * C + RWKV_W_RANK, 3 * C + RWKV_W_RANK + RWKV_A_RANK], axis=-1)
    heads = lambda t: t.reshape(Bsz, L, NA_HEADS, HEAD_DIM)
    na = neighbourhood_attention(heads(q), heads(k), heads(v), rpb).reshape(Bsz, L, NA_WIDTH)
    rw = rwkv7_bidir(r, kr, vr, w_lo, a_lo, g_lo, w0, w_up, a0, a_up, g_up, k_k, k_a, r_k, lnx_g, lnx_b)
    return jnp.concatenate([na, rw], axis=-1) @ w_out

def _complex_linear_combine(e1, e2):
    a1r, a1i, b1r, b1i = e1
    a2r, a2i, b2r, b2i = e2
    return (a2r * a1r - a2i * a1i, a2r * a1i + a2i * a1r,
            a2r * b1r - a2i * b1i + b2r, a2r * b1i + a2i * b1r + b2i)

def s5_mixer(hn, b_re, b_im, lam_re, lam_im, log_step, c_re, c_im, d, w_glu):
    Bsz, L, Dm = hn.shape
    f32 = jnp.float32
    u = hn.astype(f32)
    ug = u.reshape(Bsz, L, S5_GROUPS, S5_GROUP_CH)
    lr, li = lam_re.astype(f32), lam_im.astype(f32)
    step = jnp.exp(log_step.astype(f32))[..., None]
    mag = jnp.exp(lr * step)
    ab_re, ab_im = mag * jnp.cos(li * step), mag * jnp.sin(li * step)
    den = lr * lr + li * li
    z_re = ((ab_re - 1.0) * lr + ab_im * li) / den
    z_im = (ab_im * lr - (ab_re - 1.0) * li) / den
    br, bi = b_re.astype(f32)[None], b_im.astype(f32)[None]
    bb_re = z_re[..., None] * br - z_im[..., None] * bi
    bb_im = z_re[..., None] * bi + z_im[..., None] * br

    def per(t):
        return jnp.stack([t[0], jnp.flip(t[1], axis=1)])

    bu_re = per(jnp.einsum('dgpi,blgi->dblgp', bb_re, ug))
    bu_im = per(jnp.einsum('dgpi,blgi->dblgp', bb_im, ug))
    a_re = jnp.broadcast_to(ab_re[:, None, None], (2, 1, L, S5_GROUPS, S5_STATE))
    a_im = jnp.broadcast_to(ab_im[:, None, None], (2, 1, L, S5_GROUPS, S5_STATE))
    _, _, s_re, s_im = lax.associative_scan(_complex_linear_combine, (a_re, a_im, bu_re, bu_im), axis=2)
    y_dir = (jnp.einsum('dgip,dblgp->dblgi', c_re.astype(f32), s_re)
             - jnp.einsum('dgip,dblgp->dblgi', c_im.astype(f32), s_im))
    y = per(y_dir).sum(axis=0).reshape(Bsz, L, Dm) + d.astype(f32) * u
    hcat = jax.nn.gelu(y).astype(hn.dtype) @ w_glu
    return hcat[..., :Dm] * jax.nn.sigmoid(hcat[..., Dm:])

def hierarchical_moe(h, w_group, b_group, w_expert, b_expert, w1, w3, w2):
    Bsz, L, Dm = h.shape
    n_tok = Bsz * L
    n_assign = n_tok * MOE_TOP_K
    f32 = jnp.float32
    hf = h.reshape(n_tok, Dm)
    pg = jax.nn.softmax((hf @ w_group).astype(f32) + b_group.astype(f32), axis=-1)
    grp = jnp.argmax(pg, axis=-1)
    p_grp = jnp.take_along_axis(pg, grp[:, None], axis=-1)
    le_all = jnp.einsum('nd,gde->nge', hf, w_expert).astype(f32) + b_expert.astype(f32)
    le = jnp.take_along_axis(le_all, grp[:, None, None], axis=1)[:, 0]
    top_p, top_i = lax.top_k(jax.nn.softmax(le, axis=-1), MOE_TOP_K)
    gates = p_grp * top_p / jnp.sum(top_p, axis=-1, keepdims=True)
    flat_e = (grp[:, None] * MOE_PER_GROUP + top_i).reshape(-1)
    flat_g = gates.reshape(-1)
    flat_tok = jnp.repeat(jnp.arange(n_tok), MOE_TOP_K)
    order = jnp.argsort(flat_e)
    se, stok, sg = flat_e[order], flat_tok[order], flat_g[order]
    counts = jnp.bincount(flat_e, length=MOE_EXPERTS)
    padded = (counts + MOE_BLOCK - 1) // MOE_BLOCK * MOE_BLOCK
    pad_end = jnp.cumsum(padded)
    pad_start = pad_end - padded
    start = jnp.cumsum(counts) - counts
    dest = pad_start[se] + jnp.arange(n_assign) - start[se]
    n_blocks = -(-n_assign // MOE_BLOCK) + MOE_EXPERTS
    n_rows = n_blocks * MOE_BLOCK
    xbuf = jnp.zeros((n_rows, Dm), h.dtype).at[dest].set(hf[stok])
    blk_e = jnp.minimum(jnp.searchsorted(pad_end, jnp.arange(n_blocks) * MOE_BLOCK, side='right'),
                        MOE_EXPERTS - 1)

    def expert_block(args):
        xb, e = args
        return (jax.nn.silu(xb @ w1[e]) * (xb @ w3[e])) @ w2[e]

    ybuf = lax.map(expert_block, (xbuf.reshape(n_blocks, MOE_BLOCK, Dm), blk_e)).reshape(n_rows, Dm)
    y = ybuf[dest] * sg[:, None].astype(h.dtype)
    return jax.ops.segment_sum(y, stok, num_segments=n_tok).reshape(Bsz, L, Dm)

def setup_inputs(seed: int = 0) -> dict:
    key = jax.random.key(seed)
    keys = jax.random.split(key, 48)
    counter = [0]

    def nxt():
        kk = keys[counter[0]]
        counter[0] += 1
        return kk

    nrm = lambda shape, s: jax.random.normal(nxt(), shape, jnp.float32) * s
    uni = lambda shape, lo, hi: jax.random.uniform(nxt(), shape, jnp.float32, lo, hi)
    ne, no = (DEPTH + 1) // 2, DEPTH // 2
    C, G, P, I = RWKV_WIDTH, S5_GROUPS, S5_STATE, S5_GROUP_CH
    E, F = MOE_EXPERTS, MOE_D_FF
    return {
        'x': nrm((BATCH, SEQ, D_MODEL), 1.0),
        'meta_tokens': nrm((N_META, D_MODEL), 1.0),
        'norm_mix': 1.0 + nrm((DEPTH, D_MODEL), 0.05),
        'norm_ffn': 1.0 + nrm((DEPTH, D_MODEL), 0.05),
        'norm_final': 1.0 + nrm((D_MODEL,), 0.05),
        'mix_w_in': nrm((ne, D_MODEL, IN_COLS), D_MODEL ** -0.5),
        'mix_w_out': nrm((ne, MIX_WIDTH, D_MODEL), MIX_WIDTH ** -0.5),
        'na_rpb': nrm((ne, NA_HEADS, 2 * NA_WIN_ROWS - 1, 2 * NA_WIN_COLS - 1), 0.5),
        'rwkv_mu': uni((ne, SHIFT_COLS), 0.0, 1.0),
        'rwkv_w0': uni((ne, 2, C), -6.0, -1.0),
        'rwkv_w_up': nrm((ne, 2, RWKV_W_RANK, C), 0.1),
        'rwkv_a0': nrm((ne, 2, C), 0.5),
        'rwkv_a_up': nrm((ne, 2, RWKV_A_RANK, C), 0.1),
        'rwkv_g_up': nrm((ne, RWKV_G_RANK, C), RWKV_G_RANK ** -0.5),
        'rwkv_k_k': 0.85 + nrm((ne, C), 0.05),
        'rwkv_k_a': 1.0 + nrm((ne, C), 0.05),
        'rwkv_r_k': nrm((ne, RWKV_HEADS, HEAD_DIM), 0.1),
        'rwkv_lnx_g': 1.0 + nrm((ne, C), 0.05),
        'rwkv_lnx_b': nrm((ne, C), 0.02),
        's5_b_re': nrm((no, G, P, I), (2 * I) ** -0.5),
        's5_b_im': nrm((no, G, P, I), (2 * I) ** -0.5),
        's5_lambda_re': -0.5 + nrm((no, 2, G, P), 0.01),
        's5_lambda_im': math.pi * jnp.arange(P, dtype=jnp.float32) + nrm((no, 2, G, P), 0.01),
        's5_log_step': uni((no, 2, G), math.log(1e-3), math.log(1e-1)),
        's5_c_re': nrm((no, 2, G, I, P), P ** -0.5),
        's5_c_im': nrm((no, 2, G, I, P), P ** -0.5),
        's5_d': nrm((no, D_MODEL), 1.0),
        's5_w_glu': nrm((no, D_MODEL, 2 * D_MODEL), D_MODEL ** -0.5),
        'moe_w_group': nrm((DEPTH, D_MODEL, MOE_GROUPS), D_MODEL ** -0.5),
        'moe_b_group': nrm((DEPTH, MOE_GROUPS), 0.01),
        'moe_w_expert': nrm((DEPTH, MOE_GROUPS, D_MODEL, MOE_PER_GROUP), D_MODEL ** -0.5),
        'moe_b_expert': nrm((DEPTH, MOE_GROUPS, MOE_PER_GROUP), 0.01),
        'moe_w1': nrm((DEPTH, E, D_MODEL, F), D_MODEL ** -0.5),
        'moe_w3': nrm((DEPTH, E, D_MODEL, F), D_MODEL ** -0.5),
        'moe_w2': nrm((DEPTH, E, F, D_MODEL), F ** -0.5),
    }

def reference(x, meta_tokens, norm_mix, norm_ffn, norm_final, mix_w_in, mix_w_out, na_rpb, rwkv_mu,
              rwkv_w0, rwkv_w_up, rwkv_a0, rwkv_a_up, rwkv_g_up, rwkv_k_k, rwkv_k_a, rwkv_r_k,
              rwkv_lnx_g, rwkv_lnx_b, s5_b_re, s5_b_im, s5_lambda_re, s5_lambda_im, s5_log_step,
              s5_c_re, s5_c_im, s5_d, s5_w_glu, moe_w_group, moe_b_group, moe_w_expert, moe_b_expert,
              moe_w1, moe_w3, moe_w2):
    Bsz = x.shape[0]
    meta = jnp.broadcast_to(meta_tokens.astype(x.dtype)[None], (Bsz, N_META, D_MODEL))
    h = jnp.concatenate([meta, x], axis=1)
    for layer in range(DEPTH):
        i = layer // 2
        hn = rms_norm(h, norm_mix[layer])
        if layer % 2 == 0:
            mix = na_rwkv_mixer(hn, mix_w_in[i], mix_w_out[i], na_rpb[i], rwkv_mu[i], rwkv_w0[i],
                                rwkv_w_up[i], rwkv_a0[i], rwkv_a_up[i], rwkv_g_up[i], rwkv_k_k[i],
                                rwkv_k_a[i], rwkv_r_k[i], rwkv_lnx_g[i], rwkv_lnx_b[i])
        else:
            mix = s5_mixer(hn, s5_b_re[i], s5_b_im[i], s5_lambda_re[i], s5_lambda_im[i], s5_log_step[i],
                           s5_c_re[i], s5_c_im[i], s5_d[i], s5_w_glu[i])
        h = h + mix
        h = h + hierarchical_moe(rms_norm(h, norm_ffn[layer]), moe_w_group[layer], moe_b_group[layer],
                                 moe_w_expert[layer], moe_b_expert[layer], moe_w1[layer],
                                 moe_w3[layer], moe_w2[layer])
    return rms_norm(h, norm_final)[:, N_META:]


_drawn_inputs = setup_inputs


def setup_inputs(seed=0):
    import zlib

    import numpy as np

    out = dict(_drawn_inputs(seed))
    spreads = {}
    factors = {}
    for name, (base, spread) in spreads.items():
        noise = np.random.default_rng([zlib.crc32(name.encode()), seed]).standard_normal(out[name].shape)
        drawn = base * np.exp(spread * noise) if base else spread * noise
        out[name] = __import__('jax').numpy.asarray(drawn.astype(out[name].dtype))
    for name, factor in factors.items():
        out[name] = (out[name] * factor).astype(out[name].dtype)
    return out
```

```python
import math
from contextlib import ExitStack

import numpy as np

import concourse.bass as bass
from concourse import mybir

F32 = mybir.dt.float32
I32 = mybir.dt.int32
U32 = mybir.dt.uint32
ALU = mybir.AluOpType
ACT = mybir.ActivationFunctionType
AX = mybir.AxisListType

P = 128
D = 1024
SLOTS = D // P
N_META = 16
SEQ = 512
N_TOK = N_META + SEQ
HALF = N_TOK // 2
GRID_W = 64
GRID_H = SEQ // GRID_W
HD = 64
N_PAIRS = 4
NORM_EPS = 1e-6
N_GAINS = 5


class Core:

    def __init__(self, nc, dram):
        self.nc = nc
        self.dram = dram


class Phase:

    def __init__(self, core, name):
        self.core, self.nc, self.name = core, core.nc, name
        self.stack = ExitStack()
        self.sems = []

    def __enter__(self):
        return self

    def __exit__(self, *exc):
        self.stack.close()
        if exc[0] is None and self.sems:
            numbers = sorted(s.num for s in self.sems)
            assert numbers == list(range(numbers[0], numbers[0] + len(numbers)))
            self.nc.all_engine_barrier(sems_to_clear=range(numbers[0], numbers[-1] + 1))
            self.nc.prepend_free_semaphores(numbers)

    def sb(self, name, shape, dtype=F32):
        return self.stack.enter_context(self.nc.sbuf_tensor(f"{self.name}_{name}", shape, dtype))

    def ps(self, name, shape, dtype=F32):
        return self.stack.enter_context(self.nc.psum_tensor(f"{self.name}_{name}", shape, dtype))

    def sem(self, name):
        s = self.nc.alloc_semaphore(f"{self.name}_{name}")
        self.sems.append(s)
        return s


class Chain:

    def __init__(self, engine, sem):
        self.engine, self.sem, self.n = engine, sem, 0

    def __call__(self, instruction):
        self.n += 1
        instruction.then_inc(self.sem, 1)
        self.engine.wait_ge(self.sem, self.n)

    def restart(self):
        self.engine.sem_clear(self.sem)
        self.n = 0



def setup_phase(core):
    nc, dram = core.nc, core.dram
    with Phase(core, "setup") as ph:
        loaded = [ph.sem(f"loaded{i}") for i in range(3)]
        zeroed, ready = ph.sem("zeroed"), ph.sem("ready")
        with nc.Block() as block:
            @block.sync
            def _(sp):
                sp.dma_start(core.hT[:], dram["hT"]).then_inc(loaded[0], 16)
                sp.dma_start(core.gains[:], dram["gains"]).then_inc(loaded[1], 16)
                for s in loaded[:2]:
                    sp.wait_ge(s, 16)

            @block.gpsimd
            def _(pool):
                nc.gpsimd.memset(core.ones[:], 1.0)
                nc.gpsimd.memset(core.ident[:], 0.0).then_inc(zeroed, 1)
                pool.wait_ge(zeroed, 1)
                nc.gpsimd.affine_select(out=core.ident[:], in_=core.ident[:], compare_op=ALU.not_equal,
                                        fill=1.0, base=0, pattern=[[-1, P]], channel_multiplier=1)

            @block.vector
            def _(dve):
                nc.vector.memset(core.ones_head[:], 0.0).then_inc(ready, 1)
                dve.wait_ge(ready, 1)
                nc.vector.memset(core.ones_head[0:HD, 0:HD], 1.0)
                nc.vector.memset(core.ones_head[HD:, HD:], 1.0)


def norm_phase(core, which, dst):
    nc = core.nc
    with Phase(core, f"norm{which}") as ph:
        squares = ph.sb("squares", [P, SLOTS, N_TOK])
        rstd = ph.sb("rstd", [P, N_TOK])
        eps = ph.sb("eps", [P, 1])
        total = ph.ps("total", [P, 2, 512])
        squared, summed, rooted, eps_set = (ph.sem(n) for n in ("squared", "summed", "rooted", "eps_set"))
        inverted = ph.sem("inverted")
        with nc.Block() as block:
            @block.scalar
            def _(act):
                for s in range(0, SLOTS, 2):
                    nc.scalar.activation(squares[:, s], core.hT[:, s], ACT.Square).then_inc(squared, 1)
                act.wait_ge(summed, 1)
                act.wait_ge(eps_set, 1)
                nc.scalar.activation(rstd[:, :].rearrange("p (h n) -> p h n", h=2), total[:, :, 0:HALF],
                                     ACT.Sqrt, bias=eps[:, 0:1], scale=1.0 / D).then_inc(rooted, 1)

            @block.gpsimd
            def _(pool):
                for s in range(1, SLOTS, 2):
                    nc.gpsimd.tensor_tensor(squares[:, s], core.hT[:, s], core.hT[:, s], ALU.mult)\
                      .then_inc(squared, 1)

            @block.tensor
            def _(pe):
                pe.wait_ge(squared, SLOTS)
                for h in range(2):
                    for s in range(SLOTS):
                        last = nc.tensor.matmul(total[:, h, 0:HALF], core.ones[:, :],
                                                squares[:, s, h * HALF:(h + 1) * HALF],
                                                start=(s == 0), stop=(s == SLOTS - 1))
                last.then_inc(summed, 1)

            @block.vector
            def _(dve):
                nc.vector.memset(eps[:, :], NORM_EPS).then_inc(eps_set, 1)
                dve.wait_ge(rooted, 1)
                nc.vector.reciprocal(rstd[:, :], rstd[:, :]).then_inc(inverted, 1)
                dve.wait_ge(inverted, 1)
                for s in range(SLOTS):
                    nc.vector.scalar_tensor_tensor(out=dst[:, s], in0=core.hT[:, s],
                                                   scalar=core.gains[:, which, s:s + 1], in1=rstd[:, :],
                                                   op0=ALU.mult, op1=ALU.mult)


def dense_phase(core, name, weights, n_turns, rhs, outcome, cut=HALF):
    nc = core.nc
    spans = [(0, cut), (cut, N_TOK)]
    with Phase(core, name) as ph:
        ring = ph.sb("ring", [P, 2, SLOTS, P])
        acc = [ph.ps(f"acc{u}", [P, 2, 512]) for u in range(2)]
        loaded = [ph.sem(f"loaded{u}") for u in range(2)]
        multiplied = [ph.sem(f"multiplied{u}") for u in range(2)]
        drained = [ph.sem(f"drained{u}") for u in range(2)]
        takers = outcome(ph, acc, multiplied, drained)
        with nc.Block() as block:
            @block.sync
            def _(sp):
                with sp.Fori(0, n_turns) as i:
                    for u in range(2):
                        sp.wait_ge(multiplied[u], i)
                        sp.nop(nofuse=True)
                        sp.dma_start(ring[:, u], weights[bass.ds(i, 1), :, u]
                                     .rearrange("a p s m -> (a p) s m")).then_inc(loaded[u], 16)

            @block.tensor
            def _(pe):
                with pe.Fori(0, n_turns) as i:
                    for u in range(2):
                        pe.wait_ge(loaded[u], 16 * i + 16)
                        pe.wait_ge(drained[u], i)
                        for h, (lo, hi) in enumerate(spans):
                            for s in range(SLOTS):
                                last = nc.tensor.matmul(acc[u][:, h, 0:hi - lo], ring[:, u, s], rhs[:, s, lo:hi],
                                                        start=(s == 0), stop=(s == SLOTS - 1))
                        last.then_inc(multiplied[u], 1)

            takers(block)



def by_columns(ap):
    return ap.rearrange("p (r c) -> p c r", c=GRID_W)


def query_key_phase(core, hn, qk):
    nc = core.nc
    cut = N_META + SEQ // 2
    rows = GRID_H // 2

    def outcome(ph, acc, multiplied, drained):
        def takers(block):
            def take(copy, i, u):
                dst = qk[:, bass.ds(2 * i + u, 1), :].rearrange("p a n -> p (a n)")
                grid = dst[:, N_META:N_TOK].rearrange("p (c r) -> p r c", r=GRID_H)
                copy(dst[:, 0:N_META], acc[u][:, 0, 0:N_META])
                copy(grid[:, 0:rows, :], acc[u][:, 0, N_META:cut].rearrange("p (r c) -> p r c", r=rows))
                return copy(grid[:, rows:, :], acc[u][:, 1, 0:SEQ // 2].rearrange("p (r c) -> p r c", r=rows))

            @block.scalar
            def _(act):
                with act.Fori(0, N_PAIRS) as i:
                    act.wait_ge(multiplied[0], i + 1)
                    take(nc.scalar.copy, i, 0).then_inc(drained[0], 1)

            @block.vector
            def _(dve):
                with dve.Fori(0, N_PAIRS) as i:
                    dve.wait_ge(multiplied[1], i + 1)
                    take(nc.vector.tensor_copy, i, 1).then_inc(drained[1], 1)
        return takers

    dense_phase(core, "qk", core.dram["w_qk"], N_PAIRS, hn, outcome, cut=cut)


N_SHIFT = 14


def rwkv_projection_phase(core, hn, raw):
    nc = core.nc

    def outcome(ph, acc, multiplied, drained):
        def takers(block):
            def take(copy, i, u):
                dst = raw[:, bass.ds(2 * i + u, 1), 1:1 + N_TOK].rearrange("p a (h n) -> p (a h) n", h=2)
                return copy(dst, acc[u][:, :, 0:HALF])

            @block.gpsimd
            def _(pool):
                nc.gpsimd.memset(raw[:, :, 0:1], 0.0)
                nc.gpsimd.memset(raw[:, :, N_TOK + 1:], 0.0)

            @block.scalar
            def _(act):
                with act.Fori(0, N_SHIFT // 2) as i:
                    act.wait_ge(multiplied[0], i + 1)
                    take(nc.scalar.copy, i, 0).then_inc(drained[0], 1)

            @block.vector
            def _(dve):
                with dve.Fori(0, N_SHIFT // 2) as i:
                    dve.wait_ge(multiplied[1], i + 1)
                    take(nc.vector.tensor_copy, i, 1).then_inc(drained[1], 1)
        return takers

    dense_phase(core, "rw", core.dram["w_rw"], N_SHIFT // 2, hn, outcome)


NA_WIDTH = 512
N_BLOCKS = 4
WIN_FIRST = [0, 1, 3, 4]
WIN_TYPE = [0, 1, 1, 2]
WIN_V = [(0, 1), (4, 5), (5, 6), (2, 3)]
V_META = 7


def value_phase(core, hn, values):
    nc = core.nc
    with Phase(core, "val") as ph:
        w = ph.sb("w", [P, SLOTS, NA_WIDTH])
        grid = ph.sb("grid", [P, SLOTS, SEQ])
        acc = [ph.ps(f"acc{u}", [P, 512]) for u in range(2)]
        loaded, multiplied, drained, shifted = (ph.sem(n) for n in ("loaded", "multiplied", "drained", "shifted"))
        ordered = ph.sem("ordered")
        tiles = [0, 1, 2, 3, V_META]
        with nc.Block() as block:
            @block.sync
            def _(sp):
                sp.dma_start(w[:], core.dram["w_v"]).then_inc(loaded, 16)
                for t in range(3):
                    sp.wait_ge(drained, t + 2)
                    sp.dma_start(values[0:64, 4 + t], values[64:128, t]).then_inc(shifted, 16)
                    sp.dma_start(values[64:128, 4 + t], values[0:64, t + 1]).then_inc(shifted, 16)
                sp.wait_ge(shifted, 6 * 16)

            @block.scalar
            def _(act):
                for s in range(0, SLOTS, 2):
                    nc.scalar.copy(grid[:, s].rearrange("p (c r) -> p c r", r=GRID_H), by_columns(hn[:, s, N_META:]))\
                      .then_inc(ordered, 1)

            @block.gpsimd
            def _(pool):
                for s in range(1, SLOTS, 2):
                    nc.gpsimd.tensor_copy(grid[:, s].rearrange("p (c r) -> p c r", r=GRID_H),
                                          by_columns(hn[:, s, N_META:])).then_inc(ordered, 1)

            @block.tensor
            def _(pe):
                pe.wait_ge(loaded, 16)
                pe.wait_ge(ordered, SLOTS)
                for n, t in enumerate(tiles):
                    if n >= 2:
                        pe.wait_ge(drained, n - 1)
                    rows = N_META if t == V_META else P
                    for s in range(SLOTS):
                        tokens = hn[:, s, 0:N_META] if t == V_META else grid[:, s, P * t:P * (t + 1)]
                        last = nc.tensor.matmul(acc[n % 2][0:rows, :], tokens, w[:, s],
                                                start=(s == 0), stop=(s == SLOTS - 1))
                    last.then_inc(multiplied, 1)

            @block.vector
            def _(dve):
                for n, t in enumerate(tiles):
                    rows = N_META if t == V_META else P
                    dve.wait_ge(multiplied, n + 1)
                    nc.vector.tensor_copy(values[0:rows, t], acc[n % 2][0:rows, :]).then_inc(drained, 1)



def attention_phase(core, qk, values, mix):
    nc = core.nc
    n_keys = N_META + 2 * P
    tiles = [(hh, b) for hh in range(2) for b in range(N_BLOCKS + 1)]
    T = len(tiles)
    with Phase(core, "att") as ph:
        q = ph.sb("q", [P, N_TOK])
        k = ph.sb("k", [P, N_TOK])
        v = ph.sb("v", [P, 8, P])
        bias = ph.sb("bias", [P, 3, 2, n_keys])
        scores = ph.sb("scores", [P, 2, n_keys])
        probs = ph.sb("probs", [P, 2, n_keys])
        turned = ph.sb("turned", [P, 2, 3, P])
        neg_max = ph.sb("neg_max", [P, T])
        row_sum = ph.sb("row_sum", [P, T])
        inverse = ph.sb("inverse", [P, T])
        sc = [ph.ps(f"sc{u}", [P, 512]) for u in range(2)]
        tp = [ph.ps(f"tp{u}", [P, 4, P]) for u in range(2)]
        out = ph.ps("out", [P, 512])
        out_meta = ph.ps("out_meta", [P, 512])
        names = ("bias_loaded", "staged", "scored", "biased", "maxed", "exped", "inverted", "normed",
                 "turned_ps", "turned_sb", "weighted", "stored")
        s = {n: ph.sem(n) for n in names}
        scale = HD ** -0.5

        def size(b):
            return (N_META, N_META) if b == N_BLOCKS else (P, n_keys)

        with nc.Block() as block:
            @block.sync
            def _(sp):
                with sp.Fori(0, N_PAIRS) as i:
                    sp.wait_ge(s["biased"], T * i)
                    sp.nop(nofuse=True)
                    sp.dma_start(bias[:], core.dram["bias"][bass.ds(i, 1)].rearrange("a p t h n -> (a p) t h n"))\
                      .then_inc(s["bias_loaded"], 16)

            @block.gpsimd
            def _(pool):
                with pool.Fori(0, N_PAIRS) as i:
                    pool.wait_ge(s["weighted"], T * i)
                    nc.gpsimd.tensor_copy(q[:, :], qk[:, bass.ds(2 * i, 1), :].rearrange("p a n -> p (a n)"))\
                      .then_inc(s["staged"], 1)
                    nc.gpsimd.tensor_copy(k[:, :], qk[:, bass.ds(2 * i + 1, 1), :].rearrange("p a n -> p (a n)"))\
                      .then_inc(s["staged"], 1)
                    nc.gpsimd.tensor_copy(v[:, 0:7, :], values[:, 0:7, bass.ds(P * i, P)]).then_inc(s["staged"], 1)
                    nc.gpsimd.tensor_copy(v[0:N_META, 7, :], values[0:N_META, 7, bass.ds(P * i, P)])\
                      .then_inc(s["staged"], 1)

            @block.tensor
            def _(pe):
                with pe.Fori(0, N_PAIRS) as i:
                    def score(n):
                        hh, b = tiles[n]
                        lo = hh * HD
                        if n >= 2:
                            pe.wait_ge(s["biased"], T * i + n - 1)
                        pe.nop(nofuse=True)
                        if b == N_BLOCKS:
                            nc.tensor.matmul(sc[n % 2][0:N_META, 0:N_META], q[lo:lo + HD, 0:N_META],
                                             k[lo:lo + HD, 0:N_META], start=True, stop=True).then_inc(s["scored"], 1)
                            return
                        queries = q[lo:lo + HD, N_META + P * b:N_META + P * (b + 1)]
                        first = N_META + 64 * WIN_FIRST[b]
                        nc.tensor.matmul(sc[n % 2][:, 0:N_META], queries, k[lo:lo + HD, 0:N_META], start=True, stop=True)
                        nc.tensor.matmul(sc[n % 2][:, N_META:n_keys], queries, k[lo:lo + HD, first:first + 2 * P],
                                         start=True, stop=True).then_inc(s["scored"], 1)

                    def turn(n):
                        _, b = tiles[n]
                        rows, keys = size(b)
                        pe.wait_ge(s["normed"], T * i + n + 1)
                        if n >= 2:
                            pe.wait_ge(s["turned_sb"], T * i + n - 1)
                        if rows == N_META:
                            pe.nop(nofuse=True)
                        last = nc.tensor.transpose(tp[n % 2][0:N_META, 0, 0:rows], probs[0:rows, n % 2, 0:N_META],
                                                   core.ident[0:rows, 0:rows])
                        if keys > N_META:
                            for j in range(2):
                                last = nc.tensor.transpose(tp[n % 2][:, 1 + j, :],
                                                           probs[:, n % 2, N_META + P * j:N_META + P * (j + 1)],
                                                           core.ident[:, :])
                        last.then_inc(s["turned_ps"], 1)

                    def weigh(n):
                        hh, b = tiles[n]
                        lo = hh * HD
                        rows, keys = size(b)
                        pe.wait_ge(s["turned_sb"], T * i + n + 1)
                        if n == 0:
                            pe.wait_ge(s["stored"], i)
                        pe.nop(nofuse=True)
                        if b == N_BLOCKS:
                            nc.tensor.matmul(out_meta[lo:lo + HD, 0:N_META], v[0:N_META, V_META, lo:lo + HD],
                                             turned[0:N_META, n % 2, 0, 0:N_META], start=True, stop=True)\
                              .then_inc(s["weighted"], 1)
                            return
                        dst = out[lo:lo + HD, P * b:P * (b + 1)]
                        nc.tensor.matmul(dst, v[0:N_META, V_META, lo:lo + HD], turned[0:N_META, n % 2, 0, :],
                                         start=True, stop=False)
                        for j in range(2):
                            last = nc.tensor.matmul(dst, v[:, WIN_V[b][j], lo:lo + HD], turned[:, n % 2, 1 + j, :],
                                                    start=False, stop=(j == 1))
                        last.then_inc(s["weighted"], 1)

                    pe.wait_ge(s["staged"], 4 * i + 4)
                    pe.wait_ge(s["biased"], T * i)
                    score(0)
                    score(1)
                    for n in range(T):
                        turn(n)
                        if n + 2 < T:
                            score(n + 2)
                        weigh(n)

            @block.vector
            def _(dve):
                with dve.Fori(0, N_PAIRS) as i:
                    def add_bias(n):
                        hh, b = tiles[n]
                        rows, keys = size(b)
                        dve.wait_ge(s["scored"], T * i + n + 1)
                        if n >= 2:
                            dve.wait_ge(s["exped"], T * i + n - 1)
                        kind = 0 if b == N_BLOCKS else WIN_TYPE[b]
                        nc.vector.scalar_tensor_tensor(
                            out=scores[0:rows, n % 2, 0:keys], in0=sc[n % 2][0:rows, 0:keys], scalar=scale,
                            in1=bias[0:rows, kind, hh, 0:keys], op0=ALU.mult, op1=ALU.add).then_inc(s["biased"], 1)
                        dve.wait_ge(s["biased"], T * i + n + 1)
                        nc.vector.tensor_reduce(neg_max[0:rows, n:n + 1], scores[0:rows, n % 2, 0:keys], AX.X, ALU.max,
                                                negate=True).then_inc(s["maxed"], 1)

                    def normalise(n):
                        _, b = tiles[n]
                        rows, keys = size(b)
                        dve.wait_ge(s["exped"], T * i + n + 1)
                        nc.vector.reciprocal(inverse[0:rows, n:n + 1], row_sum[0:rows, n:n + 1]).then_inc(s["inverted"], 1)
                        dve.wait_ge(s["inverted"], T * i + n + 1)
                        nc.vector.tensor_scalar(probs[0:rows, n % 2, 0:keys], probs[0:rows, n % 2, 0:keys],
                                                inverse[0:rows, n:n + 1], None, ALU.mult).then_inc(s["normed"], 1)

                    dve.wait_ge(s["bias_loaded"], 16 * i + 16)
                    dve.wait_ge(s["exped"], T * i)
                    add_bias(0)
                    for n in range(T):
                        if n + 1 < T:
                            add_bias(n + 1)
                        normalise(n)
                    dve.wait_ge(s["weighted"], T * i + T)
                    pair = mix[:, bass.ds(i, 1), :].rearrange("p a n -> p (a n)")
                    nc.vector.tensor_copy(pair[:, 0:N_META], out_meta[:, 0:N_META])
                    nc.vector.tensor_copy(by_columns(pair[:, N_META:]), out[:, :].rearrange("p (c r) -> p c r", r=GRID_H))\
                      .then_inc(s["stored"], 1)

            @block.scalar
            def _(act):
                with act.Fori(0, N_PAIRS) as i:
                    def exponentiate(n):
                        _, b = tiles[n]
                        rows, keys = size(b)
                        act.wait_ge(s["maxed"], T * i + n + 1)
                        if n >= 2:
                            act.wait_ge(s["turned_ps"], T * i + n - 1)
                        nc.scalar.activation(probs[0:rows, n % 2, 0:keys], scores[0:rows, n % 2, 0:keys], ACT.Exp,
                                             bias=neg_max[0:rows, n:n + 1], accum_out=row_sum[0:rows, n:n + 1])\
                          .then_inc(s["exped"], 1)

                    def take(n):
                        _, b = tiles[n]
                        rows, keys = size(b)
                        act.wait_ge(s["turned_ps"], T * i + n + 1)
                        if n >= 2:
                            act.wait_ge(s["weighted"], T * i + n - 1)
                        last = nc.scalar.copy(turned[0:N_META, n % 2, 0, 0:rows], tp[n % 2][0:N_META, 0, 0:rows])
                        if keys > N_META:
                            last = nc.scalar.copy(turned[:, n % 2, 1:3, :], tp[n % 2][:, 1:3, :])
                        last.then_inc(s["turned_sb"], 1)

                    act.wait_ge(s["turned_ps"], T * i)
                    exponentiate(0)
                    for n in range(T):
                        if n + 1 < T:
                            exponentiate(n + 1)
                        take(n)
                        if n == 0:
                            act.wait_ge(s["weighted"], T * i)



CHUNK = 64
N_CHUNKS = -(-N_TOK // CHUNK)
N_PAD = N_CHUNKS * CHUNK
FULL = N_TOK // CHUNK
N_LEVELS = 5
LOG_DECAY = -float(np.exp(-0.5))
A_, R_, B_, K_ = range(4)


def shift_phase(core, raw, rk, v_pad, low):
    nc = core.nc
    with Phase(core, "shift") as ph:
        mu = ph.sb("mu", [P, N_SHIFT])
        near = ph.sb("near", [P, 2, N_TOK])
        off = ph.sb("off", [P, 2, N_TOK])
        loaded, added, differed, shifted, padded = (ph.sem(n) for n in ("loaded", "added", "differed", "shifted", "padded"))
        with nc.Block() as block:
            @block.sync
            def _(sp):
                sp.dma_start(mu[:], core.dram["mu"]).then_inc(loaded, 16)

            @block.gpsimd
            def _(pool):
                nc.gpsimd.memset(v_pad[:, :, N_TOK:], 0.0)
                for j in range(N_SHIFT):
                    if j >= 2:
                        pool.wait_ge(differed, j - 1)
                    nc.gpsimd.tensor_tensor(near[:, j % 2], raw[:, j, 0:N_TOK], raw[:, j, 2:N_TOK + 2], ALU.add)\
                      .then_inc(added, 1)

            @block.vector
            def _(dve):
                dve.wait_ge(loaded, 16)
                for j in range(N_SHIFT):
                    dst = rk[:, j] if j < 8 else v_pad[:, j - 8, 0:N_TOK] if j < 12 else low[:, j - 12]
                    dve.wait_ge(added, j + 1)
                    nc.vector.scalar_tensor_tensor(out=off[:, j % 2], in0=near[:, j % 2], scalar=0.5,
                                                   in1=raw[:, j, 1:N_TOK + 1], op0=ALU.mult, op1=ALU.subtract)\
                      .then_inc(differed, 1)
                    dve.wait_ge(differed, j + 1)
                    nc.vector.scalar_tensor_tensor(out=dst, in0=off[:, j % 2], scalar=mu[:, j:j + 1],
                                                   in1=raw[:, j, 1:N_TOK + 1], op0=ALU.mult, op1=ALU.add)\
                      .then_inc(shifted, 1)

            @block.scalar
            def _(act):
                act.wait_ge(shifted, 13)
                nc.scalar.activation(low[0:64, 0], low[0:64, 0], ACT.Tanh)
                act.wait_ge(shifted, 14)
                nc.scalar.activation(low[:, 1], low[:, 1], ACT.Sigmoid)


def rwkv_prepare_phase(core, rk, v_pad, low, seqs, last_decay, gate, bonus):
    nc = core.nc
    with Phase(core, "prep") as ph:
        up = ph.sb("up", [P, 3, P])
        vec = ph.sb("vec", [P, N_PAIRS, 8])
        restart = ph.sb("restart", [P, N_TOK])
        r, k, v = (ph.sb(n, [P, N_TOK]) for n in "rkv")
        kk, square, norm = (ph.sb(n, [P, N_TOK]) for n in ("kk", "square", "norm"))
        sig, a = (ph.sb(n, [P, 2, N_TOK]) for n in ("sig", "a"))
        before, after = ph.sb("before", [P, 2, N_TOK]), ph.sb("after", [P, 2, N_TOK])
        up_to = ph.sb("up_to", [P, N_TOK])
        exps = ph.sb("exps", [P, 3, N_TOK])
        k_dir = ph.sb("k_dir", [P, 2, N_TOK])
        scaled = ph.sb("scaled", [P, N_TOK])
        banks = [ph.ps(f"banks{u}", [P, 2, 512]) for u in range(4)]
        s = {n: ph.sem(n) for n in (
            "vec_loaded", "up_loaded", "restart_set", "projected", "sigmoided", "squared", "kk_summed", "rooted",
            "bonus_made", "bonus_summed", "logs", "exped", "exps_used", "gated", "turn_done", "chain")}
        halves = [(h, slice(h * HALF, (h + 1) * HALF)) for h in range(2)]

        def two(ap):
            return ap.rearrange("p (h n) -> p h n", h=2)

        with nc.Block() as block:
            @block.sync
            def _(sp):
                sp.dma_start(vec[:, :, 0:7], core.dram["rw_vec"]).then_inc(s["vec_loaded"], 16)
                with sp.Fori(0, N_PAIRS) as i:
                    sp.wait_ge(s["projected"], 5 * i)
                    sp.nop(nofuse=True)
                    sp.dma_start(up[:], core.dram["rw_up"][bass.ds(i, 1)].rearrange("a p j m -> (a p) j m"))\
                      .then_inc(s["up_loaded"], 16)

            @block.tensor
            def _(pe):
                with pe.Fori(0, N_PAIRS) as i:
                    pe.wait_ge(s["up_loaded"], 16 * i + 16)
                    pe.wait_ge(s["turn_done"], i)
                    for d in range(2):
                        for j, rows in ((0, slice(0, 64)), (1, slice(64, P))):
                            for h, cols in halves:
                                last = nc.tensor.matmul(banks[2 * d + j][:, h, 0:HALF], up[rows, d, :],
                                                        low[rows, 0, cols], start=True, stop=True)
                            last.then_inc(s["projected"], 1)
                    pe.wait_ge(s["sigmoided"], 4 * i + 1)
                    for h, cols in halves:
                        last = nc.tensor.matmul(banks[0][:, h, 0:HALF], up[:, 2, :], low[:, 1, cols],
                                                start=True, stop=True)
                    last.then_inc(s["projected"], 1)
                    pe.wait_ge(s["sigmoided"], 4 * i + 2)
                    pe.wait_ge(s["squared"], i + 1)
                    for h, cols in halves:
                        last = nc.tensor.matmul(banks[1][:, h, 0:HALF], core.ones_head[:, :], square[:, cols],
                                                start=True, stop=True)
                    last.then_inc(s["kk_summed"], 1)
                    pe.wait_ge(s["sigmoided"], 4 * i + 3)
                    pe.wait_ge(s["bonus_made"], i + 1)
                    for h, cols in halves:
                        last = nc.tensor.matmul(banks[2][:, h, 0:HALF], core.ones_head[:, :], scaled[:, cols],
                                                start=True, stop=True)
                    last.then_inc(s["bonus_summed"], 1)

            @block.scalar
            def _(act):
                act.wait_ge(s["vec_loaded"], 16)
                with act.Fori(0, N_PAIRS) as i:
                    for d in range(2):
                        act.wait_ge(s["projected"], 5 * i + 2 * d + 1)
                        act.wait_ge(s["turn_done"], i)
                        nc.scalar.activation(two(sig[:, d]), banks[2 * d][:, :, 0:HALF], ACT.Sigmoid,
                                             bias=vec[:, bass.ds(i, 1), d:d + 1].rearrange("p a b -> p (a b)"))\
                          .then_inc(s["sigmoided"], 1)
                        act.wait_ge(s["projected"], 5 * i + 2 * d + 2)
                        nc.scalar.activation(two(a[:, d]), banks[2 * d + 1][:, :, 0:HALF], ACT.Sigmoid,
                                             bias=vec[:, bass.ds(i, 1), 2 + d:3 + d].rearrange("p a b -> p (a b)"))\
                          .then_inc(s["sigmoided"], 1)
                    act.wait_ge(s["projected"], 5 * i + 5)
                    nc.scalar.copy(gate[:, bass.ds(i, 1), :].rearrange("p a (h n) -> p (a h) n", h=2),
                                   banks[0][:, :, 0:HALF]).then_inc(s["gated"], 1)
                    act.wait_ge(s["kk_summed"], i + 1)
                    nc.scalar.activation(two(norm[:, :]), banks[1][:, :, 0:HALF], ACT.Sqrt).then_inc(s["rooted"], 1)
                    for d in range(2):
                        act.wait_ge(s["logs"], 2 * i + d + 1)
                        act.wait_ge(s["exps_used"], 2 * i + d)
                        nc.scalar.activation(exps[:, 0], before[:, d], ACT.Exp)
                        nc.scalar.activation(exps[:, 1], after[:, d], ACT.Exp)
                        nc.scalar.activation(exps[:, 2], after[:, d], ACT.Exp, scale=-1.0)
                        edge = after[:, 0, CHUNK - 1:FULL * CHUNK:CHUNK] if d == 0 else after[:, 1, 0:FULL * CHUNK:CHUNK]
                        rest = after[:, 0, N_TOK - 1:N_TOK] if d == 0 else after[:, 1, FULL * CHUNK:FULL * CHUNK + 1]
                        dst = last_decay[:, d, bass.ds(i, 1), :].rearrange("p a c -> p (a c)")
                        nc.scalar.activation(dst[:, 0:FULL], edge, ACT.Exp)
                        nc.scalar.activation(dst[:, FULL:], rest, ACT.Exp).then_inc(s["exped"], 1)

            @block.gpsimd
            def _(pool):
                nc.gpsimd.memset(restart[:, :], 1.0).then_inc(s["restart_set"], 1)
                pool.wait_ge(s["restart_set"], 1)
                nc.gpsimd.memset(restart[:, 0:N_TOK:CHUNK], 0.0).then_inc(s["restart_set"], 1)
                nc.gpsimd.memset(seqs[:, :, :, :, N_TOK:], 0.0)

            @block.vector
            def _(dve):
                link = Chain(dve, s["chain"])
                dve.wait_ge(s["vec_loaded"], 16)
                dve.wait_ge(s["restart_set"], 2)
                link(nc.vector.tensor_scalar(vec[:, :, 7:8], vec[:, :, 5:6], -1.0, 1.0, ALU.mult, ALU.add))
                with dve.Fori(0, N_PAIRS) as i:
                    link.restart()

                    def col(j):
                        return vec[:, bass.ds(i, 1), j:j + 1].rearrange("p a b -> p (a b)")

                    def flat(ap):
                        return ap.rearrange("p a n -> p (a n)")

                    nc.vector.tensor_copy(r[:, :], flat(rk[:, bass.ds(i, 1), :]))
                    nc.vector.tensor_copy(v[:, :], flat(v_pad[:, bass.ds(i, 1), 0:N_TOK]))
                    link(nc.vector.tensor_copy(k[:, :], flat(rk[:, bass.ds(N_PAIRS + i, 1), :])))
                    link(nc.vector.tensor_scalar(kk[:, :], k[:, :], col(4), None, ALU.mult))
                    nc.vector.tensor_tensor(square[:, :], kk[:, :], kk[:, :], ALU.mult).then_inc(s["squared"], 1)
                    dve.wait_ge(s["rooted"], i + 1)
                    link(nc.vector.tensor_scalar(norm[:, :], norm[:, :], 1e-12, None, ALU.max))
                    link(nc.vector.reciprocal(norm[:, :], norm[:, :]))
                    link(nc.vector.tensor_tensor(kk[:, :], kk[:, :], norm[:, :], ALU.mult))
                    for d in range(2):
                        dve.wait_ge(s["sigmoided"], 4 * i + 2 * d + 2)
                        link(nc.vector.tensor_scalar(sig[:, d], sig[:, d], LOG_DECAY, None, ALU.mult))
                        if d == 0:
                            link(nc.vector.tensor_tensor_scan(after[:, 0], restart[:, :], sig[:, 0], 0.0,
                                                              ALU.mult, ALU.add))
                            nc.vector.tensor_tensor(before[:, 0], after[:, 0], sig[:, 0], ALU.subtract)\
                              .then_inc(s["logs"], 1)
                        else:
                            link(nc.vector.tensor_tensor_scan(up_to[:, :], restart[:, :], sig[:, 1], 0.0,
                                                              ALU.mult, ALU.add))
                            full = up_to[:, 0:FULL * CHUNK].rearrange("p (c n) -> p c n", n=CHUNK)
                            nc.vector.tensor_tensor(
                                before[:, 1, 0:FULL * CHUNK].rearrange("p (c n) -> p c n", n=CHUNK),
                                full[:, :, CHUNK - 1:CHUNK].to_broadcast([P, FULL, CHUNK]), full, ALU.subtract)
                            tail = slice(FULL * CHUNK, N_TOK)
                            link(nc.vector.tensor_tensor(
                                before[:, 1, tail], up_to[:, N_TOK - 1:N_TOK].to_broadcast([P, N_TOK - FULL * CHUNK]),
                                up_to[:, tail], ALU.subtract))
                            nc.vector.tensor_tensor(after[:, 1], before[:, 1], sig[:, 1], ALU.add)\
                              .then_inc(s["logs"], 1)
                        link(nc.vector.tensor_scalar(k_dir[:, d], a[:, d], col(5), col(7), ALU.mult, ALU.add))
                        link(nc.vector.tensor_tensor(k_dir[:, d], k_dir[:, d], k[:, :], ALU.mult))
                        link(nc.vector.tensor_tensor(a[:, d], a[:, d], kk[:, :], ALU.mult))
                    link(nc.vector.tensor_tensor(scaled[:, :], k_dir[:, 0], k_dir[:, 1], ALU.add))
                    nc.vector.scalar_tensor_tensor(out=scaled[:, :], in0=scaled[:, :], scalar=col(6), in1=r[:, :],
                                                   op0=ALU.mult, op1=ALU.mult).then_inc(s["bonus_made"], 1)
                    for d in range(2):
                        def seq(which):
                            return seqs[:, d, bass.ds(i, 1), which, 0:N_TOK].rearrange("p a n -> p (a n)")
                        dve.wait_ge(s["exped"], 2 * i + d + 1)
                        nc.vector.scalar_tensor_tensor(out=seq(A_), in0=kk[:, :], scalar=-1.0, in1=exps[:, 0],
                                                       op0=ALU.mult, op1=ALU.mult)
                        nc.vector.tensor_tensor(seq(R_), r[:, :], exps[:, 1], ALU.mult)
                        nc.vector.tensor_tensor(seq(B_), a[:, d], exps[:, 2], ALU.mult)
                        nc.vector.tensor_tensor(seq(K_), k_dir[:, d], exps[:, 2], ALU.mult)\
                          .then_inc(s["exps_used"], 1)
                    dve.wait_ge(s["bonus_summed"], i + 1)
                    dve.wait_ge(s["gated"], i + 1)
                    dve.wait_ge(s["exps_used"], 2 * i + 2)
                    nc.vector.tensor_tensor(bonus[:, bass.ds(i, 1), :].rearrange("p a (h n) -> p (a h) n", h=2),
                                            banks[2][:, :, 0:HALF], two(v[:, :]), ALU.mult)\
                      .then_inc(s["turn_done"], 1)
                    dve.wait_ge(s["turn_done"], i + 1)


MADE = ["AB", "AK", "M", "BK_tokens", "V_tokens"] + [f"{n}{l}" for l in range(N_LEVELS) for n in ("FQ", "Q")] \
    + ["X", "SA", "Y", "S"]
VECTOR_TAKES = ["AB", "AK", "M"] + [f"Q{l}" for l in range(N_LEVELS)] + ["S"]
SCALAR_TAKES = ["BK_tokens", "V_tokens"] + [f"FQ{l}" for l in range(N_LEVELS)] + ["X", "SA", "Y"]


def rwkv_chunk_phase(core, seqs, v_pad, last_decay, y):
    nc = core.nc
    with Phase(core, "chunk") as ph:
        stage = ph.sb("stage", [P, 2, N_PAIRS, 5, CHUNK])
        decay = ph.sb("decay", [P, 2, N_PAIRS])
        ab = ph.sb("ab", [P, 2, N_PAIRS, 2, CHUNK])
        ak = ph.sb("ak", [P, 2, N_PAIRS, 2, CHUNK])
        m = ph.sb("m", [P, 2, N_PAIRS, CHUNK])
        m_level = ph.sb("m_level", [P, 2, N_LEVELS, N_PAIRS, CHUNK])
        q = ph.sb("q", [P, 2, 2, N_PAIRS, CHUNK])
        fq = ph.sb("fq", [P, 2, N_PAIRS, CHUNK])
        bk = ph.sb("bk", [P, 2, 2, N_PAIRS, CHUNK])
        vt = ph.sb("vt", [P, 2, N_PAIRS, CHUNK])
        x = ph.sb("x", [P, 2, N_PAIRS, CHUNK])
        sa = ph.sb("sa", [P, 2, N_PAIRS, CHUNK])
        state = ph.sb("state", [P, 2, N_PAIRS, CHUNK])
        order = ph.sb("order", [P, 2, 2, CHUNK])
        order_t = ph.sb("order_t", [P, 2, CHUNK])
        level = ph.sb("level", [P, N_LEVELS + 1, CHUNK])
        eye = ph.sb("eye", [P, CHUNK])
        bank = [[ph.ps(f"bank{d}{j}", [P, 512]) for j in range(4)] for d in range(2)]
        consts_loaded = [ph.sem(f"consts_loaded{j}") for j in range(4)]
        zeroed, staged = ph.sem("zeroed"), ph.sem("staged")
        made = [ph.sem(f"made{d}") for d in range(2)]
        vector_took = [ph.sem(f"vector_took{d}") for d in range(2)]
        scalar_took = [ph.sem(f"scalar_took{d}") for d in range(2)]
        masked = [ph.sem(f"masked{d}") for d in range(2)]
        pool_chain, vector_chain = ph.sem("pool_chain"), ph.sem("vector_chain")
        pairs = range(N_PAIRS)
        heads = [slice(0, 64), slice(64, P)]

        def wait_made(eng, i, d, what):
            eng.wait_ge(made[d], len(MADE) * i + MADE.index(what) + 1)

        def wait_vector(eng, i, d, what):
            eng.wait_ge(vector_took[d], len(VECTOR_TAKES) * i + VECTOR_TAKES.index(what) + 1)

        def wait_scalar(eng, i, d, what):
            eng.wait_ge(scalar_took[d], len(SCALAR_TAKES) * i + SCALAR_TAKES.index(what) + 1)

        def by_pair(b, n):
            return b[:, 0:N_PAIRS * n].rearrange("p (g n) -> p g n", n=n)

        with nc.Block() as block:
            @block.sync
            def _(sp):
                for j, (dst, name) in enumerate(((order, "order"), (order_t, "order_t"), (level, "level"), (eye, "eye"))):
                    sp.dma_start(dst[:], core.dram[name]).then_inc(consts_loaded[j], 16)

            @block.gpsimd
            def _(pool):
                for sem in consts_loaded:
                    pool.wait_ge(sem, 16)
                nc.gpsimd.memset(state[:], 0.0).then_inc(zeroed, 1)
                link = Chain(pool, pool_chain)
                with pool.Fori(0, N_CHUNKS) as i:
                    link.restart()
                    for d in range(2):
                        at = i * CHUNK if d == 0 else (N_CHUNKS - 1 - i) * CHUNK
                        which = i if d == 0 else (N_CHUNKS - 1 - i)
                        pool.wait_ge(made[d], len(MADE) * i)
                        pool.wait_ge(vector_took[d], len(VECTOR_TAKES) * i)
                        pool.nop(nofuse=True)
                        for g in range(N_PAIRS):
                            nc.gpsimd.tensor_copy(stage[:, d, g, 0:4], seqs[:, d, g, :, bass.ds(at, CHUNK)])
                        nc.gpsimd.tensor_copy(decay[:, d].unsqueeze(2), last_decay[:, d, :, bass.ds(which, 1)])
                        nc.gpsimd.tensor_copy(stage[:, d, :, 4], v_pad[:, :, bass.ds(at, CHUNK)])\
                          .then_inc(staged, 1)
                    for d in range(2):
                        wide = [P, N_PAIRS, CHUNK]
                        wait_vector(pool, i, d, "M")
                        first = level[:, 0:1].to_broadcast(wide)
                        nc.gpsimd.tensor_tensor(q[:, d, 0], ab[:, d, :, 0], first, ALU.mult)
                        link(nc.gpsimd.tensor_tensor(q[:, d, 1], m[:, d], first, ALU.mult))
                        both = q[:, d].rearrange("p a g n -> p (a g) n")
                        nc.gpsimd.tensor_tensor(both, both, eye[:, :].unsqueeze(1).to_broadcast([P, 2 * N_PAIRS, CHUNK]),
                                                ALU.add)
                        for l in range(N_LEVELS):
                            last = nc.gpsimd.tensor_tensor(m_level[:, d, l], m[:, d],
                                                           level[:, l + 1:l + 2].to_broadcast(wide), ALU.mult)
                        last.then_inc(masked[d], 1)

            @block.tensor
            def _(pe):
                for sem in consts_loaded:
                    pe.wait_ge(sem, 16)
                pe.wait_ge(zeroed, 1)
                with pe.Fori(0, N_CHUNKS) as i:
                    def each(d, dst, n, *products):
                        pe.nop(nofuse=True)
                        for g in pairs:
                            for rows in heads:
                                for j, (lhs, rhs) in enumerate(products):
                                    last = nc.tensor.matmul(dst[rows, g * n:(g + 1) * n], lhs(rows, g), rhs(rows, g),
                                                            start=(j == 0), stop=(j == len(products) - 1))
                        return last

                    def staged_seq(d, first, count=1):
                        return lambda rows, g: stage[rows, d, g, first:first + count].rearrange("p a n -> p (a n)")

                    def plain(t, d):
                        return lambda rows, g: t[rows, d, g]

                    def second(t, d, j):
                        return lambda rows, g: t[rows, d, g, j]

                    def half_of(t, d, j):
                        return lambda rows, g: t[rows, d, j, g]

                    def unit(rows, g):
                        return eye[rows, :]

                    pe.wait_ge(staged, 2 * i + 2)
                    for d in range(2):
                        pe.wait_ge(scalar_took[d], len(SCALAR_TAKES) * i)
                        pe.wait_ge(vector_took[d], len(VECTOR_TAKES) * i)
                        each(d, bank[d][0], 2 * CHUNK, (staged_seq(d, B_), staged_seq(d, A_, 2))).then_inc(made[d], 1)
                        each(d, bank[d][1], 2 * CHUNK, (staged_seq(d, K_), staged_seq(d, A_, 2))).then_inc(made[d], 1)
                        each(d, bank[d][3], CHUNK, (staged_seq(d, A_), staged_seq(d, B_))).then_inc(made[d], 1)
                        each(d, bank[d][2][:, 0:256], CHUNK, (staged_seq(d, B_), unit))
                        each(d, bank[d][2][:, 256:512], CHUNK, (staged_seq(d, K_), unit)).then_inc(made[d], 1)
                    for d in range(2):
                        wait_scalar(pe, i, d, "BK_tokens")
                        each(d, bank[d][2], CHUNK, (staged_seq(d, 4), unit)).then_inc(made[d], 1)
                    for l in range(N_LEVELS):
                        for d in range(2):
                            if l == 0:
                                pe.wait_ge(masked[d], i + 1)
                            else:
                                wait_vector(pe, i, d, f"Q{l - 1}")
                            each(d, bank[d][0], CHUNK, (half_of(m_level, d, l), half_of(q, d, 0))).then_inc(made[d], 1)
                        for d in range(2):
                            wait_scalar(pe, i, d, f"FQ{l}")
                            last = each(d, bank[d][1], CHUNK, (half_of(q, d, 1), plain(fq, d)))
                            if l < N_LEVELS - 1:
                                last = each(d, bank[d][1][:, 256:512], CHUNK, (plain(fq, d), half_of(q, d, 1)))
                            last.then_inc(made[d], 1)
                    for d in range(2):
                        wait_scalar(pe, i, d, "V_tokens")
                        each(d, bank[d][0], CHUNK, (staged_seq(d, A_), plain(state, d)),
                             (second(ak, d, 0), plain(vt, d))).then_inc(made[d], 1)
                    for d in range(2):
                        wait_scalar(pe, i, d, "X")
                        wait_vector(pe, i, d, f"Q{N_LEVELS - 1}")
                        each(d, bank[d][3], CHUNK, (half_of(q, d, 0), plain(x, d))).then_inc(made[d], 1)
                    for d in range(2):
                        wait_scalar(pe, i, d, "SA")
                        each(d, bank[d][2], CHUNK, (plain(state, d), staged_seq(d, R_)),
                             (plain(sa, d), second(ab, d, 1)), (plain(vt, d), second(ak, d, 1))).then_inc(made[d], 1)
                        each(d, bank[d][1], CHUNK, (half_of(bk, d, 0), plain(sa, d)),
                             (half_of(bk, d, 1), plain(vt, d))).then_inc(made[d], 1)

            @block.vector
            def _(dve):
                for sem in consts_loaded:
                    dve.wait_ge(sem, 16)
                link = Chain(dve, vector_chain)
                with dve.Fori(0, N_CHUNKS) as i:
                    link.restart()
                    for d in range(2):
                        for j, (what, dst) in enumerate((("AB", ab), ("AK", ak))):
                            wait_made(dve, i, d, what)
                            nc.vector.tensor_tensor(
                                dst[:, d].rearrange("p g a n -> p g (a n)"), by_pair(bank[d][j], 2 * CHUNK),
                                order[:, d].rearrange("p a n -> p (a n)").unsqueeze(1).to_broadcast([P, N_PAIRS, 2 * CHUNK]),
                                ALU.mult).then_inc(vector_took[d], 1)
                        wait_made(dve, i, d, "M")
                        nc.vector.tensor_tensor(m[:, d], by_pair(bank[d][3], CHUNK),
                                                order_t[:, d:d + 1].to_broadcast([P, N_PAIRS, CHUNK]),
                                                ALU.mult).then_inc(vector_took[d], 1)
                    for l in range(N_LEVELS):
                        for d in range(2):
                            wait_made(dve, i, d, f"Q{l}")
                            n = N_PAIRS * CHUNK * (2 if l < N_LEVELS - 1 else 1)
                            both = q[:, d].rearrange("p a g n -> p (a g n)")[:, 0:n]
                            nc.vector.tensor_tensor(both, bank[d][1][:, 0:n], both, ALU.add)\
                              .then_inc(vector_took[d], 1)
                    for d in range(2):
                        wait_made(dve, i, d, "S")
                        link(nc.vector.tensor_tensor(state[:, d], by_pair(bank[d][1], CHUNK), state[:, d], ALU.add))
                        nc.vector.tensor_tensor(state[:, d], state[:, d],
                                                decay[:, d].unsqueeze(2).to_broadcast([P, N_PAIRS, CHUNK]),
                                                ALU.mult).then_inc(vector_took[d], 1)

            @block.scalar
            def _(act):
                with act.Fori(0, N_CHUNKS) as i:
                    def take(d, what, dst, src):
                        wait_made(act, i, d, what)
                        nc.scalar.copy(dst, src).then_inc(scalar_took[d], 1)

                    for d in range(2):
                        take(d, "BK_tokens", bk[:, d].rearrange("p a g n -> p (a g n)"), bank[d][2][:, :])
                    for d in range(2):
                        take(d, "V_tokens", vt[:, d], by_pair(bank[d][2], CHUNK))
                    for l in range(N_LEVELS):
                        for d in range(2):
                            take(d, f"FQ{l}", fq[:, d], by_pair(bank[d][0], CHUNK))
                    for d in range(2):
                        take(d, "X", x[:, d], by_pair(bank[d][0], CHUNK))
                    for d in range(2):
                        take(d, "SA", sa[:, d], by_pair(bank[d][3], CHUNK))
                    for d in range(2):
                        at = i * CHUNK if d == 0 else (N_CHUNKS - 1 - i) * CHUNK
                        take(d, "Y", y[:, d, :, bass.ds(at, CHUNK)], by_pair(bank[d][2], CHUNK))


RWKV_GN_EPS = 64e-5


def rwkv_output_phase(core, y, gate, bonus, mix):
    nc = core.nc
    with Phase(core, "rwout") as ph:
        total, square, rstd = (ph.sb(n, [P, N_TOK]) for n in ("total", "square", "rstd"))
        ln = ph.sb("ln", [P, N_PAIRS, 2])
        eps = ph.sb("eps", [P, 1])
        mean, var = ph.ps("mean", [P, 2, 512]), ph.ps("var", [P, 2, 512])
        loaded, chain, ready, averaged, squared, varied, rooted = (
            ph.sem(n) for n in ("loaded", "chain", "ready", "averaged", "squared", "varied", "rooted"))
        eps_set = ph.sem("eps_set")
        halves = [(h, slice(h * HALF, (h + 1) * HALF)) for h in range(2)]

        def two(ap):
            return ap.rearrange("p (h n) -> p h n", h=2)

        with nc.Block() as block:
            @block.sync
            def _(sp):
                sp.dma_start(ln[:], core.dram["rw_ln"]).then_inc(loaded, 16)

            @block.tensor
            def _(pe):
                with pe.Fori(0, N_PAIRS) as i:
                    for done, src, dst, said in ((ready, total, mean, averaged), (squared, square, var, varied)):
                        pe.wait_ge(done, i + 1)
                        for h, cols in halves:
                            last = nc.tensor.matmul(dst[:, h, 0:HALF], core.ones_head[:, :], src[:, cols],
                                                    start=True, stop=True)
                        last.then_inc(said, 1)

            @block.scalar
            def _(act):
                act.wait_ge(eps_set, 1)
                with act.Fori(0, N_PAIRS) as i:
                    act.wait_ge(varied, i + 1)
                    nc.scalar.activation(two(rstd[:, :]), var[:, :, 0:HALF], ACT.Sqrt, bias=eps[:, 0:1],
                                         scale=1.0 / HD).then_inc(rooted, 1)

            @block.vector
            def _(dve):
                nc.vector.memset(eps[:, :], RWKV_GN_EPS).then_inc(eps_set, 1)
                dve.wait_ge(loaded, 16)
                link = Chain(dve, chain)
                with dve.Fori(0, N_PAIRS) as i:
                    link.restart()

                    def of(t, first=0):
                        return t[:, bass.ds(first + i, 1), 0:N_TOK].rearrange("p a n -> p (a n)")

                    def col(j):
                        return ln[:, bass.ds(i, 1), j:j + 1].rearrange("p a b -> p (a b)")

                    nc.vector.tensor_tensor(total[:, :], of(y[:, 0]), of(y[:, 1]), ALU.add).then_inc(ready, 1)
                    dve.wait_ge(averaged, i + 1)
                    link(nc.vector.scalar_tensor_tensor(out=two(total[:, :]), in0=mean[:, :, 0:HALF], scalar=-1.0 / HD,
                                                        in1=two(total[:, :]), op0=ALU.mult, op1=ALU.add))
                    nc.vector.tensor_tensor(square[:, :], total[:, :], total[:, :], ALU.mult).then_inc(squared, 1)
                    dve.wait_ge(rooted, i + 1)
                    link(nc.vector.reciprocal(rstd[:, :], rstd[:, :]))
                    link(nc.vector.scalar_tensor_tensor(out=total[:, :], in0=total[:, :], scalar=col(0), in1=rstd[:, :],
                                                        op0=ALU.mult, op1=ALU.mult))
                    link(nc.vector.scalar_tensor_tensor(out=total[:, :], in0=total[:, :], scalar=col(1), in1=of(bonus),
                                                        op0=ALU.add, op1=ALU.add))
                    link(nc.vector.tensor_tensor(of(mix, N_PAIRS), total[:, :], of(gate), ALU.mult))


def rwkv(core, raw, raw_free, mix):
    nc = core.nc
    with ExitStack() as stack:
        def sb(name, shape):
            return stack.enter_context(nc.sbuf_tensor(name, shape, F32))

        v_pad = sb("v_pad", [P, N_PAIRS, N_PAD])
        last_decay = sb("last_decay", [P, 2, N_PAIRS, N_CHUNKS])
        gate, bonus = sb("gate", [P, N_PAIRS, N_TOK]), sb("bonus", [P, N_PAIRS, N_TOK])
        with ExitStack() as early:
            rk = early.enter_context(nc.sbuf_tensor("rk", [P, 2 * N_PAIRS, N_TOK], F32))
            low = early.enter_context(nc.sbuf_tensor("low", [P, 2, N_TOK], F32))
            shift_phase(core, raw, rk, v_pad, low)
            raw_free()
            seqs = stack.enter_context(nc.sbuf_tensor("seqs", [P, 2, N_PAIRS, 4, N_PAD], F32, side="right"))
            rwkv_prepare_phase(core, rk, v_pad, low, seqs, last_decay, gate, bonus)
        y = sb("y", [P, 2, N_PAIRS, N_PAD])
        rwkv_chunk_phase(core, seqs, v_pad, last_decay, y)
        rwkv_output_phase(core, y, gate, bonus, mix)


def chunk_masks():
    i, t = np.meshgrid(np.arange(CHUNK), np.arange(CHUNK), indexing="ij")
    order = np.stack([np.stack([i < t, i <= t]), np.stack([i > t, i >= t])]).astype(np.float32)
    order_t = np.stack([t < i, t > i]).astype(np.float32)
    level = np.stack([(i // (2 * b) == t // (2 * b)) & (i // b != t // b) for b in (1, 2, 4, 8, 16, 32)])
    both = lambda a: np.ascontiguousarray(np.concatenate([a, a], axis=0))
    return {"order": both(order.transpose(2, 0, 1, 3)), "order_t": both(order_t.transpose(1, 0, 2)),
            "level": both(level.astype(np.float32).transpose(1, 0, 2)), "eye": both(np.eye(CHUNK, dtype=np.float32))}



N_GROUPS = 4
PER_GROUP = 8
N_EXPERTS = N_GROUPS * PER_GROUP
D_FF = D // 2
FF_TILES = D_FF // P
N_TILES = -(-N_TOK // P)
TAIL = N_TOK - (N_TILES - 1) * P
CAP = 64
MAX_ROUNDS = -(-N_TOK // CAP)
TURNS = N_EXPERTS // 2
FAR = -1e30


def moe(core, layer, hn):
    nc = core.nc
    with ExitStack() as stack:
        def sb(name, shape, dtype=F32):
            return stack.enter_context(nc.sbuf_tensor(f"moe{layer}_{name}", shape, dtype))

        by_token = sb("by_token", [P, N_TILES, SLOTS, P])
        rank = sb("rank", [P, N_TILES, N_EXPERTS])
        gates = sb("gates", [P, 2, N_TILES])
        places = sb("places", [P, 2, 2, N_TILES])
        rounds = sb("rounds", [1, 1], I32)
        ring = sb("ring", [P, 2, 3, FF_TILES * D])
        route_phase(core, layer, hn, by_token, rank, gates, places, rounds)
        expert_phase(core, layer, by_token, rank, gates, places, rounds, ring)


def route_phase(core, layer, hn, by_token, rank, gates, places, rounds):
    nc, dram = core.nc, core.dram
    with Phase(core, f"route{layer}") as ph:
        n_logits = N_GROUPS + N_EXPERTS
        w = ph.sb("w", [P, SLOTS, n_logits])
        b = ph.sb("b", [P, n_logits])
        consts = ph.sb("consts", [P, 8 + N_EXPERTS + MAX_ROUNDS + N_TILES])
        order = ph.sb("order", [P, P])
        logits = ph.sb("logits", [P, N_TILES, n_logits])
        group = ph.sb("group", [P, N_TILES, N_GROUPS])
        chosen = ph.sb("chosen", [P, 2, N_TILES, PER_GROUP])
        of_group = ph.sb("of_group", [P, N_TILES, PER_GROUP, N_GROUPS])
        local = ph.sb("local", [P, N_TILES, PER_GROUP])
        score = ph.sb("score", [P, N_TILES, PER_GROUP])
        shifted = ph.sb("shifted", [P, N_TILES, N_GROUPS])
        best = ph.sb("best", [P, 6, N_TILES])
        assigned = ph.sb("assigned", [P, 3, N_TILES, N_EXPERTS])
        picked = ph.sb("picked", [P, N_TILES, N_EXPERTS])
        fullest = ph.sb("fullest", [P, 1])
        needed = ph.sb("needed", [P, MAX_ROUNDS])
        n_rounds = ph.sb("n_rounds", [P, 1])
        ps_logits = ph.ps("ps_logits", [P, 512])
        ps_rank = ph.ps("ps_rank", [P, 512])
        ps_count = ph.ps("ps_count", [P, 512])
        ps_tok = [ph.ps(f"ps_tok{u}", [P, 4, P]) for u in range(2)]
        loaded = [ph.sem(f"loaded{j}") for j in range(4)]
        names = ("logits_made", "exp_in", "exp_out", "assigned", "ranked", "turned", "taken", "chain")
        s = {n: ph.sem(n) for n in names}
        first8 = consts[:, 0:8]
        expert_base = consts[:, 8:8 + N_EXPERTS]
        thresholds = consts[:, 8 + N_EXPERTS:8 + N_EXPERTS + MAX_ROUNDS]
        valid = consts[:, 8 + N_EXPERTS + MAX_ROUNDS:]
        sizes = [P] * (N_TILES - 1) + [TAIL]
        parts = [(t, g) for t in range(N_TILES) for g in range(SLOTS // 4)]

        def view(t, n):
            return t[:, 0:N_TILES * n].rearrange("p (t n) -> p t n", n=n)

        with nc.Block() as block:
            @block.sync
            def _(sp):
                for j, (dst, name) in enumerate(((w, f"route_w{layer}"), (b, f"route_b{layer}"),
                                                 (consts, "route_consts"), (order, "token_order"))):
                    sp.dma_start(dst[:], dram[name]).then_inc(loaded[j], 16)

            @block.tensor
            def _(pe):
                for sem in loaded:
                    pe.wait_ge(sem, 16)
                for t, n in enumerate(sizes):
                    for k in range(SLOTS):
                        last = nc.tensor.matmul(ps_logits[0:n, t * n_logits:(t + 1) * n_logits],
                                                hn[:, k, P * t:P * t + n], w[:, k], start=(k == 0), stop=(k == SLOTS - 1))
                last.then_inc(s["logits_made"], 1)
                for j, (t, g) in enumerate(parts):
                    if j >= 2:
                        pe.wait_ge(s["taken"], j - 1)
                    for k in range(4):
                        last = nc.tensor.transpose(ps_tok[j % 2][0:sizes[t], k, :],
                                                   hn[:, 4 * g + k, P * t:P * t + sizes[t]], core.ident[:, :])
                    last.then_inc(s["turned"], 1)
                pe.wait_ge(s["assigned"], 1)
                both = assigned[:, 2]
                for t in range(N_TILES):
                    dst = ps_rank[:, t * N_EXPERTS:(t + 1) * N_EXPERTS]
                    for before in range(t):
                        nc.tensor.matmul(dst, core.ones[:, :], both[:, before], start=(before == 0), stop=False)
                    nc.tensor.matmul(dst, order[:, :], both[:, t], start=(t == 0), stop=True)
                for t in range(N_TILES):
                    last = nc.tensor.matmul(ps_count[:, 0:N_EXPERTS], core.ones[:, :], both[:, t],
                                            start=(t == 0), stop=(t == N_TILES - 1))
                last.then_inc(s["ranked"], 1)

            @block.scalar
            def _(act):
                act.wait_ge(s["exp_in"], 1)
                nc.scalar.activation(shifted[:], shifted[:], ACT.Exp).then_inc(s["exp_out"], 1)
                for j, (t, g) in enumerate(parts):
                    act.wait_ge(s["turned"], j + 1)
                    nc.scalar.copy(by_token[0:sizes[t], t, 4 * g:4 * g + 4, :], ps_tok[j % 2][0:sizes[t]])\
                      .then_inc(s["taken"], 1)
                act.wait_ge(s["exp_in"], 2)
                nc.scalar.activation(best[:, 3], best[:, 3], ACT.Exp).then_inc(s["exp_out"], 1)

            @block.vector
            def _(dve):
                link = Chain(dve, s["chain"])
                v = nc.vector
                for sem in loaded:
                    dve.wait_ge(sem, 16)
                link(v.memset(logits[:], 0.0))
                dve.wait_ge(s["logits_made"], 1)
                full = N_TILES - 1
                v.tensor_tensor(logits[:, 0:full], ps_logits[:, 0:full * n_logits].rearrange("p (t n) -> p t n", n=n_logits),
                                b[:, :].unsqueeze(1).to_broadcast([P, full, n_logits]), ALU.add)
                link(v.tensor_tensor(logits[0:TAIL, full], ps_logits[0:TAIL, full * n_logits:(full + 1) * n_logits],
                                     b[0:TAIL, :], ALU.add))
                g_logits = logits[:, :, 0:N_GROUPS]
                e_logits = logits[:, :, N_GROUPS:].rearrange("p t (g e) -> p t e g", g=N_GROUPS)

                def one_hot(out, values, top, n):
                    wide = [P, N_TILES, n]
                    link(v.tensor_tensor(score[:, :, 0:n], values, top.to_broadcast(wide), ALU.is_equal))
                    link(v.tensor_tensor(score[:, :, 0:n], score[:, :, 0:n],
                                         first8[:, 0:n].unsqueeze(1).to_broadcast(wide), ALU.mult))
                    link(v.tensor_reduce(best[:, 5], score[:, :, 0:n], AX.X, ALU.max))
                    link(v.tensor_tensor(out, score[:, :, 0:n], best[:, 5].unsqueeze(2).to_broadcast(wide), ALU.is_equal))

                link(v.tensor_reduce(best[:, 0], g_logits, AX.X, ALU.max))
                v.tensor_tensor(shifted[:], g_logits, best[:, 0].unsqueeze(2).to_broadcast([P, N_TILES, N_GROUPS]),
                                ALU.subtract).then_inc(s["exp_in"], 1)
                one_hot(group[:], g_logits, best[:, 0].unsqueeze(2), N_GROUPS)
                link(v.tensor_tensor(group[:], group[:], valid.unsqueeze(2).to_broadcast([P, N_TILES, N_GROUPS]), ALU.mult))
                link(v.tensor_tensor(of_group[:], e_logits,
                                     group[:].unsqueeze(2).to_broadcast([P, N_TILES, PER_GROUP, N_GROUPS]), ALU.mult))
                link(v.tensor_reduce(local[:], of_group[:], AX.X, ALU.add))
                link(v.tensor_reduce(best[:, 1], local[:], AX.X, ALU.max))
                one_hot(chosen[:, 0], local[:], best[:, 1].unsqueeze(2), PER_GROUP)
                link(v.scalar_tensor_tensor(out=local[:], in0=chosen[:, 0], scalar=FAR, in1=local[:],
                                            op0=ALU.mult, op1=ALU.add))
                link(v.tensor_reduce(best[:, 2], local[:], AX.X, ALU.max))
                one_hot(chosen[:, 1], local[:], best[:, 2].unsqueeze(2), PER_GROUP)
                v.tensor_tensor(best[:, 3], best[:, 2], best[:, 1], ALU.subtract).then_inc(s["exp_in"], 1)
                for c in range(2):
                    for g in range(N_GROUPS):
                        link(v.tensor_tensor(assigned[:, c, :, PER_GROUP * g:PER_GROUP * (g + 1)], chosen[:, c],
                                             group[:, :, g:g + 1].to_broadcast([P, N_TILES, PER_GROUP]), ALU.mult))
                v.tensor_tensor(assigned[:, 2], assigned[:, 0], assigned[:, 1], ALU.add).then_inc(s["assigned"], 1)
                dve.wait_ge(s["exp_out"], 2)
                link(v.tensor_reduce(best[:, 4], shifted[:], AX.X, ALU.add))
                link(v.tensor_scalar(best[:, 5], best[:, 3], 1.0, None, ALU.add))
                link(v.tensor_tensor(best[:, 4], best[:, 4], best[:, 5], ALU.mult))
                link(v.reciprocal(gates[:, 0], best[:, 4]))
                link(v.tensor_tensor(gates[:, 1], gates[:, 0], best[:, 3], ALU.mult))
                dve.wait_ge(s["ranked"], 1)
                dve.wait_ge(s["assigned"], 1)
                link(v.scalar_tensor_tensor(out=rank[:], in0=view(ps_rank, N_EXPERTS), scalar=1.0, in1=assigned[:, 2],
                                            op0=ALU.add, op1=ALU.mult))
                link(v.tensor_scalar(rank[:], rank[:], -1.0, None, ALU.add))
                for c in range(2):
                    link(v.tensor_tensor(picked[:], assigned[:, c],
                                         expert_base.unsqueeze(1).to_broadcast([P, N_TILES, N_EXPERTS]), ALU.mult))
                    link(v.tensor_reduce(places[:, 0, c], picked[:], AX.X, ALU.add))
                    link(v.tensor_tensor(picked[:], rank[:], assigned[:, c], ALU.mult))
                    link(v.tensor_reduce(places[:, 1, c], picked[:], AX.X, ALU.add))
                link(v.tensor_reduce(fullest[:, :], ps_count[:, 0:N_EXPERTS], AX.X, ALU.max))
                link(v.tensor_scalar(needed[:, :], thresholds, fullest[:, 0:1], None, ALU.is_lt))
                link(v.tensor_reduce(n_rounds[:, :], needed[:, :], AX.X, ALU.add))
                link(v.tensor_copy(rounds[0:1, 0:1], n_rounds[0:1, 0:1]))


def expert_phase(core, layer, by_token, rank, gates, places, rounds, ring):
    nc, dram = core.nc, core.dram
    fetched = [[nc.alloc_semaphore(f"moe{layer}_fetched{c}{g}") for g in range(2)] for c in range(2)]
    with Phase(core, f"exp{layer}") as ph:
        here = ph.sb("here", [P, CAP])
        pick = ph.sb("pick", [P, 2, N_TILES, CAP])
        x = ph.sb("x", [P, 2, SLOTS, CAP])
        hidden = ph.sb("hidden", [P, 2, FF_TILES, CAP])
        y = ph.sb("y", [P, 2, SLOTS, CAP])
        y_rows = ph.sb("y_rows", [CAP, 2, D])
        ps_x, ps_1, ps_3, ps_y = (ph.ps(n, [P, 512]) for n in ("ps_x", "ps_1", "ps_3", "ps_y"))
        ps_rows = [ph.ps(f"ps_rows{h}", [P, 512]) for h in range(2)]
        loaded = [[ph.sem(f"w{j}_loaded{u}") for j in range(3)] for u in range(2)]
        stored = [ph.sem(f"stored{u}") for u in range(2)]
        down = [ph.sem(f"down{u}") for u in range(2)]
        here_loaded = ph.sem("here_loaded")
        inside, row_sums, round_gates = (ph.sb(n, [P, 2, N_TILES]) for n in ("inside", "row_sums", "round_gates"))
        rows = ph.sb("rows", [P, 2, N_TILES], U32)
        got = ph.sb("got", [P, 2, 2, D])
        mixed = ph.sb("mixed", [P, 2, SLOTS, P])
        ps_mix = [ph.ps(f"ps_mix{h}", [P, 512]) for h in range(2)] + [ps_1, ps_3]
        sizes = [P] * (N_TILES - 1) + [TAIL]
        shares = [-(-N_TILES // 2), N_TILES // 2]
        s = {n: ph.sem(n) for n in ("picked", "gathered", "x_taken", "up1", "up3", "silued", "hidden_made",
                                    "y_taken", "turned", "rows_taken", "moved_on", "rows_made", "chain",
                                    "mixed", "mix_turned", "added")}
        scratch = core.scratch
        weights = [dram["moe_w1"][layer], dram["moe_w3"][layer], dram["moe_w2"][layer]]
        last_tile = N_TILES - 1

        def n_rounds(eng):
            return eng.value_load(rounds[0:1, 0:1], min_val=1, max_val=MAX_ROUNDS)

        with nc.Block() as block:
            @block.sync
            def _(sp):
                sp.dma_start(here[:], dram["places"]).then_inc(here_loaded, 16)
                with sp.Fori(0, n_rounds(sp)) as r:
                    with sp.Fori(0, TURNS) as i:
                        for u in range(2):
                            sp.wait_ge(down[u], TURNS * r + i)
                            sp.nop(nofuse=True)
                            for j in range(3):
                                src = weights[j][bass.ds(2 * i + u, 1)]
                                src = src.rearrange("a (p s) n -> (a p) (s n)", p=P) if j < 2 else \
                                    src.rearrange("a (j p) n -> (a p) j n", p=P)
                                dst = ring[:, u, j] if j < 2 else ring[:, u, j].rearrange("p (j n) -> p j n", j=FF_TILES)
                                sp.dma_start(dst, src).then_inc(loaded[u][j], 16)

            @block.vector
            def _(dve):
                dve.wait_ge(here_loaded, 16)
                link = Chain(dve, s["chain"])
                with dve.Fori(0, n_rounds(dve)) as r:
                    with dve.Fori(0, TURNS) as i:
                        e = 2 * (TURNS * r + i)
                        dve.wait_ge(s["gathered"], e)
                        for u in range(2):
                            nc.vector.tensor_tensor(
                                pick[:, u], rank[:, :, bass.ds(2 * i + u, 1)].to_broadcast([P, N_TILES, CAP]),
                                here[:, :].unsqueeze(1).to_broadcast([P, N_TILES, CAP]), ALU.is_equal)\
                              .then_inc(s["picked"], 1)
                        for u in range(2):
                            dve.wait_ge(s["up3"], e + u + 1)
                            dve.wait_ge(s["silued"], e + u + 1)
                            nc.vector.tensor_tensor(hidden[:, u].rearrange("p j n -> p (j n)"),
                                                    ps_3[:, 0:FF_TILES * CAP],
                                                    hidden[:, u].rearrange("p j n -> p (j n)"), ALU.mult)\
                              .then_inc(s["hidden_made"], 1)
                            dve.wait_ge(down[u], TURNS * r + i + 1)
                            nc.vector.tensor_copy(y[:, u].rearrange("p q n -> p (q n)"), ps_y[:, 0:SLOTS * CAP])\
                              .then_inc(s["y_taken"], 1)
                    dve.wait_ge(s["picked"], N_EXPERTS * r + N_EXPERTS)
                    nc.vector.tensor_scalar(here[:, :], here[:, :], float(CAP), None, ALU.add)\
                      .then_inc(s["moved_on"], 1)
                    dve.wait_ge(s["moved_on"], r + 1)
                    dve.nop(nofuse=True)
                    link.restart()
                    left = places[:, 1]
                    link(nc.vector.tensor_scalar(inside[:], left, 0.0, None, ALU.is_ge))
                    link(nc.vector.scalar_tensor_tensor(out=inside[:], in0=left, scalar=float(CAP), in1=inside[:],
                                                        op0=ALU.is_lt, op1=ALU.mult))
                    link(nc.vector.tensor_tensor(row_sums[:], places[:, 0], left, ALU.add))
                    link(nc.vector.tensor_tensor(row_sums[:], row_sums[:], inside[:], ALU.mult))
                    link(nc.vector.tensor_copy(rows[:], row_sums[:]))
                    link(nc.vector.tensor_scalar(left, left, -float(CAP), None, ALU.add))
                    nc.vector.tensor_tensor(round_gates[:], gates[:], inside[:], ALU.mult).then_inc(s["rows_made"], 1)
                    dve.wait_ge(s["rows_made"], r + 1)
                    for t, n in enumerate(sizes):
                        g = t % 2
                        for c in range(2):
                            dve.wait_ge(fetched[c][g], 16 * (shares[g] * r + t // 2 + 1))
                        if t >= 2:
                            dve.wait_ge(s["mix_turned"], N_TILES * r + t - 1)
                        link(nc.vector.tensor_scalar(got[0:n, g, 0], got[0:n, g, 0], round_gates[0:n, 0, t:t + 1], None,
                                                     ALU.mult))
                        nc.vector.scalar_tensor_tensor(
                            out=mixed[0:n, g].rearrange("n s p -> n p s"),
                            in0=got[0:n, g, 1].rearrange("n (p s) -> n p s", s=SLOTS), scalar=round_gates[0:n, 1, t:t + 1],
                            in1=got[0:n, g, 0].rearrange("n (p s) -> n p s", s=SLOTS), op0=ALU.mult, op1=ALU.add)\
                          .then_inc(s["mixed"], 1)
                        dve.wait_ge(s["mix_turned"], N_TILES * r + t + 1)
                        for h in range(2):
                            dst = core.hT[:, 4 * h:4 * h + 4, P * t:P * t + n]
                            last = nc.vector.tensor_tensor(dst, ps_mix[2 * g + h][:, 0:4 * P].rearrange(
                                "p (k n) -> p k n", k=4)[:, :, 0:n], dst, ALU.add)
                        last.then_inc(s["added"], 1)

            @block.gpsimd
            def _(pool):
                with pool.Fori(0, n_rounds(pool)) as r:
                    for u in range(2):
                        pool.wait_ge(stored[u], 16 * (TURNS * r + TURNS))
                    pool.wait_ge(s["rows_made"], r + 1)
                    for t, n in enumerate(sizes):
                        if t >= 2:
                            pool.wait_ge(s["mixed"], N_TILES * r + t - 1)
                        else:
                            pool.wait_ge(s["mixed"], N_TILES * r)
                        pool.nop(nofuse=True)
                        for c in range(2):
                            nc.gpsimd.indirect_dma_start(
                                got[0:n, t % 2, c], None, scratch,
                                bass.IndirectOffsetOnAxis(ap=rows[0:n, c, t:t + 1], axis=0))\
                              .then_inc(fetched[c][t % 2], 16)

            @block.scalar
            def _(act):
                with act.Fori(0, n_rounds(act)) as r:
                    for c in range(2):
                        for g in range(2):
                            act.wait_ge(fetched[c][g], 16 * shares[g] * r)
                    act.nop(nofuse=True)
                    with act.Fori(0, TURNS) as i:
                        e = 2 * (TURNS * r + i)
                        for u in range(2):
                            act.wait_ge(s["gathered"], e + u + 1)
                            nc.scalar.copy(x[:, u].rearrange("p s n -> p (s n)"), ps_x[:, 0:SLOTS * CAP]).then_inc(s["x_taken"], 1)
                            act.wait_ge(s["up1"], e + u + 1)
                            nc.scalar.activation(hidden[:, u].rearrange("p j n -> p (j n)"), ps_1[:, 0:FF_TILES * CAP],
                                                 ACT.Silu).then_inc(s["silued"], 1)
                            act.wait_ge(s["turned"], e + u + 1)
                            act.wait_ge(stored[u], 16 * (TURNS * r + i))
                            for h in range(2):
                                last = nc.scalar.copy(y_rows[:, u, 512 * h:512 * (h + 1)], ps_rows[h][0:CAP, :])
                            last.then_inc(s["rows_taken"], 1)
                            act.wait_ge(s["rows_taken"], e + u + 1)
                            act.dma_start(scratch[bass.ds((2 * i + u) * CAP, CAP), :], y_rows[:, u])\
                               .then_inc(stored[u], 16)
                    for u in range(2):
                        act.wait_ge(stored[u], 16 * (TURNS * r + TURNS))

            @block.tensor
            def _(pe):
                with pe.Fori(0, n_rounds(pe)) as r:
                    with pe.Fori(0, TURNS) as i:
                        e = 2 * (TURNS * r + i)
                        pe.wait_ge(s["added"], N_TILES * r)
                        for u in range(2):
                            w1, w3 = (ring[:, u, j].rearrange("p (s n) -> p s n", s=SLOTS) for j in range(2))
                            w2 = ring[:, u, 2].rearrange("p (j n) -> p j n", j=FF_TILES)
                            pe.wait_ge(s["picked"], e + u + 1)
                            pe.wait_ge(s["x_taken"], e + u)
                            for k in range(SLOTS):
                                for t in range(N_TILES):
                                    n = TAIL if t == last_tile else P
                                    last = nc.tensor.matmul(ps_x[:, k * CAP:(k + 1) * CAP], by_token[0:n, t, k, :],
                                                            pick[0:n, u, t], start=(t == 0), stop=(t == last_tile))
                            last.then_inc(s["gathered"], 1)
                            pe.wait_ge(s["x_taken"], e + u + 1)
                            for j, (w, dst, done, free) in enumerate(((w1, ps_1, "up1", "silued"),
                                                                      (w3, ps_3, "up3", "hidden_made"))):
                                pe.wait_ge(loaded[u][j], 16 * (TURNS * r + i) + 16)
                                pe.wait_ge(s[free], e + u)
                                for f in range(FF_TILES):
                                    for k in range(SLOTS):
                                        last = nc.tensor.matmul(dst[:, f * CAP:(f + 1) * CAP], w[:, k, P * f:P * (f + 1)],
                                                                x[:, u, k], start=(k == 0), stop=(k == SLOTS - 1))
                                last.then_inc(s[done], 1)
                            pe.wait_ge(loaded[u][2], 16 * (TURNS * r + i) + 16)
                            pe.wait_ge(s["hidden_made"], e + u + 1)
                            pe.wait_ge(s["y_taken"], e + u)
                            for q in range(SLOTS):
                                for f in range(FF_TILES):
                                    last = nc.tensor.matmul(ps_y[:, q * CAP:(q + 1) * CAP], w2[:, f, P * q:P * (q + 1)],
                                                            hidden[:, u, f], start=(f == 0), stop=(f == FF_TILES - 1))
                            last.then_inc(down[u], 1)
                            pe.wait_ge(s["y_taken"], e + u + 1)
                            pe.wait_ge(s["rows_taken"], e + u)
                            pe.nop(nofuse=True)
                            for q in range(SLOTS):
                                last = nc.tensor.transpose(ps_rows[q // 4][0:CAP, P * (q % 4):P * (q % 4 + 1)],
                                                           y[:, u, q], core.ident[:, :])
                            last.then_inc(s["turned"], 1)
                    for t, n in enumerate(sizes):
                        g = t % 2
                        pe.wait_ge(s["mixed"], N_TILES * r + t + 1)
                        if t >= 2:
                            pe.wait_ge(s["added"], N_TILES * r + t - 1)
                        pe.nop(nofuse=True)
                        for k in range(SLOTS):
                            last = nc.tensor.transpose(ps_mix[2 * g + k // 4][:, P * (k % 4):P * (k % 4) + n],
                                                       mixed[0:n, g, k], core.ident[0:n, 0:n])
                        last.then_inc(s["mix_turned"], 1)



def output_projection_phase(core, mix):
    nc = core.nc

    def outcome(ph, acc, multiplied, drained):
        def takers(block):
            @block.vector
            def _(dve):
                with dve.Fori(0, SLOTS // 2) as i:
                    for u in range(2):
                        dve.wait_ge(multiplied[u], i + 1)
                        h = core.hT[:, bass.ds(2 * i + u, 1), :].rearrange("p a (h n) -> p (a h) n", h=2)
                        nc.vector.tensor_tensor(h, acc[u][:, :, 0:HALF], h, ALU.add).then_inc(drained[u], 1)
        return takers

    dense_phase(core, "out", core.dram["w_out"], SLOTS // 2, mix, outcome)



S5_STEPS = 8
S5_CHUNKS = N_TOK // S5_STEPS
S5_CH = 16
S5_GROUPS = D // S5_CH
S5_GP = S5_GROUPS // 2
S5_P = 64
LOW, HIGH = 7, 8


def s5(core, hn):
    nc = core.nc
    with ExitStack() as stack:
        def sb(name, shape):
            return stack.enter_context(nc.sbuf_tensor(f"s5_{name}", shape, F32))

        rows = sb("rows", [S5_CHUNKS, S5_GROUPS * P])
        tables = sb("tables", [P, 3, 2, S5_GROUPS, 2, S5_STEPS])
        a8 = sb("a8", [P, 3, 2, S5_GP])
        b, c = sb("b", [P, 2, S5_GROUPS, S5_CH]), sb("c", [P, 2, S5_GROUPS, 2, S5_CH])
        s5_tables_phase(core, tables, a8, b, c)
        with ExitStack() as right:
            state = right.enter_context(nc.sbuf_tensor("s5_state", [P, 2, 2, S5_GP, S5_CHUNKS + 1], F32, side="right"))
            with nc.sbuf_tensor("s5_u", [P, S5_GROUPS, S5_CHUNKS], F32) as u:
                s5_inputs_phase(core, hn, rows, u)
                s5_local_phase(core, u, tables, b, c, rows, state)
            s5_scan_phase(core, state, a8)
            swapped = sb("swapped", [P, 2, 2, S5_GP, S5_CHUNKS + 1])
            s5_swap_phase(core, state, swapped)
        s5_entering_phase(core, swapped, tables, c, rows)
        s5_outputs_phase(core, rows, hn)


def s5_tables_phase(core, tables, a8, b, c):
    nc, dram = core.nc, core.dram
    n = 2 * S5_GROUPS
    with Phase(core, "s5t") as ph:
        lam = ph.sb("lam", [P, 3, n])
        names = ("step", "growth", "shrink", "sin", "cos", "angle", "t0", "t1", "den", "am1", "rest", "turns",
                 "sr", "cr", "m", "sm", "cm")
        t = {k: ph.sb(k, [P, n]) for k in names}
        z = ph.sb("z", [P, 2, n])
        powers = ph.sb("powers", [P, 2, LOW + 1 + HIGH, n])
        zp = ph.sb("zp", [P, 2, S5_STEPS, n])
        tmp = ph.sb("tmp", [P, 2, S5_STEPS, n])
        sign = ph.sb("sign", [P, 1])
        loaded = [ph.sem(f"loaded{i}") for i in range(3)]
        bits = ph.sb("bits", [P, n], I32)
        chain, made = ph.sem("chain"), ph.sem("made")
        magic = 1.5 * 2.0 ** 23

        with nc.Block() as block:
            @block.sync
            def _(sp):
                for i, (dst, name) in enumerate(((lam, "s5_lam"), (b, "s5_b"), (c, "s5_c"))):
                    sp.dma_start(dst[:], dram[name]).then_inc(loaded[i], 16)
                for s in loaded:
                    sp.wait_ge(s, 16)

            @block.vector
            def _(dve):
                link = Chain(dve, chain)
                v = nc.vector
                re, im = lam[:, 0], lam[:, 1]
                link(v.memset(sign[:, :], 1.0))
                link(v.memset(sign[S5_P:, :], -1.0))
                dve.wait_ge(loaded[0], 16)
                x, r, k = (t[name][:, :] for name in ("t0", "rest", "turns"))

                def reduce(value, unit):
                    hi = float(np.float32(round(unit * 2048) / 2048))
                    link(v.tensor_scalar(k, value, 1 / unit, magic, ALU.mult, ALU.add))
                    link(v.tensor_scalar(k, k, -magic, None, ALU.add))
                    link(v.scalar_tensor_tensor(out=r, in0=k, scalar=-hi, in1=value, op0=ALU.mult, op1=ALU.add))
                    link(v.scalar_tensor_tensor(out=r, in0=k, scalar=-(unit - hi), in1=r, op0=ALU.mult, op1=ALU.add))

                def series(out, y, coefficients):
                    link(v.tensor_scalar(out, y, coefficients[-1], None, ALU.mult))
                    for coefficient in coefficients[-2:0:-1]:
                        link(v.scalar_tensor_tensor(out=out, in0=out, scalar=coefficient, in1=y, op0=ALU.add, op1=ALU.mult))
                    link(v.tensor_scalar(out, out, coefficients[0], None, ALU.add))

                def exp(out, value):
                    reduce(value, np.log(2.0))
                    link(v.tensor_scalar(k, k, -126.0, 127.0, ALU.max, ALU.min))
                    link(v.tensor_scalar(k, k, 127.0, 2.0 ** 23, ALU.add, ALU.mult))
                    link(v.tensor_copy(bits[:, :], k))
                    series(out, r, [1 / math.factorial(j) for j in range(8)])
                    link(v.tensor_tensor(out, out, bits[:, :].bitcast(F32), ALU.mult))

                exp(t["step"][:, :], lam[:, 2])
                link(v.tensor_tensor(t["t0"][:, :], re, t["step"][:, :], ALU.mult))
                link(v.tensor_tensor(t["angle"][:, :], im, t["step"][:, :], ALU.mult))
                exp(t["growth"][:, :], x)
                link(v.reciprocal(t["shrink"][:, :], t["growth"][:, :]))
                reduce(t["angle"][:, :], np.pi / 2)
                square, sr, cr, m, sm, cm = (t[name][:, :] for name in ("t1", "sr", "cr", "m", "sm", "cm"))
                link(v.tensor_tensor(square, r, r, ALU.mult))
                series(sr, square, [(-1) ** j / math.factorial(2 * j + 1) for j in range(5)])
                link(v.tensor_tensor(sr, sr, r, ALU.mult))
                series(cr, square, [(-1) ** j / math.factorial(2 * j) for j in range(6)])
                link(v.tensor_scalar(m, k, 0.25, magic, ALU.mult, ALU.add))
                link(v.tensor_scalar(m, m, -magic, None, ALU.add))
                link(v.scalar_tensor_tensor(out=m, in0=m, scalar=-4.0, in1=k, op0=ALU.mult, op1=ALU.add))
                link(v.scalar_tensor_tensor(out=cm, in0=m, scalar=-1.0, in1=m, op0=ALU.mult, op1=ALU.max))
                link(v.tensor_scalar(sm, cm, -1.0, 2.0, ALU.mult, ALU.add))
                link(v.tensor_tensor(sm, sm, m, ALU.mult))
                link(v.tensor_scalar(cm, cm, -1.0, 1.0, ALU.mult, ALU.add))
                for out, y0, y1, op in (("sin", cr, sr, ALU.add), ("cos", sr, cr, ALU.subtract)):
                    link(v.tensor_tensor(t["t1"][:, :], sm, y0, ALU.mult))
                    link(v.tensor_tensor(t[out][:, :], cm, y1, ALU.mult))
                    link(v.tensor_tensor(t[out][:, :], t[out][:, :], t["t1"][:, :], op))
                one, minus_one = powers[:, :, LOW + 1], powers[:, :, LOW - 1]
                link(v.memset(powers[:, 0, LOW], 1.0))
                link(v.memset(powers[:, 1, LOW], 0.0))
                link(v.tensor_tensor(one[:, 0], t["growth"][:, :], t["cos"][:, :], ALU.mult))
                link(v.tensor_tensor(one[:, 1], t["growth"][:, :], t["sin"][:, :], ALU.mult))
                link(v.tensor_tensor(minus_one[:, 0], t["shrink"][:, :], t["cos"][:, :], ALU.mult))
                link(v.scalar_tensor_tensor(out=minus_one[:, 1], in0=t["shrink"][:, :], scalar=-1.0, in1=t["sin"][:, :],
                                            op0=ALU.mult, op1=ALU.mult))
                link(v.tensor_tensor(t["den"][:, :], re, re, ALU.mult))
                link(v.tensor_tensor(t["t1"][:, :], im, im, ALU.mult))
                link(v.tensor_tensor(t["den"][:, :], t["den"][:, :], t["t1"][:, :], ALU.add))
                link(v.reciprocal(t["den"][:, :], t["den"][:, :]))
                link(v.tensor_scalar(t["am1"][:, :], one[:, 0], -1.0, None, ALU.add))
                for part, x, y, op in ((0, t["am1"][:, :], one[:, 1], ALU.add), (1, one[:, 1], t["am1"][:, :], ALU.subtract)):
                    link(v.tensor_tensor(z[:, part], x, re, ALU.mult))
                    link(v.tensor_tensor(t["t1"][:, :], y, im, ALU.mult))
                    link(v.tensor_tensor(z[:, part], z[:, part], t["t1"][:, :], op))
                    link(v.tensor_tensor(z[:, part], z[:, part], t["den"][:, :], ALU.mult))

                def times(out, x, y, count):
                    def wide(part):
                        return y[:, part].unsqueeze(1).to_broadcast([P, count, n])
                    for part, (i, j, op) in enumerate(((0, 1, ALU.subtract), (1, 0, ALU.add))):
                        v.tensor_tensor(tmp[:, 0, 0:count], x[:, 0], wide(i), ALU.mult)
                        link(v.tensor_tensor(tmp[:, 1, 0:count], x[:, 1], wide(j), ALU.mult))
                        link(v.tensor_tensor(out[:, part], tmp[:, 0, 0:count], tmp[:, 1, 0:count], op))

                def run(lo, hi):
                    return powers[:, :, LOW + lo:LOW + hi + 1]

                for k in (1, 2, 4):
                    times(run(k + 1, 2 * k), run(1, k), powers[:, :, LOW + k], k)
                for k in (1, 2):
                    times(run(-2 * k, -k - 1), run(-k, -1), powers[:, :, LOW - k], k)
                times(run(-7, -5), run(-3, -1), powers[:, :, LOW - 4], 3)
                times(zp[:, :], run(0, 7), z, S5_STEPS)
                for g2 in range(2):
                    half = slice(g2 * S5_P, (g2 + 1) * S5_P)
                    for part in range(2):
                        src = powers[half, part, LOW + 8].rearrange("p (d gp g) -> p d gp g", d=2, g=2)[:, :, :, g2]
                        link(v.tensor_copy(a8[half, part], src))
                        if part:
                            link(v.tensor_scalar(a8[half, 2], src, -1.0, None, ALU.mult))
                v.nop(nofuse=True).then_inc(made, 1)

            def spread(eng, copy_to):
                def factors(slot, part, k_of, source, signed):
                    for d in range(2):
                        for s in range(S5_STEPS):
                            copy_to(tables[:, slot, part, :, d, s],
                                    source[:, part, k_of(d, s)].rearrange("p (d g) -> p d g", d=2)[:, d], signed)
                return factors

            @block.scalar
            def _(act):
                act.wait_ge(made, 1)
                factors = spread(act, lambda dst, src, signed: nc.scalar.activation(
                    dst, src, ACT.Copy, scale=sign[:, 0:1]) if signed else nc.scalar.copy(dst, src))
                factors(0, 0, lambda d, s: s if d else 7 - s, zp, False)
                factors(1, 0, lambda d, s: LOW - s if d else s, powers, True)
                factors(2, 0, lambda d, s: LOW + 8 - s if d else LOW + 1 + s, powers, True)

            @block.gpsimd
            def _(pool):
                pool.wait_ge(made, 1)
                factors = spread(pool, lambda dst, src, signed: nc.gpsimd.tensor_scalar(
                    dst, src, sign[:, 0:1], None, ALU.mult) if signed else nc.gpsimd.tensor_copy(dst, src))
                factors(0, 1, lambda d, s: s if d else 7 - s, zp, True)
                factors(1, 1, lambda d, s: LOW - s if d else s, powers, False)
                factors(2, 1, lambda d, s: LOW + 8 - s if d else LOW + 1 + s, powers, False)


def s5_inputs_phase(core, hn, rows, u):
    nc = core.nc
    with Phase(core, "s5i") as ph:
        acc = [ph.ps(f"acc{j}", [P, 4, P]) for j in range(4)]
        turned, taken = ph.sem("turned"), [ph.sem(f"taken{j}") for j in range(2)]
        first = [(k, h) for k in range(SLOTS) for h in range(2)]
        second = range(S5_GROUPS // 4)
        n = len(first) + len(second)
        by_group = rows[:, :].rearrange("m (g t q k) -> m g t q k", g=S5_GROUPS, t=S5_STEPS, q=2)

        def take(eng, copy, mine):
            for j in range(mine, n, 2):
                eng.wait_ge(turned, j + 1)
                if j < len(first):
                    k, h = first[j]
                    for t in range(4):
                        last = copy(by_group[:, :, 4 * h + t, :, k],
                                    acc[j % 4][0:S5_CHUNKS, t, :].rearrange("m (g q) -> m g q", q=2))
                else:
                    g = 4 * (j - len(first))
                    last = copy(u[:, g:g + 4, :], acc[j % 4][:, :, 0:S5_CHUNKS])
                last.then_inc(taken[mine], 1)

        with nc.Block() as block:
            @block.tensor
            def _(pe):
                for j in range(n):
                    if j == len(first):
                        for e in range(2):
                            pe.wait_ge(taken[e], len(first) // 2)
                    elif j >= 4:
                        pe.wait_ge(taken[j % 2], j // 2 - 1)
                    pe.nop(nofuse=True)
                    for t in range(4):
                        if j < len(first):
                            k, h = first[j]
                            last = nc.tensor.transpose(acc[j % 4][0:S5_CHUNKS, t, :], hn[:, k, 4 * h + t::S5_STEPS],
                                                       core.ident[:, :])
                        else:
                            g = 4 * (j - len(first)) + t
                            last = nc.tensor.transpose(acc[j % 4][:, t, 0:S5_CHUNKS], rows[:, g * P:(g + 1) * P],
                                                       core.ident[0:S5_CHUNKS, 0:S5_CHUNKS])
                    last.then_inc(turned, 1)

            @block.scalar
            def _(act):
                take(act, nc.scalar.copy, 0)

            @block.vector
            def _(dve):
                take(dve, nc.vector.tensor_copy, 1)


def output_rows(rows, g):
    view = rows[:, :].rearrange("m (k t p) -> m t p k", k=SLOTS, t=S5_STEPS)
    return view[:, :, bass.ds(2 * g, 2), :]


def group_rows(acc, g2):
    return acc[0:S5_CHUNKS, g2, :].rearrange("m (t q k) -> m t q k", t=S5_STEPS, q=2)


def factored(v, out, tmp, one, two, x1, x2):
    yield v.tensor_tensor(out, one, x1, ALU.mult)
    yield v.tensor_tensor(tmp, two, x2, ALU.mult)
    yield v.tensor_tensor(out, out, tmp, ALU.subtract)


def state_factor(tables, slot, c, n):
    shape = [P, 4, S5_STEPS, S5_CH]

    def tab(part):
        view = tables[:, slot, part, bass.ds(2 * n, 2)].rearrange("p g d t -> p (g d) t")
        return view.unsqueeze(3).to_broadcast(shape)

    def weight(part):
        return c[:, part, bass.ds(2 * n, 2)].rearrange("p g d i -> p (g d) i").unsqueeze(2).to_broadcast(shape)

    return tab(0), tab(1), weight(0), weight(1)


def s5_local_phase(core, u, tables, b, c, rows, state):
    nc = core.nc
    with Phase(core, "s5l") as ph:
        g_mat = [ph.sb(f"g_mat{x}", [P, 4, P]) for x in range(2)]
        f_mat = [ph.sb(f"f_mat{x}", [P, 4, P]) for x in range(2)]
        g_tmp, f_tmp = ph.sb("g_tmp", [P, 4, P]), ph.sb("f_tmp", [P, 4, P])
        g_turned = [ph.sb(f"g_turned{x}", [P, 4, P]) for x in range(2)]
        own = [ph.sb(f"own{x}", [P, 4, P]) for x in range(2)]
        inputs = [ph.sb(f"inputs{x}", [P, 2, S5_CHUNKS]) for x in range(2)]
        masks = ph.sb("masks", [P, 2 * P])
        ps_g, ps_own, ps_add, ps_y = ([ph.ps(f"{k}{x}", [P, 4, P]) for x in range(2)] for k in ("psg", "psown", "psadd", "psy"))
        names = ("masks_loaded", "g_ready", "f_ready", "g_transposed", "g_copied", "own_summed", "own_masked",
                 "inputs_ready", "added", "added_taken", "y_made", "y_taken", "g_chain", "f_chain", "edges")
        s = {k: ph.sem(k) for k in names}
        with nc.Block() as block:
            @block.sync
            def _(sp):
                sp.dma_start(masks[:], core.dram["s5_masks"]).then_inc(s["masks_loaded"], 16)

            @block.gpsimd
            def _(pool):
                nc.gpsimd.memset(state[:, :, 0, :, 0:1], 0.0).then_inc(s["edges"], 1)
                nc.gpsimd.memset(state[:, :, 1, :, S5_CHUNKS:], 0.0).then_inc(s["edges"], 1)
                pool.wait_ge(s["edges"], 2)
                link = Chain(pool, s["f_chain"])
                with pool.Fori(0, S5_GP // 2) as i:
                    pool.nop(nofuse=True)
                    link.restart()
                    for x in range(2):
                        n = 2 * i + x
                        pool.wait_ge(s["own_summed"], n - 1 if x else n)
                        pool.nop(nofuse=True)
                        one, two, x1, x2 = state_factor(tables, 1, c, n)
                        f4 = f_mat[x][:].rearrange("p a (t i) -> p a t i", i=S5_CH)
                        t4 = f_tmp[:].rearrange("p a (t i) -> p a t i", i=S5_CH)
                        link(nc.gpsimd.tensor_tensor(f4, one, x1, ALU.mult))
                        link(nc.gpsimd.tensor_tensor(t4, two, x2, ALU.mult))
                        link(nc.gpsimd.tensor_tensor(f4, f4, t4, ALU.subtract))
                        nc.gpsimd.nop(nofuse=True).then_inc(s["f_ready"], 1)

            @block.vector
            def _(dve):
                dve.wait_ge(s["masks_loaded"], 16)
                link = Chain(dve, s["g_chain"])
                with dve.Fori(0, S5_GP // 2) as i:
                    dve.nop(nofuse=True)
                    link.restart()
                    for x in range(2):
                        n = 2 * i + x
                        dve.wait_ge(s["own_summed"], n - 1 if x else n)
                        shape = [P, 2, 16, S5_CH]

                        def tab(part):
                            return tables[:, 0, part, bass.ds(2 * n, 2)].rearrange("p g d t -> p g (d t)")\
                                .unsqueeze(3).to_broadcast(shape)

                        def weight(part):
                            return b[:, part, bass.ds(2 * n, 2)].unsqueeze(2).to_broadcast(shape)

                        g4 = g_mat[x][:].rearrange("p (g d) (t i) -> p g (d t) i", g=2, i=S5_CH)
                        t4 = g_tmp[:].rearrange("p (g d) (t i) -> p g (d t) i", g=2, i=S5_CH)
                        link(nc.vector.tensor_tensor(g4, tab(0), weight(0), ALU.mult))
                        link(nc.vector.tensor_tensor(t4, tab(1), weight(1), ALU.mult))
                        link(nc.vector.tensor_tensor(g4, g4, t4, ALU.subtract))
                        nc.vector.nop(nofuse=True).then_inc(s["g_ready"], 1)
                    for x in range(2):
                        n = 2 * i + x
                        dve.wait_ge(s["own_summed"], n + 1)
                        dve.wait_ge(s["y_made"], n - 1 if x else n)
                        nc.vector.tensor_tensor(own[x][:].rearrange("p (g d) n -> p g (d n)", g=2),
                                                ps_own[x][:].rearrange("p (g d) n -> p g (d n)", g=2),
                                                masks[:, :].unsqueeze(1).to_broadcast([P, 2, 2 * P]), ALU.mult)\
                          .then_inc(s["own_masked"], 1)

            @block.scalar
            def _(act):
                with act.Fori(0, S5_GP // 2) as i:
                    for x in range(2):
                        n = 2 * i + x
                        act.wait_ge(s["y_made"], n - 1 if x else n)
                        nc.scalar.copy(inputs[x][:], u[:, bass.ds(2 * n, 2), :]).then_inc(s["inputs_ready"], 1)
                        act.wait_ge(s["g_transposed"], n + 1)
                        act.wait_ge(s["added"], n - 1 if x else n)
                        nc.scalar.copy(g_turned[x][:], ps_g[x][:]).then_inc(s["g_copied"], 1)
                    for x in range(2):
                        n = 2 * i + x
                        act.wait_ge(s["added"], n + 1)
                        for d in range(2):
                            last = nc.scalar.copy(
                                state[:, :, d, bass.ds(n, 1), 1 - d:1 - d + S5_CHUNKS].rearrange("p r a m -> p (r a) m"),
                                ps_add[x][:].rearrange("p (r d) n -> p r d n", r=2)[:, :, d, 0:S5_CHUNKS])
                        last.then_inc(s["added_taken"], 1)
                        act.wait_ge(s["y_made"], n + 1)
                        for g2 in range(2):
                            last = nc.scalar.copy(output_rows(rows, 2 * n + g2), group_rows(ps_y[x], g2))
                        last.then_inc(s["y_taken"], 1)

            @block.tensor
            def _(pe):
                with pe.Fori(0, S5_GP // 2) as i:
                    for x in range(2):
                        n = 2 * i + x
                        pe.wait_ge(s["g_ready"], n + 1)
                        pe.wait_ge(s["g_copied"], n - 1 if x else n)
                        for a in range(4):
                            last = nc.tensor.transpose(ps_g[x][:, a, :], g_mat[x][:, a, :], core.ident[:, :])
                        last.then_inc(s["g_transposed"], 1)
                        pe.wait_ge(s["f_ready"], n + 1)
                        pe.wait_ge(s["own_masked"], n - 1 if x else n)
                        for a in range(4):
                            last = nc.tensor.matmul(ps_own[x][:, a, :], g_mat[x][:, a, :], f_mat[x][:, a, :],
                                                    start=True, stop=True)
                        last.then_inc(s["own_summed"], 1)
                    for x in range(2):
                        n = 2 * i + x
                        pe.wait_ge(s["g_copied"], n + 1)
                        pe.wait_ge(s["inputs_ready"], n + 1)
                        pe.wait_ge(s["added_taken"], n - 1 if x else n)
                        pe.nop(nofuse=True)
                        for g2 in range(2):
                            for d in range(2):
                                for r in range(2):
                                    last = nc.tensor.matmul(
                                        ps_add[x][S5_P * g2:S5_P * (g2 + 1), 2 * r + d, 0:S5_CHUNKS],
                                        g_turned[x][:, 2 * g2 + d, S5_P * r:S5_P * (r + 1)], inputs[x][:, g2, :],
                                        start=True, stop=True)
                        last.then_inc(s["added"], 1)
                        pe.wait_ge(s["own_masked"], n + 1)
                        pe.wait_ge(s["y_taken"], n - 1 if x else n)
                        pe.nop(nofuse=True)
                        for g2 in range(2):
                            for d in range(2):
                                last = nc.tensor.matmul(ps_y[x][0:S5_CHUNKS, g2, :], inputs[x][:, g2, :],
                                                        own[x][:, 2 * g2 + d, :], start=(d == 0), stop=(d == 1))
                        last.then_inc(s["y_made"], 1)


def s5_scan_phase(core, state, a8):
    nc = core.nc
    with Phase(core, "s5s") as ph:
        mults = [ph.sb(f"mults{d}", [P, 2, 2, S5_GP]) for d in range(2)]
        multiplied, summed, stepped = ([ph.sem(f"{k}{d}") for d in range(2)] for k in ("multiplied", "summed", "stepped"))
        ready = [ph.sem(f"ready{d}") for d in range(2)]
        same = ph.sb("same", [P, 2, 2, S5_GP])

        def scan(eng, ops, d):
            for r in range(2):
                last = ops.tensor_copy(same[:, d, r], a8[:, 0, d])
            last.then_inc(ready[d], 1)
            eng.wait_ge(ready[d], 1)
            with eng.Fori(0, S5_CHUNKS) as m:
                before = m if d == 0 else S5_CHUNKS - m
                after = m + 1 if d == 0 else S5_CHUNKS - 1 - m

                def at(place, r=slice(0, 2)):
                    return state[:, r, d, :, bass.ds(place, 1)].rearrange("p r g a -> p r (g a)")

                eng.wait_ge(stepped[d], m)
                eng.nop(nofuse=True)
                ops.tensor_tensor(mults[d][:, 0], at(before), same[:, d], ALU.mult)
                ops.tensor_tensor(mults[d][:, 1, 0:1], at(before, slice(1, 2)), a8[:, 2:3, d], ALU.mult)
                ops.tensor_tensor(mults[d][:, 1, 1:2], at(before, slice(0, 1)), a8[:, 1:2, d], ALU.mult)\
                   .then_inc(multiplied[d], 1)
                eng.wait_ge(multiplied[d], m + 1)
                ops.tensor_tensor(mults[d][:, 0], mults[d][:, 0], mults[d][:, 1], ALU.add).then_inc(summed[d], 1)
                eng.wait_ge(summed[d], m + 1)
                eng.nop(nofuse=True)
                ops.tensor_tensor(at(after), at(after), mults[d][:, 0], ALU.add).then_inc(stepped[d], 1)

        with nc.Block() as block:
            @block.vector
            def _(dve):
                scan(dve, nc.vector, 0)

            @block.gpsimd
            def _(pool):
                scan(pool, nc.gpsimd, 1)


def s5_swap_phase(core, state, swapped):
    nc = core.nc
    with Phase(core, "s5w") as ph:
        moved = ph.sem("moved")
        with nc.Block() as block:
            @block.sync
            def _(sp):
                for g2 in range(2):
                    for r in range(2):
                        sp.dma_start(swapped[S5_P * r:S5_P * (r + 1), g2], state[S5_P * g2:S5_P * (g2 + 1), r])\
                          .then_inc(moved, 16)
                sp.wait_ge(moved, 4 * 16)


def s5_entering_phase(core, swapped, tables, c, rows):
    nc = core.nc
    with Phase(core, "s5e") as ph:
        f_mat = [ph.sb(f"f_mat{x}", [P, 4, P]) for x in range(2)]
        f_tmp = ph.sb("f_tmp", [P, 4, P])
        entering = [ph.sb(f"entering{x}", [P, 2, 2, S5_CHUNKS]) for x in range(2)]
        ps_y = [ph.ps(f"psy{x}", [P, 4, P]) for x in range(2)]
        s = {k: ph.sem(k) for k in ("f_ready", "entering_ready", "y_made", "y_added", "chain")}
        with nc.Block() as block:
            @block.vector
            def _(dve):
                link = Chain(dve, s["chain"])
                with dve.Fori(0, S5_GP // 2) as i:
                    dve.nop(nofuse=True)
                    link.restart()
                    for x in range(2):
                        n = 2 * i + x
                        one, two, x1, x2 = state_factor(tables, 2, c, n)
                        f4 = f_mat[x][:].rearrange("p a (t i) -> p a t i", i=S5_CH)
                        t4 = f_tmp[:].rearrange("p a (t i) -> p a t i", i=S5_CH)
                        link(nc.vector.tensor_tensor(f4, one, x1, ALU.mult))
                        link(nc.vector.tensor_tensor(t4, two, x2, ALU.mult))
                        link(nc.vector.tensor_tensor(f4, f4, t4, ALU.subtract))
                        nc.vector.nop(nofuse=True).then_inc(s["f_ready"], 1)
                    for x in range(2):
                        n = 2 * i + x
                        dve.wait_ge(s["y_made"], n + 1)
                        for g2 in range(2):
                            dst = output_rows(rows, 2 * n + g2)
                            last = nc.vector.tensor_tensor(dst, group_rows(ps_y[x], g2), dst, ALU.add)
                        last.then_inc(s["y_added"], 1)

            @block.scalar
            def _(act):
                with act.Fori(0, S5_GP // 2) as i:
                    for x in range(2):
                        n = 2 * i + x
                        act.wait_ge(s["y_made"], n - 1 if x else n)
                        for d in range(2):
                            last = nc.scalar.copy(
                                entering[x][:, :, d, :],
                                swapped[:, :, d, bass.ds(n, 1), d:d + S5_CHUNKS].rearrange("p g a m -> p (g a) m"))
                        last.then_inc(s["entering_ready"], 1)

            @block.tensor
            def _(pe):
                with pe.Fori(0, S5_GP // 2) as i:
                    for x in range(2):
                        n = 2 * i + x
                        pe.wait_ge(s["f_ready"], n + 1)
                        pe.wait_ge(s["entering_ready"], n + 1)
                        pe.wait_ge(s["y_added"], n - 1 if x else n)
                        pe.nop(nofuse=True)
                        for g2 in range(2):
                            for d in range(2):
                                last = nc.tensor.matmul(ps_y[x][0:S5_CHUNKS, g2, :], entering[x][:, g2, d, :],
                                                        f_mat[x][:, 2 * g2 + d, :], start=(d == 0), stop=(d == 1))
                        last.then_inc(s["y_made"], 1)


def s5_outputs_phase(core, rows, hn):
    nc = core.nc
    with Phase(core, "s5o") as ph:
        d_gain = ph.sb("d_gain", [P, SLOTS])
        acc = [ph.ps(f"acc{j}", [P, 4, P]) for j in range(4)]
        loaded, turned, added, slot_done = (ph.sem(k) for k in ("loaded", "turned", "added", "slot_done"))
        tiles = [(k, h) for k in range(SLOTS) for h in range(2)]
        with nc.Block() as block:
            @block.sync
            def _(sp):
                sp.dma_start(d_gain[:], core.dram["s5_d"]).then_inc(loaded, 16)

            @block.tensor
            def _(pe):
                for j, (k, h) in enumerate(tiles):
                    if j >= 4:
                        pe.wait_ge(added, j - 3)
                    for t in range(4):
                        at = (k * S5_STEPS + 4 * h + t) * P
                        last = nc.tensor.transpose(acc[j % 4][:, t, 0:S5_CHUNKS], rows[:, at:at + P],
                                                   core.ident[0:S5_CHUNKS, 0:S5_CHUNKS])
                    last.then_inc(turned, 1)

            @block.vector
            def _(dve):
                dve.wait_ge(loaded, 16)
                for j, (k, h) in enumerate(tiles):
                    dve.wait_ge(turned, j + 1)
                    x = hn[:, k, :].rearrange("p (m t) -> p t m", t=S5_STEPS)[:, 4 * h:4 * h + 4]
                    nc.vector.scalar_tensor_tensor(out=x, in0=x, scalar=d_gain[:, k:k + 1],
                                                   in1=acc[j % 4][:, :, 0:S5_CHUNKS], op0=ALU.mult, op1=ALU.add)\
                      .then_inc(added, 1)

            @block.scalar
            def _(act):
                for k in range(SLOTS):
                    act.wait_ge(added, 2 * k + 2)
                    nc.scalar.activation(hn[:, k], hn[:, k], ACT.Gelu_apprx_tanh).then_inc(slot_done, 1)


def glu_phase(core, hn):
    nc = core.nc

    def outcome(ph, acc, multiplied, drained):
        gate = ph.sb("gate", [P, N_TOK])
        gated, product_made = ph.sem("gated"), ph.sem("product_made")

        def two(ap):
            return ap.rearrange("p (h n) -> p h n", h=2)

        def takers(block):
            @block.scalar
            def _(act):
                with act.Fori(0, SLOTS) as i:
                    act.wait_ge(multiplied[1], i + 1)
                    act.wait_ge(drained[0], i)
                    act.nop(nofuse=True)
                    nc.scalar.activation(two(gate[:, :]), acc[1][:, :, 0:HALF], ACT.Sigmoid).then_inc(drained[1], 1)

            @block.vector
            def _(dve):
                with dve.Fori(0, SLOTS) as i:
                    dve.wait_ge(multiplied[0], i + 1)
                    dve.wait_ge(drained[1], i + 1)
                    nc.vector.tensor_tensor(two(gate[:, :]), acc[0][:, :, 0:HALF], two(gate[:, :]), ALU.mult)\
                      .then_inc(product_made, 1)
                    dve.wait_ge(product_made, i + 1)
                    h = core.hT[:, bass.ds(i, 1), :].rearrange("p a n -> p (a n)")
                    nc.vector.tensor_tensor(h, h, gate[:, :], ALU.add).then_inc(drained[0], 1)
        return takers

    dense_phase(core, "glu", core.dram["w_glu"], SLOTS, hn, outcome)


def store_phase(core, result, stored):
    nc = core.nc
    with nc.Block() as block:
        @block.sync
        def _(sp):
            sp.dma_start(core.dram["out"], result[:, :, N_META:]).then_inc(stored, 16)
            sp.wait_ge(stored, 16)



def features(a):
    return a.reshape(P, SLOTS, *a.shape[1:])


def column_tiles(w, columns, rows_are_features=True):
    rows = features(w) if rows_are_features else w.reshape(SLOTS, P, -1).transpose(1, 0, 2)
    return np.stack([rows[:, :, c] for c in columns])


def in_pairs(tiles):
    return np.ascontiguousarray(tiles.reshape(-1, 2, P, SLOTS, P).transpose(0, 2, 1, 3, 4))


def attention_bias(rpb):
    ci = np.arange(16)[:, None, None, None]
    r = np.arange(8)[None, :, None, None]
    cj = np.arange(32)[None, None, :, None]
    rk = np.arange(8)[None, None, None, :]
    out = np.zeros((8, 3, P, N_META + 2 * P), rpb.dtype)
    for kind, block in enumerate((0, 1, 3)):
        base = 8 * WIN_FIRST[block]
        c, ck = 16 * block + ci, base + cj
        start = np.clip(c - 8, 0, GRID_W - 16)
        inside = np.broadcast_to((ck >= start) & (ck < start + 16), (16, 8, 32, 8))
        dc = np.clip(ck - c + 15, 0, 30)
        dr = rk - r + 7
        spread = rpb[:, np.broadcast_to(dr, inside.shape), np.broadcast_to(dc, inside.shape)]
        spread = np.where(inside[None], spread, rpb.dtype.type(-1e30))
        out[:, kind, :, N_META:] = spread.reshape(8, P, 2 * P)
    return np.ascontiguousarray(out.reshape(N_PAIRS, 2, 3, P, -1).transpose(0, 3, 2, 1, 4))


def rwkv_layout(w):
    pairs = lambda a: a.reshape(N_PAIRS, P).T
    up = np.stack([np.concatenate([w["rwkv_w_up"][d], w["rwkv_a_up"][d]], axis=0) for d in range(2)]
                  + [w["rwkv_g_up"]])
    vec = [w["rwkv_w0"][0], w["rwkv_w0"][1], w["rwkv_a0"][0], w["rwkv_a0"][1], w["rwkv_k_k"], w["rwkv_k_a"],
           w["rwkv_r_k"].reshape(-1)]
    return {"mu": np.ascontiguousarray(w["rwkv_mu"].reshape(N_SHIFT, P).T),
            "rw_up": np.ascontiguousarray(up.reshape(3, P, N_PAIRS, P).transpose(2, 1, 0, 3)),
            "rw_vec": np.ascontiguousarray(np.stack([pairs(a) for a in vec], axis=-1)),
            "rw_ln": np.ascontiguousarray(np.stack([pairs(w["rwkv_lnx_g"]), pairs(w["rwkv_lnx_b"])], axis=-1))}


def route_consts():
    row = np.concatenate([np.arange(8, 0, -1), np.arange(N_EXPERTS) * CAP, np.arange(MAX_ROUNDS) * CAP])
    token = np.arange(P)[:, None] + P * np.arange(N_TILES)[None, :]
    consts = np.concatenate([np.tile(row, (P, 1)), token < N_TOK], axis=1).astype(np.float32)
    return {"route_consts": consts, "token_order": np.triu(np.ones((P, P), np.float32), 1),
            "places": np.tile(np.arange(CAP, dtype=np.float32), (P, 1))}


def route_layout(w_group, b_group, w_expert, b_expert):
    w = np.concatenate([w_group, w_expert.transpose(1, 0, 2).reshape(D, N_EXPERTS)], axis=1)
    b = np.concatenate([b_group, b_expert.reshape(-1)])
    return np.ascontiguousarray(features(w)), np.ascontiguousarray(np.tile(b, (P, 1)))


def s5_layout(w):
    twice = lambda a: np.concatenate([a, a], axis=0)
    lam = [w["s5_lambda_re"], w["s5_lambda_im"], np.broadcast_to(w["s5_log_step"][..., None], (2, S5_GROUPS, S5_P))]
    lam = np.stack([twice(a.transpose(2, 0, 1).reshape(S5_P, -1)) for a in lam], axis=1)
    b = [w["s5_b_re"].transpose(1, 0, 2), w["s5_b_im"].transpose(1, 0, 2)]
    c = [w["s5_c_re"].transpose(3, 1, 0, 2), w["s5_c_im"].transpose(3, 1, 0, 2)]
    both = lambda x: np.ascontiguousarray(np.stack([np.concatenate([x[0], x[1]]), np.concatenate([x[1], x[0]])], axis=1))
    step = np.arange(P) // S5_CH
    masks = np.concatenate([step[:, None] <= step[None, :], step[:, None] >= step[None, :]], axis=1)
    return {"s5_lam": np.ascontiguousarray(lam), "s5_b": both(b), "s5_c": both(c),
            "s5_masks": masks.astype(np.float32), "s5_d": np.ascontiguousarray(w["s5_d"].reshape(P, SLOTS))}



def build_program(nc, dram):
    core = Core(nc, dram)

    def keep(name, shape):
        return nc.alloc_sbuf_tensor(name, shape, F32)

    core.hT = keep("hT", [P, SLOTS, N_TOK])
    core.gains = keep("gains", [P, N_GAINS, SLOTS])
    core.ones, core.ones_head, core.ident = (keep(name, [P, P]) for name in ("ones", "ones_head", "ident"))
    core.scratch = nc.dram_tensor("expert_rows", [N_EXPERTS * CAP, D], F32, kind="Internal").ap()
    stored = nc.alloc_semaphore("result_stored")
    states = [P, SLOTS, N_TOK]
    setup_phase(core)
    with nc.sbuf_tensor("mix", states, F32) as mix:
        projected = ExitStack()
        raw = projected.enter_context(nc.sbuf_tensor("raw", [P, N_SHIFT, N_TOK + 2], F32, side="right"))
        with nc.sbuf_tensor("hn0", states, F32) as hn:
            norm_phase(core, 0, hn)
            with nc.sbuf_tensor("queries_keys", [P, 2 * N_PAIRS, N_TOK], F32) as qk, \
                    nc.sbuf_tensor("values", [P, 8, NA_WIDTH], F32) as values:
                query_key_phase(core, hn, qk)
                value_phase(core, hn, values)
                attention_phase(core, qk, values, mix)
            rwkv_projection_phase(core, hn, raw)
        rwkv(core, raw, projected.close, mix)
        output_projection_phase(core, mix)
    with nc.sbuf_tensor("hn1", states, F32) as hn:
        norm_phase(core, 1, hn)
        moe(core, 0, hn)
    with nc.sbuf_tensor("hn2", states, F32) as hn:
        norm_phase(core, 2, hn)
        s5(core, hn)
        glu_phase(core, hn)
    with nc.sbuf_tensor("hn3", states, F32) as hn:
        norm_phase(core, 3, hn)
        moe(core, 1, hn)
    with nc.sbuf_tensor("result", states, F32) as result:
        norm_phase(core, 4, result)
        store_phase(core, result, stored)


def lay_out(w):
    h = np.concatenate([w["meta_tokens"], w["x"][0]], axis=0)
    gains = [w["norm_mix"][0], w["norm_ffn"][0], w["norm_mix"][1], w["norm_ffn"][1], w["norm_final"]]
    w_in = w["mix_w_in"][0]
    run = lambda at: np.arange(at, at + P)
    qk = [run(part * NA_WIDTH + P * j) for j in range(N_PAIRS) for part in range(2)]
    slot = lambda m: SLOTS * np.arange(P) + m
    glu = [slot(m) + part * D for m in range(SLOTS) for part in range(2)]
    out = {"hT": np.ascontiguousarray(h.T.reshape(P, SLOTS, N_TOK)),
           "gains": np.ascontiguousarray(np.stack([g.reshape(P, SLOTS) for g in gains], axis=1)),
           "w_qk": in_pairs(column_tiles(w_in, qk)),
           "w_v": np.ascontiguousarray(features(w_in)[:, :, 2 * NA_WIDTH:3 * NA_WIDTH]),
           "w_rw": in_pairs(column_tiles(w_in, [run(3 * NA_WIDTH + P * j) for j in range(N_SHIFT)])),
           "bias": attention_bias(w["na_rpb"][0]),
           "w_out": in_pairs(column_tiles(w["mix_w_out"][0], [slot(m) for m in range(SLOTS)], rows_are_features=False)),
           "w_glu": in_pairs(column_tiles(w["s5_w_glu"][0], glu))}
    out.update(chunk_masks())
    out.update(rwkv_layout({k: a[0] for k, a in w.items() if k.startswith("rwkv")}))
    out.update(s5_layout({k: a[0] for k, a in w.items() if k.startswith("s5")}))
    out.update(route_consts())
    for layer in range(2):
        out[f"route_w{layer}"], out[f"route_b{layer}"] = route_layout(
            *[w[f"moe_{name}"][layer] for name in ("w_group", "b_group", "w_expert", "b_expert")])
    for name in ("moe_w1", "moe_w3", "moe_w2"):
        out[name] = w[name]
    return out


def kernel(**inputs):
    import concourse.bacc as bacc
    from concourse.bass_utils import run_bass_kernel_spmd

    nc = bacc.Bacc("TRN2", target_bir_lowering=False, num_devices=1)
    arrays, dram = {}, {}
    for name, a in lay_out({k: np.asarray(v) for k, v in inputs.items()}).items():
        a = np.ascontiguousarray(a)
        arrays[f"in_{name}"] = a
        dram[name] = nc.dram_tensor(f"in_{name}", a.shape, mybir.dt.from_np(a.dtype), kind="ExternalInput").ap()
    dram["out"] = nc.dram_tensor("out_states", [P, SLOTS, SEQ], F32, kind="ExternalOutput").ap()
    build_program(nc, dram)
    result = run_bass_kernel_spmd(nc, [arrays], core_ids=[0]).results[0]["out_states"]
    return np.ascontiguousarray(result.reshape(D, SEQ).T[None])
```

```python
import math
from contextlib import ExitStack

import numpy as np

import concourse.bass as bass
from concourse import mybir

F32 = mybir.dt.float32
I32 = mybir.dt.int32
U32 = mybir.dt.uint32
ALU = mybir.AluOpType
ACT = mybir.ActivationFunctionType
AX = mybir.AxisListType

P = 128
D = 1024
SLOTS = D // P
N_META = 16
SEQ = 512
N_TOK = N_META + SEQ
HALF = N_TOK // 2
GRID_W = 64
GRID_H = SEQ // GRID_W
HD = 64
N_PAIRS = 4
NORM_EPS = 1e-6
N_GAINS = 5


class Core:

    def __init__(self, nc, dram):
        self.nc = nc
        self.dram = dram


class Phase:

    def __init__(self, core, name):
        self.core, self.nc, self.name = core, core.nc, name
        self.stack = ExitStack()
        self.sems = []

    def __enter__(self):
        return self

    def __exit__(self, *exc):
        self.stack.close()
        if exc[0] is None and self.sems:
            numbers = sorted(s.num for s in self.sems)
            assert numbers == list(range(numbers[0], numbers[0] + len(numbers)))
            self.nc.all_engine_barrier(sems_to_clear=range(numbers[0], numbers[-1] + 1))
            self.nc.prepend_free_semaphores(numbers)

    def sb(self, name, shape, dtype=F32):
        return self.stack.enter_context(self.nc.sbuf_tensor(f"{self.name}_{name}", shape, dtype))

    def ps(self, name, shape, dtype=F32):
        return self.stack.enter_context(self.nc.psum_tensor(f"{self.name}_{name}", shape, dtype))

    def sem(self, name):
        s = self.nc.alloc_semaphore(f"{self.name}_{name}")
        self.sems.append(s)
        return s

    def prime(self):
        for s in self.sems:
            self.nc.sync.nop(nofuse=True).then_inc(s, 1)

    def block(self):
        self.prime()
        self.nc.all_engine_barrier()
        return self.nc.Block()


class Chain:

    def __init__(self, engine, sem):
        self.engine, self.sem, self.n = engine, sem, 1

    def __call__(self, instruction):
        self.n += 1
        instruction.then_inc(self.sem, 1)
        self.engine.wait_ge(self.sem, self.n)

    def restart(self):
        self.engine.sem_clear(self.sem)
        self.n = 0



def setup_phase(core):
    nc, dram = core.nc, core.dram
    with Phase(core, "setup") as ph:
        loaded = [ph.sem(f"loaded{i}") for i in range(3)]
        zeroed, ready = ph.sem("zeroed"), ph.sem("ready")
        with ph.block() as block:
            @block.sync
            def _(sp):
                sp.dma_start(core.hT[:], dram["hT"]).then_inc(loaded[0], 16)
                sp.dma_start(core.gains[:], dram["gains"]).then_inc(loaded[1], 16)
                for s in loaded[:2]:
                    sp.wait_ge(s, 1 + 16)

            @block.gpsimd
            def _(pool):
                nc.gpsimd.memset(core.ones[:], 1.0)
                nc.gpsimd.memset(core.ident[:], 0.0).then_inc(zeroed, 1)
                pool.wait_ge(zeroed, 1 + 1)
                nc.gpsimd.affine_select(out=core.ident[:], in_=core.ident[:], compare_op=ALU.not_equal,
                                        fill=1.0, base=0, pattern=[[-1, P]], channel_multiplier=1)

            @block.vector
            def _(dve):
                nc.vector.memset(core.ones_head[:], 0.0).then_inc(ready, 1)
                dve.wait_ge(ready, 1 + 1)
                nc.vector.memset(core.ones_head[0:HD, 0:HD], 1.0)
                nc.vector.memset(core.ones_head[HD:, HD:], 1.0)


def norm_phase(core, which, dst):
    nc = core.nc
    with Phase(core, f"norm{which}") as ph:
        squares = ph.sb("squares", [P, SLOTS, N_TOK])
        rstd = ph.sb("rstd", [P, N_TOK])
        eps = ph.sb("eps", [P, 1])
        total = ph.ps("total", [P, 2, 512])
        squared, summed, rooted, eps_set = (ph.sem(n) for n in ("squared", "summed", "rooted", "eps_set"))
        inverted = ph.sem("inverted")
        with ph.block() as block:
            @block.scalar
            def _(act):
                for s in range(0, SLOTS, 2):
                    nc.scalar.activation(squares[:, s], core.hT[:, s], ACT.Square).then_inc(squared, 1)
                act.wait_ge(summed, 1 + 1)
                act.wait_ge(eps_set, 1 + 1)
                nc.scalar.activation(rstd[:, :].rearrange("p (h n) -> p h n", h=2), total[:, :, 0:HALF],
                                     ACT.Sqrt, bias=eps[:, 0:1], scale=1.0 / D).then_inc(rooted, 1)

            @block.gpsimd
            def _(pool):
                for s in range(1, SLOTS, 2):
                    nc.gpsimd.tensor_tensor(squares[:, s], core.hT[:, s], core.hT[:, s], ALU.mult)\
                      .then_inc(squared, 1)

            @block.tensor
            def _(pe):
                pe.wait_ge(squared, 1 + SLOTS)
                for h in range(2):
                    for s in range(SLOTS):
                        last = nc.tensor.matmul(total[:, h, 0:HALF], core.ones[:, :],
                                                squares[:, s, h * HALF:(h + 1) * HALF],
                                                start=(s == 0), stop=(s == SLOTS - 1))
                last.then_inc(summed, 1)

            @block.vector
            def _(dve):
                nc.vector.memset(eps[:, :], NORM_EPS).then_inc(eps_set, 1)
                dve.wait_ge(rooted, 1 + 1)
                nc.vector.reciprocal(rstd[:, :], rstd[:, :]).then_inc(inverted, 1)
                dve.wait_ge(inverted, 1 + 1)
                for s in range(SLOTS):
                    nc.vector.scalar_tensor_tensor(out=dst[:, s], in0=core.hT[:, s],
                                                   scalar=core.gains[:, which, s:s + 1], in1=rstd[:, :],
                                                   op0=ALU.mult, op1=ALU.mult)


def dense_phase(core, name, weights, n_turns, rhs, outcome, cut=HALF):
    nc = core.nc
    spans = [(0, cut), (cut, N_TOK)]
    with Phase(core, name) as ph:
        ring = ph.sb("ring", [P, 2, SLOTS, P])
        acc = [ph.ps(f"acc{u}", [P, 2, 512]) for u in range(2)]
        loaded = [ph.sem(f"loaded{u}") for u in range(2)]
        multiplied = [ph.sem(f"multiplied{u}") for u in range(2)]
        drained = [ph.sem(f"drained{u}") for u in range(2)]
        takers = outcome(ph, acc, multiplied, drained)
        with ph.block() as block:
            @block.sync
            def _(sp):
                with sp.Fori(0, n_turns) as i:
                    for u in range(2):
                        sp.wait_ge(multiplied[u], 1 + i)
                        sp.nop(nofuse=True)
                        sp.dma_start(ring[:, u], weights[bass.ds(i, 1), :, u]
                                     .rearrange("a p s m -> (a p) s m")).then_inc(loaded[u], 16)

            @block.tensor
            def _(pe):
                with pe.Fori(0, n_turns) as i:
                    for u in range(2):
                        pe.wait_ge(loaded[u], 1 + 16 * i + 16)
                        pe.wait_ge(drained[u], 1 + i)
                        for h, (lo, hi) in enumerate(spans):
                            for s in range(SLOTS):
                                last = nc.tensor.matmul(acc[u][:, h, 0:hi - lo], ring[:, u, s], rhs[:, s, lo:hi],
                                                        start=(s == 0), stop=(s == SLOTS - 1))
                        last.then_inc(multiplied[u], 1)

            takers(block)



def by_columns(ap):
    return ap.rearrange("p (r c) -> p c r", c=GRID_W)


def query_key_phase(core, hn, qk):
    nc = core.nc
    cut = N_META + SEQ // 2
    rows = GRID_H // 2

    def outcome(ph, acc, multiplied, drained):
        def takers(block):
            def take(copy, i, u):
                dst = qk[:, bass.ds(2 * i + u, 1), :].rearrange("p a n -> p (a n)")
                grid = dst[:, N_META:N_TOK].rearrange("p (c r) -> p r c", r=GRID_H)
                copy(dst[:, 0:N_META], acc[u][:, 0, 0:N_META])
                copy(grid[:, 0:rows, :], acc[u][:, 0, N_META:cut].rearrange("p (r c) -> p r c", r=rows))
                return copy(grid[:, rows:, :], acc[u][:, 1, 0:SEQ // 2].rearrange("p (r c) -> p r c", r=rows))

            @block.scalar
            def _(act):
                with act.Fori(0, N_PAIRS) as i:
                    act.wait_ge(multiplied[0], 1 + i + 1)
                    take(nc.scalar.copy, i, 0).then_inc(drained[0], 1)

            @block.vector
            def _(dve):
                with dve.Fori(0, N_PAIRS) as i:
                    dve.wait_ge(multiplied[1], 1 + i + 1)
                    take(nc.vector.tensor_copy, i, 1).then_inc(drained[1], 1)
        return takers

    dense_phase(core, "qk", core.dram["w_qk"], N_PAIRS, hn, outcome, cut=cut)


N_SHIFT = 14


def rwkv_projection_phase(core, hn, raw):
    nc = core.nc

    def outcome(ph, acc, multiplied, drained):
        def takers(block):
            def take(copy, i, u):
                dst = raw[:, bass.ds(2 * i + u, 1), 1:1 + N_TOK].rearrange("p a (h n) -> p (a h) n", h=2)
                return copy(dst, acc[u][:, :, 0:HALF])

            @block.gpsimd
            def _(pool):
                nc.gpsimd.memset(raw[:, :, 0:1], 0.0)
                nc.gpsimd.memset(raw[:, :, N_TOK + 1:], 0.0)

            @block.scalar
            def _(act):
                with act.Fori(0, N_SHIFT // 2) as i:
                    act.wait_ge(multiplied[0], 1 + i + 1)
                    take(nc.scalar.copy, i, 0).then_inc(drained[0], 1)

            @block.vector
            def _(dve):
                with dve.Fori(0, N_SHIFT // 2) as i:
                    dve.wait_ge(multiplied[1], 1 + i + 1)
                    take(nc.vector.tensor_copy, i, 1).then_inc(drained[1], 1)
        return takers

    dense_phase(core, "rw", core.dram["w_rw"], N_SHIFT // 2, hn, outcome)


NA_WIDTH = 512
N_BLOCKS = 4
WIN_FIRST = [0, 1, 3, 4]
WIN_TYPE = [0, 1, 1, 2]
WIN_V = [(0, 1), (4, 5), (5, 6), (2, 3)]
V_META = 7


def value_phase(core, hn, values):
    nc = core.nc
    with Phase(core, "val") as ph:
        w = ph.sb("w", [P, SLOTS, NA_WIDTH])
        grid = ph.sb("grid", [P, SLOTS, SEQ])
        acc = [ph.ps(f"acc{u}", [P, 512]) for u in range(2)]
        loaded, multiplied, drained, shifted = (ph.sem(n) for n in ("loaded", "multiplied", "drained", "shifted"))
        ordered = ph.sem("ordered")
        tiles = [0, 1, 2, 3, V_META]
        with ph.block() as block:
            @block.sync
            def _(sp):
                sp.dma_start(w[:], core.dram["w_v"]).then_inc(loaded, 16)
                for t in range(3):
                    sp.wait_ge(drained, 1 + t + 2)
                    sp.dma_start(values[0:64, 4 + t], values[64:128, t]).then_inc(shifted, 16)
                    sp.dma_start(values[64:128, 4 + t], values[0:64, t + 1]).then_inc(shifted, 16)
                sp.wait_ge(shifted, 1 + 6 * 16)

            @block.scalar
            def _(act):
                for s in range(0, SLOTS, 2):
                    nc.scalar.copy(grid[:, s].rearrange("p (c r) -> p c r", r=GRID_H), by_columns(hn[:, s, N_META:]))\
                      .then_inc(ordered, 1)

            @block.gpsimd
            def _(pool):
                for s in range(1, SLOTS, 2):
                    nc.gpsimd.tensor_copy(grid[:, s].rearrange("p (c r) -> p c r", r=GRID_H),
                                          by_columns(hn[:, s, N_META:])).then_inc(ordered, 1)

            @block.tensor
            def _(pe):
                pe.wait_ge(loaded, 1 + 16)
                pe.wait_ge(ordered, 1 + SLOTS)
                for n, t in enumerate(tiles):
                    if n >= 2:
                        pe.wait_ge(drained, 1 + n - 1)
                    rows = N_META if t == V_META else P
                    for s in range(SLOTS):
                        tokens = hn[:, s, 0:N_META] if t == V_META else grid[:, s, P * t:P * (t + 1)]
                        last = nc.tensor.matmul(acc[n % 2][0:rows, :], tokens, w[:, s],
                                                start=(s == 0), stop=(s == SLOTS - 1))
                    last.then_inc(multiplied, 1)

            @block.vector
            def _(dve):
                for n, t in enumerate(tiles):
                    rows = N_META if t == V_META else P
                    dve.wait_ge(multiplied, 1 + n + 1)
                    nc.vector.tensor_copy(values[0:rows, t], acc[n % 2][0:rows, :]).then_inc(drained, 1)



def attention_phase(core, qk, values, mix):
    nc = core.nc
    n_keys = N_META + 2 * P
    tiles = [(hh, b) for hh in range(2) for b in range(N_BLOCKS + 1)]
    T = len(tiles)
    with Phase(core, "att") as ph:
        q = ph.sb("q", [P, N_TOK])
        k = ph.sb("k", [P, N_TOK])
        v = ph.sb("v", [P, 8, P])
        bias = ph.sb("bias", [P, 3, 2, n_keys])
        scores = ph.sb("scores", [P, 2, n_keys])
        probs = ph.sb("probs", [P, 2, n_keys])
        turned = ph.sb("turned", [P, 2, 3, P])
        neg_max = ph.sb("neg_max", [P, T])
        row_sum = ph.sb("row_sum", [P, T])
        inverse = ph.sb("inverse", [P, T])
        sc = [ph.ps(f"sc{u}", [P, 512]) for u in range(2)]
        tp = [ph.ps(f"tp{u}", [P, 4, P]) for u in range(2)]
        out = ph.ps("out", [P, 512])
        out_meta = ph.ps("out_meta", [P, 512])
        names = ("bias_loaded", "staged", "scored", "biased", "maxed", "exped", "inverted", "normed",
                 "turned_ps", "turned_sb", "weighted", "stored")
        s = {n: ph.sem(n) for n in names}
        scale = HD ** -0.5

        def size(b):
            return (N_META, N_META) if b == N_BLOCKS else (P, n_keys)

        with ph.block() as block:
            @block.sync
            def _(sp):
                with sp.Fori(0, N_PAIRS) as i:
                    sp.wait_ge(s["biased"], 1 + T * i)
                    sp.nop(nofuse=True)
                    sp.dma_start(bias[:], core.dram["bias"][bass.ds(i, 1)].rearrange("a p t h n -> (a p) t h n"))\
                      .then_inc(s["bias_loaded"], 16)

            @block.gpsimd
            def _(pool):
                with pool.Fori(0, N_PAIRS) as i:
                    pool.wait_ge(s["weighted"], 1 + T * i)
                    nc.gpsimd.tensor_copy(q[:, :], qk[:, bass.ds(2 * i, 1), :].rearrange("p a n -> p (a n)"))\
                      .then_inc(s["staged"], 1)
                    nc.gpsimd.tensor_copy(k[:, :], qk[:, bass.ds(2 * i + 1, 1), :].rearrange("p a n -> p (a n)"))\
                      .then_inc(s["staged"], 1)
                    nc.gpsimd.tensor_copy(v[:, 0:7, :], values[:, 0:7, bass.ds(P * i, P)]).then_inc(s["staged"], 1)
                    nc.gpsimd.tensor_copy(v[0:N_META, 7, :], values[0:N_META, 7, bass.ds(P * i, P)])\
                      .then_inc(s["staged"], 1)

            @block.tensor
            def _(pe):
                with pe.Fori(0, N_PAIRS) as i:
                    def score(n):
                        hh, b = tiles[n]
                        lo = hh * HD
                        if n >= 2:
                            pe.wait_ge(s["biased"], 1 + T * i + n - 1)
                        pe.nop(nofuse=True)
                        if b == N_BLOCKS:
                            nc.tensor.matmul(sc[n % 2][0:N_META, 0:N_META], q[lo:lo + HD, 0:N_META],
                                             k[lo:lo + HD, 0:N_META], start=True, stop=True).then_inc(s["scored"], 1)
                            return
                        queries = q[lo:lo + HD, N_META + P * b:N_META + P * (b + 1)]
                        first = N_META + 64 * WIN_FIRST[b]
                        nc.tensor.matmul(sc[n % 2][:, 0:N_META], queries, k[lo:lo + HD, 0:N_META], start=True, stop=True)
                        nc.tensor.matmul(sc[n % 2][:, N_META:n_keys], queries, k[lo:lo + HD, first:first + 2 * P],
                                         start=True, stop=True).then_inc(s["scored"], 1)

                    def turn(n):
                        _, b = tiles[n]
                        rows, keys = size(b)
                        pe.wait_ge(s["normed"], 1 + T * i + n + 1)
                        if n >= 2:
                            pe.wait_ge(s["turned_sb"], 1 + T * i + n - 1)
                        if rows == N_META:
                            pe.nop(nofuse=True)
                        last = nc.tensor.transpose(tp[n % 2][0:N_META, 0, 0:rows], probs[0:rows, n % 2, 0:N_META],
                                                   core.ident[0:rows, 0:rows])
                        if keys > N_META:
                            for j in range(2):
                                last = nc.tensor.transpose(tp[n % 2][:, 1 + j, :],
                                                           probs[:, n % 2, N_META + P * j:N_META + P * (j + 1)],
                                                           core.ident[:, :])
                        last.then_inc(s["turned_ps"], 1)

                    def weigh(n):
                        hh, b = tiles[n]
                        lo = hh * HD
                        rows, keys = size(b)
                        pe.wait_ge(s["turned_sb"], 1 + T * i + n + 1)
                        if n == 0:
                            pe.wait_ge(s["stored"], 1 + i)
                        pe.nop(nofuse=True)
                        if b == N_BLOCKS:
                            nc.tensor.matmul(out_meta[lo:lo + HD, 0:N_META], v[0:N_META, V_META, lo:lo + HD],
                                             turned[0:N_META, n % 2, 0, 0:N_META], start=True, stop=True)\
                              .then_inc(s["weighted"], 1)
                            return
                        dst = out[lo:lo + HD, P * b:P * (b + 1)]
                        nc.tensor.matmul(dst, v[0:N_META, V_META, lo:lo + HD], turned[0:N_META, n % 2, 0, :],
                                         start=True, stop=False)
                        for j in range(2):
                            last = nc.tensor.matmul(dst, v[:, WIN_V[b][j], lo:lo + HD], turned[:, n % 2, 1 + j, :],
                                                    start=False, stop=(j == 1))
                        last.then_inc(s["weighted"], 1)

                    pe.wait_ge(s["staged"], 1 + 4 * i + 4)
                    pe.wait_ge(s["biased"], 1 + T * i)
                    score(0)
                    score(1)
                    for n in range(T):
                        turn(n)
                        if n + 2 < T:
                            score(n + 2)
                        weigh(n)

            @block.vector
            def _(dve):
                with dve.Fori(0, N_PAIRS) as i:
                    def add_bias(n):
                        hh, b = tiles[n]
                        rows, keys = size(b)
                        dve.wait_ge(s["scored"], 1 + T * i + n + 1)
                        if n >= 2:
                            dve.wait_ge(s["exped"], 1 + T * i + n - 1)
                        kind = 0 if b == N_BLOCKS else WIN_TYPE[b]
                        nc.vector.scalar_tensor_tensor(
                            out=scores[0:rows, n % 2, 0:keys], in0=sc[n % 2][0:rows, 0:keys], scalar=scale,
                            in1=bias[0:rows, kind, hh, 0:keys], op0=ALU.mult, op1=ALU.add).then_inc(s["biased"], 1)
                        dve.wait_ge(s["biased"], 1 + T * i + n + 1)
                        nc.vector.tensor_reduce(neg_max[0:rows, n:n + 1], scores[0:rows, n % 2, 0:keys], AX.X, ALU.max,
                                                negate=True).then_inc(s["maxed"], 1)

                    def normalise(n):
                        _, b = tiles[n]
                        rows, keys = size(b)
                        dve.wait_ge(s["exped"], 1 + T * i + n + 1)
                        nc.vector.reciprocal(inverse[0:rows, n:n + 1], row_sum[0:rows, n:n + 1]).then_inc(s["inverted"], 1)
                        dve.wait_ge(s["inverted"], 1 + T * i + n + 1)
                        nc.vector.tensor_scalar(probs[0:rows, n % 2, 0:keys], probs[0:rows, n % 2, 0:keys],
                                                inverse[0:rows, n:n + 1], None, ALU.mult).then_inc(s["normed"], 1)

                    dve.wait_ge(s["bias_loaded"], 1 + 16 * i + 16)
                    dve.wait_ge(s["exped"], 1 + T * i)
                    add_bias(0)
                    for n in range(T):
                        if n + 1 < T:
                            add_bias(n + 1)
                        normalise(n)
                    dve.wait_ge(s["weighted"], 1 + T * i + T)
                    pair = mix[:, bass.ds(i, 1), :].rearrange("p a n -> p (a n)")
                    nc.vector.tensor_copy(pair[:, 0:N_META], out_meta[:, 0:N_META])
                    nc.vector.tensor_copy(by_columns(pair[:, N_META:]), out[:, :].rearrange("p (c r) -> p c r", r=GRID_H))\
                      .then_inc(s["stored"], 1)

            @block.scalar
            def _(act):
                with act.Fori(0, N_PAIRS) as i:
                    def exponentiate(n):
                        _, b = tiles[n]
                        rows, keys = size(b)
                        act.wait_ge(s["maxed"], 1 + T * i + n + 1)
                        if n >= 2:
                            act.wait_ge(s["turned_ps"], 1 + T * i + n - 1)
                        nc.scalar.activation(probs[0:rows, n % 2, 0:keys], scores[0:rows, n % 2, 0:keys], ACT.Exp,
                                             bias=neg_max[0:rows, n:n + 1], accum_out=row_sum[0:rows, n:n + 1])\
                          .then_inc(s["exped"], 1)

                    def take(n):
                        _, b = tiles[n]
                        rows, keys = size(b)
                        act.wait_ge(s["turned_ps"], 1 + T * i + n + 1)
                        if n >= 2:
                            act.wait_ge(s["weighted"], 1 + T * i + n - 1)
                        last = nc.scalar.copy(turned[0:N_META, n % 2, 0, 0:rows], tp[n % 2][0:N_META, 0, 0:rows])
                        if keys > N_META:
                            last = nc.scalar.copy(turned[:, n % 2, 1:3, :], tp[n % 2][:, 1:3, :])
                        last.then_inc(s["turned_sb"], 1)

                    act.wait_ge(s["turned_ps"], 1 + T * i)
                    exponentiate(0)
                    for n in range(T):
                        if n + 1 < T:
                            exponentiate(n + 1)
                        take(n)
                        if n == 0:
                            act.wait_ge(s["weighted"], 1 + T * i)



CHUNK = 64
N_CHUNKS = -(-N_TOK // CHUNK)
N_PAD = N_CHUNKS * CHUNK
FULL = N_TOK // CHUNK
N_LEVELS = 5
LOG_DECAY = -float(np.exp(-0.5))
A_, R_, B_, K_ = range(4)


def shift_phase(core, raw, rk, v_pad, low):
    nc = core.nc
    with Phase(core, "shift") as ph:
        mu = ph.sb("mu", [P, N_SHIFT])
        near = ph.sb("near", [P, 2, N_TOK])
        off = ph.sb("off", [P, 2, N_TOK])
        loaded, added, differed, shifted, padded = (ph.sem(n) for n in ("loaded", "added", "differed", "shifted", "padded"))
        with ph.block() as block:
            @block.sync
            def _(sp):
                sp.dma_start(mu[:], core.dram["mu"]).then_inc(loaded, 16)

            @block.gpsimd
            def _(pool):
                nc.gpsimd.memset(v_pad[:, :, N_TOK:], 0.0)
                for j in range(N_SHIFT):
                    if j >= 2:
                        pool.wait_ge(differed, 1 + j - 1)
                    nc.gpsimd.tensor_tensor(near[:, j % 2], raw[:, j, 0:N_TOK], raw[:, j, 2:N_TOK + 2], ALU.add)\
                      .then_inc(added, 1)

            @block.vector
            def _(dve):
                dve.wait_ge(loaded, 1 + 16)
                for j in range(N_SHIFT):
                    dst = rk[:, j] if j < 8 else v_pad[:, j - 8, 0:N_TOK] if j < 12 else low[:, j - 12]
                    dve.wait_ge(added, 1 + j + 1)
                    nc.vector.scalar_tensor_tensor(out=off[:, j % 2], in0=near[:, j % 2], scalar=0.5,
                                                   in1=raw[:, j, 1:N_TOK + 1], op0=ALU.mult, op1=ALU.subtract)\
                      .then_inc(differed, 1)
                    dve.wait_ge(differed, 1 + j + 1)
                    nc.vector.scalar_tensor_tensor(out=dst, in0=off[:, j % 2], scalar=mu[:, j:j + 1],
                                                   in1=raw[:, j, 1:N_TOK + 1], op0=ALU.mult, op1=ALU.add)\
                      .then_inc(shifted, 1)

            @block.scalar
            def _(act):
                act.wait_ge(shifted, 1 + 13)
                nc.scalar.activation(low[0:64, 0], low[0:64, 0], ACT.Tanh)
                act.wait_ge(shifted, 1 + 14)
                nc.scalar.activation(low[:, 1], low[:, 1], ACT.Sigmoid)


def rwkv_prepare_phase(core, rk, v_pad, low, seqs, last_decay, gate, bonus):
    nc = core.nc
    with Phase(core, "prep") as ph:
        up = ph.sb("up", [P, 3, P])
        vec = ph.sb("vec", [P, N_PAIRS, 8])
        restart = ph.sb("restart", [P, N_TOK])
        r, k, v = (ph.sb(n, [P, N_TOK]) for n in "rkv")
        kk, square, norm = (ph.sb(n, [P, N_TOK]) for n in ("kk", "square", "norm"))
        sig, a = (ph.sb(n, [P, 2, N_TOK]) for n in ("sig", "a"))
        before, after = ph.sb("before", [P, 2, N_TOK]), ph.sb("after", [P, 2, N_TOK])
        up_to = ph.sb("up_to", [P, N_TOK])
        exps = ph.sb("exps", [P, 3, N_TOK])
        k_dir = ph.sb("k_dir", [P, 2, N_TOK])
        scaled = ph.sb("scaled", [P, N_TOK])
        banks = [ph.ps(f"banks{u}", [P, 2, 512]) for u in range(4)]
        s = {n: ph.sem(n) for n in (
            "vec_loaded", "up_loaded", "restart_set", "projected", "sigmoided", "squared", "kk_summed", "rooted",
            "bonus_made", "bonus_summed", "logs", "exped", "exps_used", "gated", "turn_done", "chain")}
        halves = [(h, slice(h * HALF, (h + 1) * HALF)) for h in range(2)]

        def two(ap):
            return ap.rearrange("p (h n) -> p h n", h=2)

        with ph.block() as block:
            @block.sync
            def _(sp):
                sp.dma_start(vec[:, :, 0:7], core.dram["rw_vec"]).then_inc(s["vec_loaded"], 16)
                with sp.Fori(0, N_PAIRS) as i:
                    sp.wait_ge(s["projected"], 1 + 5 * i)
                    sp.nop(nofuse=True)
                    sp.dma_start(up[:], core.dram["rw_up"][bass.ds(i, 1)].rearrange("a p j m -> (a p) j m"))\
                      .then_inc(s["up_loaded"], 16)

            @block.tensor
            def _(pe):
                with pe.Fori(0, N_PAIRS) as i:
                    pe.wait_ge(s["up_loaded"], 1 + 16 * i + 16)
                    pe.wait_ge(s["turn_done"], 1 + i)
                    for d in range(2):
                        for j, rows in ((0, slice(0, 64)), (1, slice(64, P))):
                            for h, cols in halves:
                                last = nc.tensor.matmul(banks[2 * d + j][:, h, 0:HALF], up[rows, d, :],
                                                        low[rows, 0, cols], start=True, stop=True)
                            last.then_inc(s["projected"], 1)
                    pe.wait_ge(s["sigmoided"], 1 + 4 * i + 1)
                    for h, cols in halves:
                        last = nc.tensor.matmul(banks[0][:, h, 0:HALF], up[:, 2, :], low[:, 1, cols],
                                                start=True, stop=True)
                    last.then_inc(s["projected"], 1)
                    pe.wait_ge(s["sigmoided"], 1 + 4 * i + 2)
                    pe.wait_ge(s["squared"], 1 + i + 1)
                    for h, cols in halves:
                        last = nc.tensor.matmul(banks[1][:, h, 0:HALF], core.ones_head[:, :], square[:, cols],
                                                start=True, stop=True)
                    last.then_inc(s["kk_summed"], 1)
                    pe.wait_ge(s["sigmoided"], 1 + 4 * i + 3)
                    pe.wait_ge(s["bonus_made"], 1 + i + 1)
                    for h, cols in halves:
                        last = nc.tensor.matmul(banks[2][:, h, 0:HALF], core.ones_head[:, :], scaled[:, cols],
                                                start=True, stop=True)
                    last.then_inc(s["bonus_summed"], 1)

            @block.scalar
            def _(act):
                act.wait_ge(s["vec_loaded"], 1 + 16)
                with act.Fori(0, N_PAIRS) as i:
                    for d in range(2):
                        act.wait_ge(s["projected"], 1 + 5 * i + 2 * d + 1)
                        act.wait_ge(s["turn_done"], 1 + i)
                        nc.scalar.activation(two(sig[:, d]), banks[2 * d][:, :, 0:HALF], ACT.Sigmoid,
                                             bias=vec[:, bass.ds(i, 1), d:d + 1].rearrange("p a b -> p (a b)"))\
                          .then_inc(s["sigmoided"], 1)
                        act.wait_ge(s["projected"], 1 + 5 * i + 2 * d + 2)
                        nc.scalar.activation(two(a[:, d]), banks[2 * d + 1][:, :, 0:HALF], ACT.Sigmoid,
                                             bias=vec[:, bass.ds(i, 1), 2 + d:3 + d].rearrange("p a b -> p (a b)"))\
                          .then_inc(s["sigmoided"], 1)
                    act.wait_ge(s["projected"], 1 + 5 * i + 5)
                    nc.scalar.copy(gate[:, bass.ds(i, 1), :].rearrange("p a (h n) -> p (a h) n", h=2),
                                   banks[0][:, :, 0:HALF]).then_inc(s["gated"], 1)
                    act.wait_ge(s["kk_summed"], 1 + i + 1)
                    nc.scalar.activation(two(norm[:, :]), banks[1][:, :, 0:HALF], ACT.Sqrt).then_inc(s["rooted"], 1)
                    for d in range(2):
                        act.wait_ge(s["logs"], 1 + 2 * i + d + 1)
                        act.wait_ge(s["exps_used"], 1 + 2 * i + d)
                        nc.scalar.activation(exps[:, 0], before[:, d], ACT.Exp)
                        nc.scalar.activation(exps[:, 1], after[:, d], ACT.Exp)
                        nc.scalar.activation(exps[:, 2], after[:, d], ACT.Exp, scale=-1.0)
                        edge = after[:, 0, CHUNK - 1:FULL * CHUNK:CHUNK] if d == 0 else after[:, 1, 0:FULL * CHUNK:CHUNK]
                        rest = after[:, 0, N_TOK - 1:N_TOK] if d == 0 else after[:, 1, FULL * CHUNK:FULL * CHUNK + 1]
                        dst = last_decay[:, d, bass.ds(i, 1), :].rearrange("p a c -> p (a c)")
                        nc.scalar.activation(dst[:, 0:FULL], edge, ACT.Exp)
                        nc.scalar.activation(dst[:, FULL:], rest, ACT.Exp).then_inc(s["exped"], 1)

            @block.gpsimd
            def _(pool):
                nc.gpsimd.memset(restart[:, :], 1.0).then_inc(s["restart_set"], 1)
                pool.wait_ge(s["restart_set"], 1 + 1)
                nc.gpsimd.memset(restart[:, 0:N_TOK:CHUNK], 0.0).then_inc(s["restart_set"], 1)
                nc.gpsimd.memset(seqs[:, :, :, :, N_TOK:], 0.0)

            @block.vector
            def _(dve):
                link = Chain(dve, s["chain"])
                dve.wait_ge(s["vec_loaded"], 1 + 16)
                dve.wait_ge(s["restart_set"], 1 + 2)
                link(nc.vector.tensor_scalar(vec[:, :, 7:8], vec[:, :, 5:6], -1.0, 1.0, ALU.mult, ALU.add))
                with dve.Fori(0, N_PAIRS) as i:
                    link.restart()

                    def col(j):
                        return vec[:, bass.ds(i, 1), j:j + 1].rearrange("p a b -> p (a b)")

                    def flat(ap):
                        return ap.rearrange("p a n -> p (a n)")

                    nc.vector.tensor_copy(r[:, :], flat(rk[:, bass.ds(i, 1), :]))
                    nc.vector.tensor_copy(v[:, :], flat(v_pad[:, bass.ds(i, 1), 0:N_TOK]))
                    link(nc.vector.tensor_copy(k[:, :], flat(rk[:, bass.ds(N_PAIRS + i, 1), :])))
                    link(nc.vector.tensor_scalar(kk[:, :], k[:, :], col(4), None, ALU.mult))
                    nc.vector.tensor_tensor(square[:, :], kk[:, :], kk[:, :], ALU.mult).then_inc(s["squared"], 1)
                    dve.wait_ge(s["rooted"], 1 + i + 1)
                    link(nc.vector.tensor_scalar(norm[:, :], norm[:, :], 1e-12, None, ALU.max))
                    link(nc.vector.reciprocal(norm[:, :], norm[:, :]))
                    link(nc.vector.tensor_tensor(kk[:, :], kk[:, :], norm[:, :], ALU.mult))
                    for d in range(2):
                        dve.wait_ge(s["sigmoided"], 1 + 4 * i + 2 * d + 2)
                        link(nc.vector.tensor_scalar(sig[:, d], sig[:, d], LOG_DECAY, None, ALU.mult))
                        if d == 0:
                            link(nc.vector.tensor_tensor_scan(after[:, 0], restart[:, :], sig[:, 0], 0.0,
                                                              ALU.mult, ALU.add))
                            nc.vector.tensor_tensor(before[:, 0], after[:, 0], sig[:, 0], ALU.subtract)\
                              .then_inc(s["logs"], 1)
                        else:
                            link(nc.vector.tensor_tensor_scan(up_to[:, :], restart[:, :], sig[:, 1], 0.0,
                                                              ALU.mult, ALU.add))
                            full = up_to[:, 0:FULL * CHUNK].rearrange("p (c n) -> p c n", n=CHUNK)
                            nc.vector.tensor_tensor(
                                before[:, 1, 0:FULL * CHUNK].rearrange("p (c n) -> p c n", n=CHUNK),
                                full[:, :, CHUNK - 1:CHUNK].to_broadcast([P, FULL, CHUNK]), full, ALU.subtract)
                            tail = slice(FULL * CHUNK, N_TOK)
                            link(nc.vector.tensor_tensor(
                                before[:, 1, tail], up_to[:, N_TOK - 1:N_TOK].to_broadcast([P, N_TOK - FULL * CHUNK]),
                                up_to[:, tail], ALU.subtract))
                            nc.vector.tensor_tensor(after[:, 1], before[:, 1], sig[:, 1], ALU.add)\
                              .then_inc(s["logs"], 1)
                        link(nc.vector.tensor_scalar(k_dir[:, d], a[:, d], col(5), col(7), ALU.mult, ALU.add))
                        link(nc.vector.tensor_tensor(k_dir[:, d], k_dir[:, d], k[:, :], ALU.mult))
                        link(nc.vector.tensor_tensor(a[:, d], a[:, d], kk[:, :], ALU.mult))
                    link(nc.vector.tensor_tensor(scaled[:, :], k_dir[:, 0], k_dir[:, 1], ALU.add))
                    nc.vector.scalar_tensor_tensor(out=scaled[:, :], in0=scaled[:, :], scalar=col(6), in1=r[:, :],
                                                   op0=ALU.mult, op1=ALU.mult).then_inc(s["bonus_made"], 1)
                    for d in range(2):
                        def seq(which):
                            return seqs[:, d, bass.ds(i, 1), which, 0:N_TOK].rearrange("p a n -> p (a n)")
                        dve.wait_ge(s["exped"], 1 + 2 * i + d + 1)
                        nc.vector.scalar_tensor_tensor(out=seq(A_), in0=kk[:, :], scalar=-1.0, in1=exps[:, 0],
                                                       op0=ALU.mult, op1=ALU.mult)
                        nc.vector.tensor_tensor(seq(R_), r[:, :], exps[:, 1], ALU.mult)
                        nc.vector.tensor_tensor(seq(B_), a[:, d], exps[:, 2], ALU.mult)
                        nc.vector.tensor_tensor(seq(K_), k_dir[:, d], exps[:, 2], ALU.mult)\
                          .then_inc(s["exps_used"], 1)
                    dve.wait_ge(s["bonus_summed"], 1 + i + 1)
                    dve.wait_ge(s["gated"], 1 + i + 1)
                    dve.wait_ge(s["exps_used"], 1 + 2 * i + 2)
                    nc.vector.tensor_tensor(bonus[:, bass.ds(i, 1), :].rearrange("p a (h n) -> p (a h) n", h=2),
                                            banks[2][:, :, 0:HALF], two(v[:, :]), ALU.mult)\
                      .then_inc(s["turn_done"], 1)
                    dve.wait_ge(s["turn_done"], 1 + i + 1)


MADE = ["AB", "AK", "M", "BK_tokens", "V_tokens"] + [f"{n}{l}" for l in range(N_LEVELS) for n in ("FQ", "Q")] \
    + ["X", "SA", "Y", "S"]
VECTOR_TAKES = ["AB", "AK", "M"] + [f"Q{l}" for l in range(N_LEVELS)] + ["S"]
SCALAR_TAKES = ["BK_tokens", "V_tokens"] + [f"FQ{l}" for l in range(N_LEVELS)] + ["X", "SA", "Y"]


def rwkv_chunk_phase(core, seqs, v_pad, last_decay, y):
    nc = core.nc
    with Phase(core, "chunk") as ph:
        stage = ph.sb("stage", [P, 2, N_PAIRS, 5, CHUNK])
        decay = ph.sb("decay", [P, 2, N_PAIRS])
        ab = ph.sb("ab", [P, 2, N_PAIRS, 2, CHUNK])
        ak = ph.sb("ak", [P, 2, N_PAIRS, 2, CHUNK])
        m = ph.sb("m", [P, 2, N_PAIRS, CHUNK])
        m_level = ph.sb("m_level", [P, 2, N_LEVELS, N_PAIRS, CHUNK])
        q = ph.sb("q", [P, 2, 2, N_PAIRS, CHUNK])
        fq = ph.sb("fq", [P, 2, N_PAIRS, CHUNK])
        bk = ph.sb("bk", [P, 2, 2, N_PAIRS, CHUNK])
        vt = ph.sb("vt", [P, 2, N_PAIRS, CHUNK])
        x = ph.sb("x", [P, 2, N_PAIRS, CHUNK])
        sa = ph.sb("sa", [P, 2, N_PAIRS, CHUNK])
        state = ph.sb("state", [P, 2, N_PAIRS, CHUNK])
        order = ph.sb("order", [P, 2, 2, CHUNK])
        order_t = ph.sb("order_t", [P, 2, CHUNK])
        level = ph.sb("level", [P, N_LEVELS + 1, CHUNK])
        eye = ph.sb("eye", [P, CHUNK])
        bank = [[ph.ps(f"bank{d}{j}", [P, 512]) for j in range(4)] for d in range(2)]
        consts_loaded = [ph.sem(f"consts_loaded{j}") for j in range(4)]
        zeroed, staged = ph.sem("zeroed"), ph.sem("staged")
        made = [ph.sem(f"made{d}") for d in range(2)]
        vector_took = [ph.sem(f"vector_took{d}") for d in range(2)]
        scalar_took = [ph.sem(f"scalar_took{d}") for d in range(2)]
        masked = [ph.sem(f"masked{d}") for d in range(2)]
        pool_chain, vector_chain = ph.sem("pool_chain"), ph.sem("vector_chain")
        pairs = range(N_PAIRS)
        heads = [slice(0, 64), slice(64, P)]

        def wait_made(eng, i, d, what):
            eng.wait_ge(made[d], 1 + len(MADE) * i + MADE.index(what) + 1)

        def wait_vector(eng, i, d, what):
            eng.wait_ge(vector_took[d], 1 + len(VECTOR_TAKES) * i + VECTOR_TAKES.index(what) + 1)

        def wait_scalar(eng, i, d, what):
            eng.wait_ge(scalar_took[d], 1 + len(SCALAR_TAKES) * i + SCALAR_TAKES.index(what) + 1)

        def by_pair(b, n):
            return b[:, 0:N_PAIRS * n].rearrange("p (g n) -> p g n", n=n)

        with ph.block() as block:
            @block.sync
            def _(sp):
                for j, (dst, name) in enumerate(((order, "order"), (order_t, "order_t"), (level, "level"), (eye, "eye"))):
                    sp.dma_start(dst[:], core.dram[name]).then_inc(consts_loaded[j], 16)

            @block.gpsimd
            def _(pool):
                for sem in consts_loaded:
                    pool.wait_ge(sem, 1 + 16)
                nc.gpsimd.memset(state[:], 0.0).then_inc(zeroed, 1)
                link = Chain(pool, pool_chain)

                def place(d, i):
                    return i if d == 0 else N_CHUNKS - 1 - i

                def stage_seqs(d, i, first, count):
                    at = place(d, i) * CHUNK
                    for g in range(N_PAIRS):
                        last = nc.gpsimd.tensor_copy(stage[:, d, g, first:first + count],
                                                     seqs[:, d, g, first:first + count, bass.ds(at, CHUNK)])
                    return last

                def stage_one(d, i, which):
                    at = place(d, i) * CHUNK
                    return nc.gpsimd.tensor_copy(stage[:, d, :, which], seqs[:, d, :, which, bass.ds(at, CHUNK)])

                def stage_values(d, i):
                    nc.gpsimd.tensor_copy(stage[:, d, :, 4], v_pad[:, :, bass.ds(place(d, i) * CHUNK, CHUNK)])

                def stage_decay(d, i):
                    return nc.gpsimd.tensor_copy(decay[:, d].unsqueeze(2), last_decay[:, d, :, bass.ds(place(d, i), 1)])

                for d in range(2):
                    stage_seqs(d, 0, 0, 4)
                    stage_values(d, 0)
                    stage_decay(d, 0).then_inc(staged, 1)

                def make_masks(i):
                    pool.nop(nofuse=True)
                    link.restart()
                    for d in range(2):
                        wide = [P, N_PAIRS, CHUNK]
                        wait_vector(pool, i, d, "M")
                        first = level[:, 0:1].to_broadcast(wide)
                        nc.gpsimd.tensor_tensor(q[:, d, 0], ab[:, d, :, 0], first, ALU.mult)
                        link(nc.gpsimd.tensor_tensor(q[:, d, 1], m[:, d], first, ALU.mult))
                        both = q[:, d].rearrange("p a g n -> p (a g) n")
                        nc.gpsimd.tensor_tensor(both, both, eye[:, :].unsqueeze(1).to_broadcast([P, 2 * N_PAIRS, CHUNK]),
                                                ALU.add)
                        for l in range(N_LEVELS):
                            last = nc.gpsimd.tensor_tensor(m_level[:, d, l], m[:, d],
                                                           level[:, l + 1:l + 2].to_broadcast(wide), ALU.mult)
                        last.then_inc(masked[d], 1)

                with pool.Fori(0, N_CHUNKS - 1) as i:
                    make_masks(i)
                    for d in range(2):
                        wait_made(pool, i, d, "V_tokens")
                        pool.nop(nofuse=True)
                        stage_seqs(d, i + 1, B_, 2)
                        stage_values(d, i + 1)
                    for d in range(2):
                        wait_made(pool, i, d, "X")
                        pool.nop(nofuse=True)
                        stage_one(d, i + 1, A_)
                    for d in range(2):
                        wait_made(pool, i, d, "Y")
                        pool.nop(nofuse=True)
                        stage_one(d, i + 1, R_)
                        wait_vector(pool, i, d, "S")
                        pool.nop(nofuse=True)
                        stage_decay(d, i + 1).then_inc(staged, 1)
                make_masks(N_CHUNKS - 1)

            @block.tensor
            def _(pe):
                for sem in consts_loaded:
                    pe.wait_ge(sem, 1 + 16)
                pe.wait_ge(zeroed, 1 + 1)
                with pe.Fori(0, N_CHUNKS) as i:
                    def each(d, dst, n, *products):
                        pe.nop(nofuse=True)
                        for g in pairs:
                            for rows in heads:
                                for j, (lhs, rhs) in enumerate(products):
                                    last = nc.tensor.matmul(dst[rows, g * n:(g + 1) * n], lhs(rows, g), rhs(rows, g),
                                                            start=(j == 0), stop=(j == len(products) - 1))
                        return last

                    def staged_seq(d, first, count=1):
                        return lambda rows, g: stage[rows, d, g, first:first + count].rearrange("p a n -> p (a n)")

                    def plain(t, d):
                        return lambda rows, g: t[rows, d, g]

                    def second(t, d, j):
                        return lambda rows, g: t[rows, d, g, j]

                    def half_of(t, d, j):
                        return lambda rows, g: t[rows, d, j, g]

                    def unit(rows, g):
                        return eye[rows, :]

                    pe.wait_ge(staged, 1 + 2 * i + 2)
                    for d in range(2):
                        pe.wait_ge(scalar_took[d], 1 + len(SCALAR_TAKES) * i)
                        pe.wait_ge(vector_took[d], 1 + len(VECTOR_TAKES) * i)
                        each(d, bank[d][0], 2 * CHUNK, (staged_seq(d, B_), staged_seq(d, A_, 2))).then_inc(made[d], 1)
                        each(d, bank[d][1], 2 * CHUNK, (staged_seq(d, K_), staged_seq(d, A_, 2))).then_inc(made[d], 1)
                        each(d, bank[d][3], CHUNK, (staged_seq(d, A_), staged_seq(d, B_))).then_inc(made[d], 1)
                        each(d, bank[d][2][:, 0:256], CHUNK, (staged_seq(d, B_), unit))
                        each(d, bank[d][2][:, 256:512], CHUNK, (staged_seq(d, K_), unit)).then_inc(made[d], 1)
                    for d in range(2):
                        wait_scalar(pe, i, d, "BK_tokens")
                        each(d, bank[d][2], CHUNK, (staged_seq(d, 4), unit)).then_inc(made[d], 1)
                    for l in range(N_LEVELS):
                        for d in range(2):
                            if l == 0:
                                pe.wait_ge(masked[d], 1 + i + 1)
                            else:
                                wait_vector(pe, i, d, f"Q{l - 1}")
                            each(d, bank[d][0], CHUNK, (half_of(m_level, d, l), half_of(q, d, 0))).then_inc(made[d], 1)
                        for d in range(2):
                            wait_scalar(pe, i, d, f"FQ{l}")
                            last = each(d, bank[d][1], CHUNK, (half_of(q, d, 1), plain(fq, d)))
                            if l < N_LEVELS - 1:
                                last = each(d, bank[d][1][:, 256:512], CHUNK, (plain(fq, d), half_of(q, d, 1)))
                            last.then_inc(made[d], 1)
                    for d in range(2):
                        wait_scalar(pe, i, d, "V_tokens")
                        each(d, bank[d][0], CHUNK, (staged_seq(d, A_), plain(state, d)),
                             (second(ak, d, 0), plain(vt, d))).then_inc(made[d], 1)
                    for d in range(2):
                        wait_scalar(pe, i, d, "X")
                        wait_vector(pe, i, d, f"Q{N_LEVELS - 1}")
                        each(d, bank[d][3], CHUNK, (half_of(q, d, 0), plain(x, d))).then_inc(made[d], 1)
                    for d in range(2):
                        wait_scalar(pe, i, d, "SA")
                        each(d, bank[d][2], CHUNK, (plain(state, d), staged_seq(d, R_)),
                             (plain(sa, d), second(ab, d, 1)), (plain(vt, d), second(ak, d, 1))).then_inc(made[d], 1)
                        each(d, bank[d][1], CHUNK, (half_of(bk, d, 0), plain(sa, d)),
                             (half_of(bk, d, 1), plain(vt, d))).then_inc(made[d], 1)

            @block.vector
            def _(dve):
                for sem in consts_loaded:
                    dve.wait_ge(sem, 1 + 16)
                link = Chain(dve, vector_chain)
                with dve.Fori(0, N_CHUNKS) as i:
                    link.restart()
                    for d in range(2):
                        for j, (what, dst) in enumerate((("AB", ab), ("AK", ak))):
                            wait_made(dve, i, d, what)
                            nc.vector.tensor_tensor(
                                dst[:, d].rearrange("p g a n -> p g (a n)"), by_pair(bank[d][j], 2 * CHUNK),
                                order[:, d].rearrange("p a n -> p (a n)").unsqueeze(1).to_broadcast([P, N_PAIRS, 2 * CHUNK]),
                                ALU.mult).then_inc(vector_took[d], 1)
                        wait_made(dve, i, d, "M")
                        nc.vector.tensor_tensor(m[:, d], by_pair(bank[d][3], CHUNK),
                                                order_t[:, d:d + 1].to_broadcast([P, N_PAIRS, CHUNK]),
                                                ALU.mult).then_inc(vector_took[d], 1)
                    for l in range(N_LEVELS):
                        for d in range(2):
                            wait_made(dve, i, d, f"Q{l}")
                            n = N_PAIRS * CHUNK * (2 if l < N_LEVELS - 1 else 1)
                            both = q[:, d].rearrange("p a g n -> p (a g n)")[:, 0:n]
                            nc.vector.tensor_tensor(both, bank[d][1][:, 0:n], both, ALU.add)\
                              .then_inc(vector_took[d], 1)
                    for d in range(2):
                        wait_made(dve, i, d, "S")
                        link(nc.vector.tensor_tensor(state[:, d], by_pair(bank[d][1], CHUNK), state[:, d], ALU.add))
                        nc.vector.tensor_tensor(state[:, d], state[:, d],
                                                decay[:, d].unsqueeze(2).to_broadcast([P, N_PAIRS, CHUNK]),
                                                ALU.mult).then_inc(vector_took[d], 1)

            @block.scalar
            def _(act):
                with act.Fori(0, N_CHUNKS) as i:
                    def take(d, what, dst, src):
                        wait_made(act, i, d, what)
                        nc.scalar.copy(dst, src).then_inc(scalar_took[d], 1)

                    for d in range(2):
                        take(d, "BK_tokens", bk[:, d].rearrange("p a g n -> p (a g n)"), bank[d][2][:, :])
                    for d in range(2):
                        take(d, "V_tokens", vt[:, d], by_pair(bank[d][2], CHUNK))
                    for l in range(N_LEVELS):
                        for d in range(2):
                            take(d, f"FQ{l}", fq[:, d], by_pair(bank[d][0], CHUNK))
                    for d in range(2):
                        take(d, "X", x[:, d], by_pair(bank[d][0], CHUNK))
                    for d in range(2):
                        take(d, "SA", sa[:, d], by_pair(bank[d][3], CHUNK))
                    for d in range(2):
                        at = i * CHUNK if d == 0 else (N_CHUNKS - 1 - i) * CHUNK
                        take(d, "Y", y[:, d, :, bass.ds(at, CHUNK)], by_pair(bank[d][2], CHUNK))


RWKV_GN_EPS = 64e-5


def rwkv_output_phase(core, y, gate, bonus, mix):
    nc = core.nc
    with Phase(core, "rwout") as ph:
        total, square, rstd = (ph.sb(n, [P, N_TOK]) for n in ("total", "square", "rstd"))
        ln = ph.sb("ln", [P, N_PAIRS, 2])
        eps = ph.sb("eps", [P, 1])
        mean, var = ph.ps("mean", [P, 2, 512]), ph.ps("var", [P, 2, 512])
        loaded, chain, ready, averaged, squared, varied, rooted = (
            ph.sem(n) for n in ("loaded", "chain", "ready", "averaged", "squared", "varied", "rooted"))
        eps_set = ph.sem("eps_set")
        halves = [(h, slice(h * HALF, (h + 1) * HALF)) for h in range(2)]

        def two(ap):
            return ap.rearrange("p (h n) -> p h n", h=2)

        with ph.block() as block:
            @block.sync
            def _(sp):
                sp.dma_start(ln[:], core.dram["rw_ln"]).then_inc(loaded, 16)

            @block.tensor
            def _(pe):
                with pe.Fori(0, N_PAIRS) as i:
                    for done, src, dst, said in ((ready, total, mean, averaged), (squared, square, var, varied)):
                        pe.wait_ge(done, 1 + i + 1)
                        for h, cols in halves:
                            last = nc.tensor.matmul(dst[:, h, 0:HALF], core.ones_head[:, :], src[:, cols],
                                                    start=True, stop=True)
                        last.then_inc(said, 1)

            @block.scalar
            def _(act):
                act.wait_ge(eps_set, 1 + 1)
                with act.Fori(0, N_PAIRS) as i:
                    act.wait_ge(varied, 1 + i + 1)
                    nc.scalar.activation(two(rstd[:, :]), var[:, :, 0:HALF], ACT.Sqrt, bias=eps[:, 0:1],
                                         scale=1.0 / HD).then_inc(rooted, 1)

            @block.vector
            def _(dve):
                nc.vector.memset(eps[:, :], RWKV_GN_EPS).then_inc(eps_set, 1)
                dve.wait_ge(loaded, 1 + 16)
                link = Chain(dve, chain)
                with dve.Fori(0, N_PAIRS) as i:
                    link.restart()

                    def of(t, first=0):
                        return t[:, bass.ds(first + i, 1), 0:N_TOK].rearrange("p a n -> p (a n)")

                    def col(j):
                        return ln[:, bass.ds(i, 1), j:j + 1].rearrange("p a b -> p (a b)")

                    nc.vector.tensor_tensor(total[:, :], of(y[:, 0]), of(y[:, 1]), ALU.add).then_inc(ready, 1)
                    dve.wait_ge(averaged, 1 + i + 1)
                    link(nc.vector.scalar_tensor_tensor(out=two(total[:, :]), in0=mean[:, :, 0:HALF], scalar=-1.0 / HD,
                                                        in1=two(total[:, :]), op0=ALU.mult, op1=ALU.add))
                    nc.vector.tensor_tensor(square[:, :], total[:, :], total[:, :], ALU.mult).then_inc(squared, 1)
                    dve.wait_ge(rooted, 1 + i + 1)
                    link(nc.vector.reciprocal(rstd[:, :], rstd[:, :]))
                    link(nc.vector.scalar_tensor_tensor(out=total[:, :], in0=total[:, :], scalar=col(0), in1=rstd[:, :],
                                                        op0=ALU.mult, op1=ALU.mult))
                    link(nc.vector.scalar_tensor_tensor(out=total[:, :], in0=total[:, :], scalar=col(1), in1=of(bonus),
                                                        op0=ALU.add, op1=ALU.add))
                    link(nc.vector.tensor_tensor(of(mix, N_PAIRS), total[:, :], of(gate), ALU.mult))


def rwkv(core, raw, raw_free, mix):
    nc = core.nc
    with ExitStack() as stack:
        def sb(name, shape):
            return stack.enter_context(nc.sbuf_tensor(name, shape, F32))

        v_pad = sb("v_pad", [P, N_PAIRS, N_PAD])
        last_decay = sb("last_decay", [P, 2, N_PAIRS, N_CHUNKS])
        gate, bonus = sb("gate", [P, N_PAIRS, N_TOK]), sb("bonus", [P, N_PAIRS, N_TOK])
        with ExitStack() as early:
            rk = early.enter_context(nc.sbuf_tensor("rk", [P, 2 * N_PAIRS, N_TOK], F32))
            low = early.enter_context(nc.sbuf_tensor("low", [P, 2, N_TOK], F32))
            shift_phase(core, raw, rk, v_pad, low)
            raw_free()
            seqs = stack.enter_context(nc.sbuf_tensor("seqs", [P, 2, N_PAIRS, 4, N_PAD], F32, side="right"))
            rwkv_prepare_phase(core, rk, v_pad, low, seqs, last_decay, gate, bonus)
        y = sb("y", [P, 2, N_PAIRS, N_PAD])
        rwkv_chunk_phase(core, seqs, v_pad, last_decay, y)
        rwkv_output_phase(core, y, gate, bonus, mix)


def chunk_masks():
    i, t = np.meshgrid(np.arange(CHUNK), np.arange(CHUNK), indexing="ij")
    order = np.stack([np.stack([i < t, i <= t]), np.stack([i > t, i >= t])]).astype(np.float32)
    order_t = np.stack([t < i, t > i]).astype(np.float32)
    level = np.stack([(i // (2 * b) == t // (2 * b)) & (i // b != t // b) for b in (1, 2, 4, 8, 16, 32)])
    both = lambda a: np.ascontiguousarray(np.concatenate([a, a], axis=0))
    return {"order": both(order.transpose(2, 0, 1, 3)), "order_t": both(order_t.transpose(1, 0, 2)),
            "level": both(level.astype(np.float32).transpose(1, 0, 2)), "eye": both(np.eye(CHUNK, dtype=np.float32))}



N_GROUPS = 4
PER_GROUP = 8
N_EXPERTS = N_GROUPS * PER_GROUP
D_FF = D // 2
FF_TILES = D_FF // P
N_TILES = -(-N_TOK // P)
TAIL = N_TOK - (N_TILES - 1) * P
CAP = 64
MAX_ROUNDS = -(-N_TOK // CAP)
TURNS = N_EXPERTS // 2
FAR = -1e30


def moe(core, layer, hn):
    fetched = [[core.nc.alloc_semaphore(f"moe{layer}_fetched{c}{g}") for g in range(2)] for c in range(2)]
    x_fetched = core.nc.alloc_semaphore(f"moe{layer}_x_fetched")
    with Phase(core, f"moe{layer}") as ph:
        rank = ph.sb("rank", [P, N_TILES, N_EXPERTS])
        gates = ph.sb("gates", [P, 2, N_TILES])
        places = ph.sb("places", [P, 2, 2, N_TILES])
        rounds = ph.sb("rounds", [1, 1], I32)
        ring = ph.sb("ring", [P, 2, 3, FF_TILES * D])
        loaded = [[ph.sem(f"w{j}_loaded{u}") for j in range(3)] for u in range(2)]
        weights = [core.dram["moe_w1"][layer], core.dram["moe_w3"][layer], core.dram["moe_w2"][layer]]

        def load(sp, expert, u, j):
            src = weights[j][bass.ds(expert, 1)]
            src = src.rearrange("a (p s) n -> (a p) (s n)", p=P) if j < 2 else \
                src.rearrange("a (j p) n -> (a p) j n", p=P)
            dst = ring[:, u, j] if j < 2 else ring[:, u, j].rearrange("p (j n) -> p j n", j=FF_TILES)
            sp.dma_start(dst, src).then_inc(loaded[u][j], 16)

        ph.prime()
        route_phase(core, layer, hn, rank, gates, places, rounds, load)
        expert_phase(core, layer, rank, gates, places, rounds, ring, load, loaded, x_fetched, fetched)


def route_phase(core, layer, hn, rank, gates, places, rounds, load):
    nc, dram = core.nc, core.dram
    with Phase(core, f"route{layer}") as ph:
        n_logits = N_GROUPS + N_EXPERTS
        by_token = ph.sb("by_token", [P, N_TILES, SLOTS, P])
        w = ph.sb("w", [P, SLOTS, n_logits])
        b = ph.sb("b", [P, n_logits])
        consts = ph.sb("consts", [P, 8 + N_EXPERTS + MAX_ROUNDS + N_TILES])
        order = ph.sb("order", [P, P])
        logits = ph.sb("logits", [P, N_TILES, n_logits])
        group = ph.sb("group", [P, N_TILES, N_GROUPS])
        chosen = ph.sb("chosen", [P, 2, N_TILES, PER_GROUP])
        of_group = ph.sb("of_group", [P, N_TILES, PER_GROUP, N_GROUPS])
        local = ph.sb("local", [P, N_TILES, PER_GROUP])
        score = ph.sb("score", [P, N_TILES, PER_GROUP])
        shifted = ph.sb("shifted", [P, N_TILES, N_GROUPS])
        best = ph.sb("best", [P, 6, N_TILES])
        assigned = ph.sb("assigned", [P, 3, N_TILES, N_EXPERTS])
        picked = ph.sb("picked", [P, N_TILES, N_EXPERTS])
        fullest = ph.sb("fullest", [P, 1])
        needed = ph.sb("needed", [P, MAX_ROUNDS])
        n_rounds = ph.sb("n_rounds", [P, 1])
        ps_logits = ph.ps("ps_logits", [P, 512])
        ps_rank = ph.ps("ps_rank", [P, 512])
        ps_count = ph.ps("ps_count", [P, 512])
        ps_tok = [ph.ps(f"ps_tok{u}", [P, 4, P]) for u in range(2)]
        loaded = [ph.sem(f"loaded{j}") for j in range(4)]
        rows_stored = [ph.sem(f"rows_stored{j}") for j in range(2)]
        names = ("logits_made", "exp_in", "exp_out", "assigned", "ranked", "turned", "taken", "chain")
        s = {n: ph.sem(n) for n in names}
        first8 = consts[:, 0:8]
        expert_base = consts[:, 8:8 + N_EXPERTS]
        thresholds = consts[:, 8 + N_EXPERTS:8 + N_EXPERTS + MAX_ROUNDS]
        valid = consts[:, 8 + N_EXPERTS + MAX_ROUNDS:]
        sizes = [P] * (N_TILES - 1) + [TAIL]
        parts = [(t, g) for t in range(N_TILES) for g in range(SLOTS // 4)]

        def view(t, n):
            return t[:, 0:N_TILES * n].rearrange("p (t n) -> p t n", n=n)

        with ph.block() as block:
            @block.sync
            def _(sp):
                for j, (dst, name) in enumerate(((w, f"route_w{layer}"), (b, f"route_b{layer}"),
                                                 (consts, "route_consts"), (order, "token_order"))):
                    sp.dma_start(dst[:], dram[name]).then_inc(loaded[j], 16)
                for u, j in LOAD_ORDER:
                    load(sp, u, u, j)
                sp.wait_ge(s["taken"], 1 + len(parts))
                full = N_TILES - 1
                sp.dma_start(core.hn_rows[0:full * P].rearrange("(t p) n -> p t n", p=P),
                             by_token[:, 0:full].rearrange("p t k n -> p t (k n)")).then_inc(rows_stored[0], 16)
                sp.dma_start(core.hn_rows[full * P:], by_token[0:TAIL, full].rearrange("p k n -> p (k n)"))\
                  .then_inc(rows_stored[1], 16)
                for sem in rows_stored:
                    sp.wait_ge(sem, 1 + 16)

            @block.tensor
            def _(pe):
                for sem in loaded:
                    pe.wait_ge(sem, 1 + 16)
                for t, n in enumerate(sizes):
                    for k in range(SLOTS):
                        last = nc.tensor.matmul(ps_logits[0:n, t * n_logits:(t + 1) * n_logits],
                                                hn[:, k, P * t:P * t + n], w[:, k], start=(k == 0), stop=(k == SLOTS - 1))
                last.then_inc(s["logits_made"], 1)
                for j, (t, g) in enumerate(parts):
                    if j >= 2:
                        pe.wait_ge(s["taken"], 1 + j - 1)
                    for k in range(4):
                        last = nc.tensor.transpose(ps_tok[j % 2][0:sizes[t], k, :],
                                                   hn[:, 4 * g + k, P * t:P * t + sizes[t]], core.ident[:, :])
                    last.then_inc(s["turned"], 1)
                pe.wait_ge(s["assigned"], 1 + 1)
                both = assigned[:, 2]
                for t in range(N_TILES):
                    dst = ps_rank[:, t * N_EXPERTS:(t + 1) * N_EXPERTS]
                    for before in range(t):
                        nc.tensor.matmul(dst, core.ones[:, :], both[:, before], start=(before == 0), stop=False)
                    nc.tensor.matmul(dst, order[:, :], both[:, t], start=(t == 0), stop=True)
                for t in range(N_TILES):
                    last = nc.tensor.matmul(ps_count[:, 0:N_EXPERTS], core.ones[:, :], both[:, t],
                                            start=(t == 0), stop=(t == N_TILES - 1))
                last.then_inc(s["ranked"], 1)

            @block.scalar
            def _(act):
                act.wait_ge(s["exp_in"], 1 + 1)
                nc.scalar.activation(shifted[:], shifted[:], ACT.Exp).then_inc(s["exp_out"], 1)
                for j, (t, g) in enumerate(parts):
                    act.wait_ge(s["turned"], 1 + j + 1)
                    nc.scalar.copy(by_token[0:sizes[t], t, 4 * g:4 * g + 4, :], ps_tok[j % 2][0:sizes[t]])\
                      .then_inc(s["taken"], 1)
                act.wait_ge(s["exp_in"], 1 + 2)
                nc.scalar.activation(best[:, 3], best[:, 3], ACT.Exp).then_inc(s["exp_out"], 1)

            @block.vector
            def _(dve):
                link = Chain(dve, s["chain"])
                v = nc.vector
                for sem in loaded:
                    dve.wait_ge(sem, 1 + 16)
                link(v.memset(logits[:], 0.0))
                dve.wait_ge(s["logits_made"], 1 + 1)
                full = N_TILES - 1
                v.tensor_tensor(logits[:, 0:full], ps_logits[:, 0:full * n_logits].rearrange("p (t n) -> p t n", n=n_logits),
                                b[:, :].unsqueeze(1).to_broadcast([P, full, n_logits]), ALU.add)
                link(v.tensor_tensor(logits[0:TAIL, full], ps_logits[0:TAIL, full * n_logits:(full + 1) * n_logits],
                                     b[0:TAIL, :], ALU.add))
                g_logits = logits[:, :, 0:N_GROUPS]
                e_logits = logits[:, :, N_GROUPS:].rearrange("p t (g e) -> p t e g", g=N_GROUPS)

                def one_hot(out, values, top, n):
                    wide = [P, N_TILES, n]
                    link(v.tensor_tensor(score[:, :, 0:n], values, top.to_broadcast(wide), ALU.is_equal))
                    link(v.tensor_tensor(score[:, :, 0:n], score[:, :, 0:n],
                                         first8[:, 0:n].unsqueeze(1).to_broadcast(wide), ALU.mult))
                    link(v.tensor_reduce(best[:, 5], score[:, :, 0:n], AX.X, ALU.max))
                    link(v.tensor_tensor(out, score[:, :, 0:n], best[:, 5].unsqueeze(2).to_broadcast(wide), ALU.is_equal))

                link(v.tensor_reduce(best[:, 0], g_logits, AX.X, ALU.max))
                v.tensor_tensor(shifted[:], g_logits, best[:, 0].unsqueeze(2).to_broadcast([P, N_TILES, N_GROUPS]),
                                ALU.subtract).then_inc(s["exp_in"], 1)
                one_hot(group[:], g_logits, best[:, 0].unsqueeze(2), N_GROUPS)
                link(v.tensor_tensor(group[:], group[:], valid.unsqueeze(2).to_broadcast([P, N_TILES, N_GROUPS]), ALU.mult))
                link(v.tensor_tensor(of_group[:], e_logits,
                                     group[:].unsqueeze(2).to_broadcast([P, N_TILES, PER_GROUP, N_GROUPS]), ALU.mult))
                link(v.tensor_reduce(local[:], of_group[:], AX.X, ALU.add))
                link(v.tensor_reduce(best[:, 1], local[:], AX.X, ALU.max))
                one_hot(chosen[:, 0], local[:], best[:, 1].unsqueeze(2), PER_GROUP)
                link(v.scalar_tensor_tensor(out=local[:], in0=chosen[:, 0], scalar=FAR, in1=local[:],
                                            op0=ALU.mult, op1=ALU.add))
                link(v.tensor_reduce(best[:, 2], local[:], AX.X, ALU.max))
                one_hot(chosen[:, 1], local[:], best[:, 2].unsqueeze(2), PER_GROUP)
                v.tensor_tensor(best[:, 3], best[:, 2], best[:, 1], ALU.subtract).then_inc(s["exp_in"], 1)
                for c in range(2):
                    for g in range(N_GROUPS):
                        link(v.tensor_tensor(assigned[:, c, :, PER_GROUP * g:PER_GROUP * (g + 1)], chosen[:, c],
                                             group[:, :, g:g + 1].to_broadcast([P, N_TILES, PER_GROUP]), ALU.mult))
                v.tensor_tensor(assigned[:, 2], assigned[:, 0], assigned[:, 1], ALU.add).then_inc(s["assigned"], 1)
                dve.wait_ge(s["exp_out"], 1 + 2)
                link(v.tensor_reduce(best[:, 4], shifted[:], AX.X, ALU.add))
                link(v.tensor_scalar(best[:, 5], best[:, 3], 1.0, None, ALU.add))
                link(v.tensor_tensor(best[:, 4], best[:, 4], best[:, 5], ALU.mult))
                link(v.reciprocal(gates[:, 0], best[:, 4]))
                link(v.tensor_tensor(gates[:, 1], gates[:, 0], best[:, 3], ALU.mult))
                dve.wait_ge(s["ranked"], 1 + 1)
                dve.wait_ge(s["assigned"], 1 + 1)
                link(v.scalar_tensor_tensor(out=rank[:], in0=view(ps_rank, N_EXPERTS), scalar=1.0, in1=assigned[:, 2],
                                            op0=ALU.add, op1=ALU.mult))
                link(v.tensor_scalar(rank[:], rank[:], -1.0, None, ALU.add))
                for c in range(2):
                    link(v.tensor_tensor(picked[:], assigned[:, c],
                                         expert_base.unsqueeze(1).to_broadcast([P, N_TILES, N_EXPERTS]), ALU.mult))
                    link(v.tensor_reduce(places[:, 0, c], picked[:], AX.X, ALU.add))
                    link(v.tensor_tensor(picked[:], rank[:], assigned[:, c], ALU.mult))
                    link(v.tensor_reduce(places[:, 1, c], picked[:], AX.X, ALU.add))
                link(v.tensor_reduce(fullest[:, :], ps_count[:, 0:N_EXPERTS], AX.X, ALU.max))
                link(v.tensor_scalar(needed[:, :], thresholds, fullest[:, 0:1], None, ALU.is_lt))
                link(v.tensor_reduce(n_rounds[:, :], needed[:, :], AX.X, ALU.add))
                link(v.tensor_copy(rounds[0:1, 0:1], n_rounds[0:1, 0:1]))


LOAD_ORDER = [(0, 0), (0, 1), (1, 0), (1, 1), (0, 2), (1, 2)]


def expert_phase(core, layer, rank, gates, places, rounds, ring, load, loaded, x_fetched, fetched):
    nc, dram = core.nc, core.dram
    blocks = TURNS + 1
    with Phase(core, f"exp{layer}") as ph:
        here = ph.sb("here", [P, CAP])
        numbers = ph.sb("numbers", [P, N_TILES])
        pick = ph.sb("pick", [P, N_TILES, 2, CAP])
        index = ph.sb("index", [2 * CAP, blocks], U32)
        index_now = ph.sb("index_now", [2 * CAP, 1], U32)
        x_rows = ph.sb("x_rows", [2 * CAP, D])
        x = ph.sb("x", [P, SLOTS, 2 * CAP])
        hidden = ph.sb("hidden", [CAP, 2, D_FF])
        hidden_t = ph.sb("hidden_t", [P, 2, FF_TILES, CAP])
        y_rows = ph.sb("y_rows", [CAP, 2, D])
        ps_x, ps_1, ps_3, ps_y = ([ph.ps(f"{n}{u}", [P, 512]) for u in range(2)] for n in ("ps_x", "ps_1", "ps_3", "ps_y"))
        ps_index = ps_3[0]
        ps_mix = ps_1 + ps_3
        stored = [ph.sem(f"stored{u}") for u in range(2)]
        used = [[ph.sem(f"w{j}_used{u}") for j in range(3)] for u in range(2)]
        here_loaded, numbers_loaded = ph.sem("here_loaded"), ph.sem("numbers_loaded")
        inside, row_sums, round_gates = (ph.sb(n, [P, 2, N_TILES]) for n in ("inside", "row_sums", "round_gates"))
        rows = ph.sb("rows", [P, 2, N_TILES], U32)
        got = ph.sb("got", [P, 2, 2, D])
        mixed = ph.sb("mixed", [P, 2, SLOTS, P])
        sizes = [P] * (N_TILES - 1) + [TAIL]
        shares = [-(-N_TILES // 2), N_TILES // 2]
        s = {n: ph.sem(n) for n in ("picked", "index_summed", "index_made", "index_staged", "last_set", "x_turned",
                                    "x_taken", "silued0", "silued1", "hidden_made0", "hidden_made1",
                                    "hidden_turned0", "hidden_turned1", "hidden_taken0", "hidden_taken1",
                                    "y_taken0", "y_taken1", "moved_on", "rows_made", "chain",
                                    "mixed", "mix_turned", "added")}
        scratch = core.scratch
        last_tile = N_TILES - 1

        def n_rounds(eng):
            return eng.value_load(rounds[0:1, 0:1], min_val=1, max_val=MAX_ROUNDS)

        with ph.block() as block:
            @block.sync
            def _(sp):
                sp.dma_start(here[:], dram["places"]).then_inc(here_loaded, 16)
                sp.dma_start(numbers[:], dram["token_numbers"]).then_inc(numbers_loaded, 16)
                with sp.Fori(0, n_rounds(sp)) as r:
                    with sp.Fori(0, TURNS) as i:
                        n = TURNS * r + i
                        with sp.If(n > 0):
                            for u, j in LOAD_ORDER:
                                sp.wait_ge(used[u][j], 1 + n)
                                sp.nop(nofuse=True)
                                load(sp, 2 * i + u, u, j)

            @block.vector
            def _(dve):
                link = Chain(dve, s["chain"])
                v = nc.vector
                dve.wait_ge(here_loaded, 1 + 16)
                v.memset(index[:, TURNS:], 0).then_inc(s["last_set"], 1)
                with dve.Fori(0, n_rounds(dve)) as r:
                    with dve.Fori(0, TURNS) as i:
                        n = TURNS * r + i
                        dve.wait_ge(s["index_summed"], 1 + n)
                        for h in range(2):
                            last = v.tensor_tensor(
                                pick[:, :, h], rank[:, :, bass.ds(2 * i + h, 1)].to_broadcast([P, N_TILES, CAP]),
                                here[:, :].unsqueeze(1).to_broadcast([P, N_TILES, CAP]), ALU.is_equal)
                        last.then_inc(s["picked"], 1)
                        dve.wait_ge(s["index_summed"], 1 + n + 1)
                        v.tensor_copy(index[:, bass.ds(i, 1)], ps_index[0:2 * CAP, 0:1]).then_inc(s["index_made"], 1)

                    def take_x(count):
                        dve.wait_ge(s["x_turned"], 1 + count)
                        for h in range(2):
                            last = v.tensor_copy(x[:, 4 * h:4 * h + 4, :].rearrange("p k n -> p (k n)"),
                                                 ps_x[h][:, 0:8 * CAP])
                        last.then_inc(s["x_taken"], 1)

                    def make_hidden(u, n):
                        dve.wait_ge(used[u][1], 1 + n)
                        dve.wait_ge(s[f"silued{u}"], 1 + n)
                        v.tensor_tensor(hidden[:, u], ps_3[u][0:CAP, :], hidden[:, u], ALU.mult)\
                         .then_inc(s[f"hidden_made{u}"], 1)

                    def take_hidden(u, n):
                        dve.wait_ge(s[f"hidden_turned{u}"], 1 + n)
                        v.tensor_copy(hidden_t[:, u].rearrange("p f n -> p (f n)"), ps_1[u][:, 0:FF_TILES * CAP])\
                         .then_inc(s[f"hidden_taken{u}"], 1)

                    def take_y(u, n):
                        dve.wait_ge(used[u][2], 1 + n)
                        dve.wait_ge(stored[u], 1 + 16 * (n - 1))
                        for h in range(2):
                            last = v.tensor_copy(y_rows[:, u, 512 * h:512 * (h + 1)], ps_y[h][0:CAP, :])
                        last.then_inc(s[f"y_taken{u}"], 1)

                    take_x(blocks * r + 1)
                    with dve.Fori(0, TURNS) as i:
                        n = TURNS * r + i + 1
                        make_hidden(0, n)
                        take_hidden(0, n)
                        make_hidden(1, n)
                        take_y(0, n)
                        take_hidden(1, n)
                        take_x(blocks * r + i + 2)
                        take_y(1, n)
                    dve.wait_ge(s["picked"], 1 + TURNS * r + TURNS)
                    v.tensor_scalar(here[:, :], here[:, :], float(CAP), None, ALU.add).then_inc(s["moved_on"], 1)
                    dve.wait_ge(s["moved_on"], 1 + r + 1)
                    dve.nop(nofuse=True)
                    link.restart()
                    left = places[:, 1]
                    link(v.tensor_scalar(inside[:], left, 0.0, None, ALU.is_ge))
                    link(v.scalar_tensor_tensor(out=inside[:], in0=left, scalar=float(CAP), in1=inside[:],
                                                op0=ALU.is_lt, op1=ALU.mult))
                    link(v.tensor_tensor(row_sums[:], places[:, 0], left, ALU.add))
                    link(v.tensor_tensor(row_sums[:], row_sums[:], inside[:], ALU.mult))
                    link(v.tensor_copy(rows[:], row_sums[:]))
                    link(v.tensor_scalar(left, left, -float(CAP), None, ALU.add))
                    v.tensor_tensor(round_gates[:], gates[:], inside[:], ALU.mult).then_inc(s["rows_made"], 1)
                    dve.wait_ge(s["rows_made"], 1 + r + 1)
                    for t, n in enumerate(sizes):
                        g = t % 2
                        for c in range(2):
                            dve.wait_ge(fetched[c][g], 16 * (shares[g] * r + t // 2 + 1))
                        if t >= 2:
                            dve.wait_ge(s["mix_turned"], 1 + N_TILES * r + t - 1)
                        link(v.tensor_scalar(got[0:n, g, 0], got[0:n, g, 0], round_gates[0:n, 0, t:t + 1], None, ALU.mult))
                        v.scalar_tensor_tensor(
                            out=mixed[0:n, g].rearrange("n s p -> n p s"),
                            in0=got[0:n, g, 1].rearrange("n (p s) -> n p s", s=SLOTS), scalar=round_gates[0:n, 1, t:t + 1],
                            in1=got[0:n, g, 0].rearrange("n (p s) -> n p s", s=SLOTS), op0=ALU.mult, op1=ALU.add)\
                         .then_inc(s["mixed"], 1)
                        dve.wait_ge(s["mix_turned"], 1 + N_TILES * r + t + 1)
                        for h in range(2):
                            dst = core.hT[:, 4 * h:4 * h + 4, P * t:P * t + n]
                            last = v.tensor_tensor(dst, ps_mix[2 * g + h][:, 0:4 * P].rearrange(
                                "p (k n) -> p k n", k=4)[:, :, 0:n], dst, ALU.add)
                        last.then_inc(s["added"], 1)

            @block.gpsimd
            def _(pool):
                pool.wait_ge(s["last_set"], 1 + 1)
                with pool.Fori(0, n_rounds(pool)) as r:
                    with pool.Fori(0, blocks - 1) as j:
                        pool.wait_ge(s["index_made"], 1 + TURNS * r + j + 1)
                        pool.wait_ge(s["x_turned"], 1 + blocks * r + j)
                        pool.nop(nofuse=True)
                        nc.gpsimd.tensor_copy(index_now[:, :], index[:, bass.ds(j, 1)]).then_inc(s["index_staged"], 1)
                        pool.wait_ge(s["index_staged"], 1 + blocks * r + j + 1)
                        pool.nop(nofuse=True)
                        nc.gpsimd.indirect_dma_start(x_rows[:, :], None, core.hn_rows,
                                                     bass.IndirectOffsetOnAxis(ap=index_now[:, 0:1], axis=0))\
                          .then_inc(x_fetched, 16)
                    pool.wait_ge(s["x_turned"], 1 + blocks * r + blocks - 1)
                    pool.nop(nofuse=True)
                    nc.gpsimd.tensor_copy(index_now[:, :], index[:, TURNS:]).then_inc(s["index_staged"], 1)
                    pool.wait_ge(s["index_staged"], 1 + blocks * r + blocks)
                    pool.nop(nofuse=True)
                    nc.gpsimd.indirect_dma_start(x_rows[:, :], None, core.hn_rows,
                                                 bass.IndirectOffsetOnAxis(ap=index_now[:, 0:1], axis=0))\
                      .then_inc(x_fetched, 16)
                    for u in range(2):
                        pool.wait_ge(stored[u], 1 + 16 * (TURNS * r + TURNS))
                    pool.wait_ge(s["rows_made"], 1 + r + 1)
                    for t, n in enumerate(sizes):
                        if t >= 2:
                            pool.wait_ge(s["mixed"], 1 + N_TILES * r + t - 1)
                        else:
                            pool.wait_ge(s["mixed"], 1 + N_TILES * r)
                        pool.nop(nofuse=True)
                        for c in range(2):
                            nc.gpsimd.indirect_dma_start(
                                got[0:n, t % 2, c], None, scratch,
                                bass.IndirectOffsetOnAxis(ap=rows[0:n, c, t:t + 1], axis=0))\
                              .then_inc(fetched[c][t % 2], 16)

            @block.scalar
            def _(act):
                with act.Fori(0, n_rounds(act)) as r:
                    act.wait_ge(s["mixed"], 1 + N_TILES * r)
                    act.nop(nofuse=True)
                    with act.Fori(0, TURNS) as i:
                        n = TURNS * r + i + 1
                        for u in range(2):
                            act.wait_ge(used[u][0], 1 + n)
                            act.wait_ge(s[f"hidden_turned{u}"], 1 + n - 1)
                            act.nop(nofuse=True)
                            nc.scalar.activation(hidden[:, u], ps_1[u][0:CAP, :], ACT.Silu).then_inc(s[f"silued{u}"], 1)
                        for u in range(2):
                            act.wait_ge(s[f"y_taken{u}"], 1 + n)
                            act.nop(nofuse=True)
                            act.dma_start(scratch[bass.ds((2 * i + u) * CAP, CAP), :], y_rows[:, u])\
                               .then_inc(stored[u], 16)
                    for u in range(2):
                        act.wait_ge(stored[u], 1 + 16 * (TURNS * r + TURNS))

            @block.tensor
            def _(pe):
                pe.wait_ge(numbers_loaded, 1 + 16)
                with pe.Fori(0, n_rounds(pe)) as r:
                    pe.wait_ge(s["added"], 1 + N_TILES * r)
                    pe.nop(nofuse=True)
                    with pe.Fori(0, TURNS) as i:
                        n = TURNS * r + i
                        pe.wait_ge(s["picked"], 1 + n + 1)
                        pe.wait_ge(s["index_made"], 1 + n)
                        pe.nop(nofuse=True)
                        for t in range(N_TILES):
                            rows_t = TAIL if t == last_tile else P
                            last = nc.tensor.matmul(ps_index[0:2 * CAP, 0:1], pick[0:rows_t, t].rearrange("p h n -> p (h n)"),
                                                    numbers[0:rows_t, t:t + 1], start=(t == 0), stop=(t == last_tile))
                        last.then_inc(s["index_summed"], 1)

                    def turn_x(count):
                        pe.wait_ge(x_fetched, 16 * count)
                        pe.wait_ge(s["x_taken"], 1 + count - 1)
                        pe.nop(nofuse=True)
                        for k in range(SLOTS):
                            last = nc.tensor.transpose(ps_x[k // 4][:, 2 * CAP * (k % 4):2 * CAP * (k % 4 + 1)],
                                                       x_rows[:, P * k:P * (k + 1)], core.ident[0:2 * CAP, 0:2 * CAP])
                        last.then_inc(s["x_turned"], 1)

                    def up(u, j, n):
                        w = ring[:, u, j].rearrange("p (s n) -> p s n", s=SLOTS)
                        dst = (ps_1, ps_3)[j][u]
                        pe.wait_ge(loaded[u][j], 1 + 16 * n)
                        pe.wait_ge(s[f"hidden_taken{u}"] if j == 0 else s[f"hidden_made{u}"], 1 + n - 1)
                        pe.nop(nofuse=True)
                        for k in range(SLOTS):
                            last = nc.tensor.matmul(dst[0:CAP, :], x[:, k, CAP * u:CAP * (u + 1)], w[:, k],
                                                    start=(k == 0), stop=(k == SLOTS - 1))
                        last.then_inc(used[u][j], 1)

                    def turn_hidden(u, n):
                        pe.wait_ge(s[f"hidden_made{u}"], 1 + n)
                        pe.nop(nofuse=True)
                        for f in range(FF_TILES):
                            last = nc.tensor.transpose(ps_1[u][:, CAP * f:CAP * (f + 1)], hidden[:, u, P * f:P * (f + 1)],
                                                       core.ident[0:CAP, 0:CAP])
                        last.then_inc(s[f"hidden_turned{u}"], 1)

                    def down(u, n):
                        w = ring[:, u, 2].rearrange("p (j n) -> p j n", j=FF_TILES)
                        pe.wait_ge(loaded[u][2], 1 + 16 * n)
                        pe.wait_ge(s[f"hidden_taken{u}"], 1 + n)
                        pe.wait_ge(s["y_taken0"] if u else s["y_taken1"], 1 + (n if u else n - 1))
                        pe.nop(nofuse=True)
                        for h in range(2):
                            for f in range(FF_TILES):
                                last = nc.tensor.matmul(ps_y[h][0:CAP, :], hidden_t[:, u, f], w[:, f, 512 * h:512 * (h + 1)],
                                                        start=(f == 0), stop=(f == FF_TILES - 1))
                        last.then_inc(used[u][2], 1)

                    turn_x(blocks * r + 1)
                    with pe.Fori(0, TURNS) as i:
                        n = TURNS * r + i + 1
                        pe.wait_ge(s["x_taken"], 1 + blocks * r + i + 1)
                        pe.nop(nofuse=True)
                        up(0, 0, n)
                        up(0, 1, n)
                        up(1, 0, n)
                        turn_hidden(0, n)
                        up(1, 1, n)
                        down(0, n)
                        turn_hidden(1, n)
                        turn_x(blocks * r + i + 2)
                        down(1, n)
                    for t, n in enumerate(sizes):
                        g = t % 2
                        pe.wait_ge(s["mixed"], 1 + N_TILES * r + t + 1)
                        if t >= 2:
                            pe.wait_ge(s["added"], 1 + N_TILES * r + t - 1)
                        pe.nop(nofuse=True)
                        for k in range(SLOTS):
                            last = nc.tensor.transpose(ps_mix[2 * g + k // 4][:, P * (k % 4):P * (k % 4) + n],
                                                       mixed[0:n, g, k], core.ident[0:n, 0:n])
                        last.then_inc(s["mix_turned"], 1)



def output_projection_phase(core, mix):
    nc = core.nc

    def outcome(ph, acc, multiplied, drained):
        def takers(block):
            @block.vector
            def _(dve):
                with dve.Fori(0, SLOTS // 2) as i:
                    for u in range(2):
                        dve.wait_ge(multiplied[u], 1 + i + 1)
                        h = core.hT[:, bass.ds(2 * i + u, 1), :].rearrange("p a (h n) -> p (a h) n", h=2)
                        nc.vector.tensor_tensor(h, acc[u][:, :, 0:HALF], h, ALU.add).then_inc(drained[u], 1)
        return takers

    dense_phase(core, "out", core.dram["w_out"], SLOTS // 2, mix, outcome)



S5_STEPS = 8
S5_CHUNKS = N_TOK // S5_STEPS
S5_CH = 16
S5_GROUPS = D // S5_CH
S5_GP = S5_GROUPS // 2
S5_P = 64
LOW, HIGH = 7, 8


def s5(core, hn):
    nc = core.nc
    with ExitStack() as stack:
        def sb(name, shape):
            return stack.enter_context(nc.sbuf_tensor(f"s5_{name}", shape, F32))

        rows = sb("rows", [S5_CHUNKS, S5_GROUPS * P])
        tables = sb("tables", [P, 3, 2, S5_GROUPS, 2, S5_STEPS])
        a8 = sb("a8", [P, 3, 2, S5_GP])
        b, c = sb("b", [P, 2, S5_GROUPS, S5_CH]), sb("c", [P, 2, S5_GROUPS, 2, S5_CH])
        s5_tables_phase(core, tables, a8, b, c)
        with ExitStack() as right:
            state = right.enter_context(nc.sbuf_tensor("s5_state", [P, 2, 2, S5_GP, S5_CHUNKS + 1], F32, side="right"))
            with nc.sbuf_tensor("s5_u", [P, S5_GROUPS, S5_CHUNKS], F32) as u:
                s5_inputs_phase(core, hn, rows, u)
                s5_local_phase(core, u, tables, b, c, rows, state)
            s5_scan_phase(core, state, a8)
            swapped = sb("swapped", [P, 2, 2, S5_GP, S5_CHUNKS + 1])
            s5_swap_phase(core, state, swapped)
        s5_entering_phase(core, swapped, tables, c, rows)
        s5_outputs_phase(core, rows, hn)


def s5_tables_phase(core, tables, a8, b, c):
    nc, dram = core.nc, core.dram
    n = 2 * S5_GROUPS
    with Phase(core, "s5t") as ph:
        lam = ph.sb("lam", [P, 3, n])
        names = ("step", "growth", "shrink", "sin", "cos", "angle", "t0", "t1", "den", "am1", "rest", "turns",
                 "sr", "cr", "m", "sm", "cm")
        t = {k: ph.sb(k, [P, n]) for k in names}
        z = ph.sb("z", [P, 2, n])
        powers = ph.sb("powers", [P, 2, LOW + 1 + HIGH, n])
        zp = ph.sb("zp", [P, 2, S5_STEPS, n])
        tmp = ph.sb("tmp", [P, 2, S5_STEPS, n])
        sign = ph.sb("sign", [P, 1])
        loaded = [ph.sem(f"loaded{i}") for i in range(3)]
        bits = ph.sb("bits", [P, n], I32)
        chain, made = ph.sem("chain"), ph.sem("made")
        magic = 1.5 * 2.0 ** 23

        with ph.block() as block:
            @block.sync
            def _(sp):
                for i, (dst, name) in enumerate(((lam, "s5_lam"), (b, "s5_b"), (c, "s5_c"))):
                    sp.dma_start(dst[:], dram[name]).then_inc(loaded[i], 16)
                for s in loaded:
                    sp.wait_ge(s, 1 + 16)

            @block.vector
            def _(dve):
                link = Chain(dve, chain)
                v = nc.vector
                re, im = lam[:, 0], lam[:, 1]
                link(v.memset(sign[:, :], 1.0))
                link(v.memset(sign[S5_P:, :], -1.0))
                dve.wait_ge(loaded[0], 1 + 16)
                x, r, k = (t[name][:, :] for name in ("t0", "rest", "turns"))

                def reduce(value, unit):
                    hi = float(np.float32(round(unit * 2048) / 2048))
                    link(v.tensor_scalar(k, value, 1 / unit, magic, ALU.mult, ALU.add))
                    link(v.tensor_scalar(k, k, -magic, None, ALU.add))
                    link(v.scalar_tensor_tensor(out=r, in0=k, scalar=-hi, in1=value, op0=ALU.mult, op1=ALU.add))
                    link(v.scalar_tensor_tensor(out=r, in0=k, scalar=-(unit - hi), in1=r, op0=ALU.mult, op1=ALU.add))

                def series(out, y, coefficients):
                    link(v.tensor_scalar(out, y, coefficients[-1], None, ALU.mult))
                    for coefficient in coefficients[-2:0:-1]:
                        link(v.scalar_tensor_tensor(out=out, in0=out, scalar=coefficient, in1=y, op0=ALU.add, op1=ALU.mult))
                    link(v.tensor_scalar(out, out, coefficients[0], None, ALU.add))

                def exp(out, value):
                    reduce(value, np.log(2.0))
                    link(v.tensor_scalar(k, k, -126.0, 127.0, ALU.max, ALU.min))
                    link(v.tensor_scalar(k, k, 127.0, 2.0 ** 23, ALU.add, ALU.mult))
                    link(v.tensor_copy(bits[:, :], k))
                    series(out, r, [1 / math.factorial(j) for j in range(8)])
                    link(v.tensor_tensor(out, out, bits[:, :].bitcast(F32), ALU.mult))

                exp(t["step"][:, :], lam[:, 2])
                link(v.tensor_tensor(t["t0"][:, :], re, t["step"][:, :], ALU.mult))
                link(v.tensor_tensor(t["angle"][:, :], im, t["step"][:, :], ALU.mult))
                exp(t["growth"][:, :], x)
                link(v.reciprocal(t["shrink"][:, :], t["growth"][:, :]))
                reduce(t["angle"][:, :], np.pi / 2)
                square, sr, cr, m, sm, cm = (t[name][:, :] for name in ("t1", "sr", "cr", "m", "sm", "cm"))
                link(v.tensor_tensor(square, r, r, ALU.mult))
                series(sr, square, [(-1) ** j / math.factorial(2 * j + 1) for j in range(5)])
                link(v.tensor_tensor(sr, sr, r, ALU.mult))
                series(cr, square, [(-1) ** j / math.factorial(2 * j) for j in range(6)])
                link(v.tensor_scalar(m, k, 0.25, magic, ALU.mult, ALU.add))
                link(v.tensor_scalar(m, m, -magic, None, ALU.add))
                link(v.scalar_tensor_tensor(out=m, in0=m, scalar=-4.0, in1=k, op0=ALU.mult, op1=ALU.add))
                link(v.scalar_tensor_tensor(out=cm, in0=m, scalar=-1.0, in1=m, op0=ALU.mult, op1=ALU.max))
                link(v.tensor_scalar(sm, cm, -1.0, 2.0, ALU.mult, ALU.add))
                link(v.tensor_tensor(sm, sm, m, ALU.mult))
                link(v.tensor_scalar(cm, cm, -1.0, 1.0, ALU.mult, ALU.add))
                for out, y0, y1, op in (("sin", cr, sr, ALU.add), ("cos", sr, cr, ALU.subtract)):
                    link(v.tensor_tensor(t["t1"][:, :], sm, y0, ALU.mult))
                    link(v.tensor_tensor(t[out][:, :], cm, y1, ALU.mult))
                    link(v.tensor_tensor(t[out][:, :], t[out][:, :], t["t1"][:, :], op))
                one, minus_one = powers[:, :, LOW + 1], powers[:, :, LOW - 1]
                link(v.memset(powers[:, 0, LOW], 1.0))
                link(v.memset(powers[:, 1, LOW], 0.0))
                link(v.tensor_tensor(one[:, 0], t["growth"][:, :], t["cos"][:, :], ALU.mult))
                link(v.tensor_tensor(one[:, 1], t["growth"][:, :], t["sin"][:, :], ALU.mult))
                link(v.tensor_tensor(minus_one[:, 0], t["shrink"][:, :], t["cos"][:, :], ALU.mult))
                link(v.scalar_tensor_tensor(out=minus_one[:, 1], in0=t["shrink"][:, :], scalar=-1.0, in1=t["sin"][:, :],
                                            op0=ALU.mult, op1=ALU.mult))
                link(v.tensor_tensor(t["den"][:, :], re, re, ALU.mult))
                link(v.tensor_tensor(t["t1"][:, :], im, im, ALU.mult))
                link(v.tensor_tensor(t["den"][:, :], t["den"][:, :], t["t1"][:, :], ALU.add))
                link(v.reciprocal(t["den"][:, :], t["den"][:, :]))
                link(v.tensor_scalar(t["am1"][:, :], one[:, 0], -1.0, None, ALU.add))
                for part, x, y, op in ((0, t["am1"][:, :], one[:, 1], ALU.add), (1, one[:, 1], t["am1"][:, :], ALU.subtract)):
                    link(v.tensor_tensor(z[:, part], x, re, ALU.mult))
                    link(v.tensor_tensor(t["t1"][:, :], y, im, ALU.mult))
                    link(v.tensor_tensor(z[:, part], z[:, part], t["t1"][:, :], op))
                    link(v.tensor_tensor(z[:, part], z[:, part], t["den"][:, :], ALU.mult))

                def times(out, x, y, count):
                    def wide(part):
                        return y[:, part].unsqueeze(1).to_broadcast([P, count, n])
                    for part, (i, j, op) in enumerate(((0, 1, ALU.subtract), (1, 0, ALU.add))):
                        v.tensor_tensor(tmp[:, 0, 0:count], x[:, 0], wide(i), ALU.mult)
                        link(v.tensor_tensor(tmp[:, 1, 0:count], x[:, 1], wide(j), ALU.mult))
                        link(v.tensor_tensor(out[:, part], tmp[:, 0, 0:count], tmp[:, 1, 0:count], op))

                def run(lo, hi):
                    return powers[:, :, LOW + lo:LOW + hi + 1]

                for k in (1, 2, 4):
                    times(run(k + 1, 2 * k), run(1, k), powers[:, :, LOW + k], k)
                for k in (1, 2):
                    times(run(-2 * k, -k - 1), run(-k, -1), powers[:, :, LOW - k], k)
                times(run(-7, -5), run(-3, -1), powers[:, :, LOW - 4], 3)
                times(zp[:, :], run(0, 7), z, S5_STEPS)
                for g2 in range(2):
                    half = slice(g2 * S5_P, (g2 + 1) * S5_P)
                    for part in range(2):
                        src = powers[half, part, LOW + 8].rearrange("p (d gp g) -> p d gp g", d=2, g=2)[:, :, :, g2]
                        link(v.tensor_copy(a8[half, part], src))
                        if part:
                            link(v.tensor_scalar(a8[half, 2], src, -1.0, None, ALU.mult))
                v.nop(nofuse=True).then_inc(made, 1)

            def spread(eng, copy_to):
                def factors(slot, part, k_of, source, signed):
                    for d in range(2):
                        for s in range(S5_STEPS):
                            copy_to(tables[:, slot, part, :, d, s],
                                    source[:, part, k_of(d, s)].rearrange("p (d g) -> p d g", d=2)[:, d], signed)
                return factors

            @block.scalar
            def _(act):
                act.wait_ge(made, 1 + 1)
                factors = spread(act, lambda dst, src, signed: nc.scalar.activation(
                    dst, src, ACT.Copy, scale=sign[:, 0:1]) if signed else nc.scalar.copy(dst, src))
                factors(0, 0, lambda d, s: s if d else 7 - s, zp, False)
                factors(1, 0, lambda d, s: LOW - s if d else s, powers, True)
                factors(2, 0, lambda d, s: LOW + 8 - s if d else LOW + 1 + s, powers, True)

            @block.gpsimd
            def _(pool):
                pool.wait_ge(made, 1 + 1)
                factors = spread(pool, lambda dst, src, signed: nc.gpsimd.tensor_scalar(
                    dst, src, sign[:, 0:1], None, ALU.mult) if signed else nc.gpsimd.tensor_copy(dst, src))
                factors(0, 1, lambda d, s: s if d else 7 - s, zp, True)
                factors(1, 1, lambda d, s: LOW - s if d else s, powers, False)
                factors(2, 1, lambda d, s: LOW + 8 - s if d else LOW + 1 + s, powers, False)


def s5_inputs_phase(core, hn, rows, u):
    nc = core.nc
    with Phase(core, "s5i") as ph:
        acc = [ph.ps(f"acc{j}", [P, 4, P]) for j in range(4)]
        turned, taken = ph.sem("turned"), [ph.sem(f"taken{j}") for j in range(2)]
        first = [(k, h) for k in range(SLOTS) for h in range(2)]
        second = range(S5_GROUPS // 4)
        n = len(first) + len(second)
        by_group = rows[:, :].rearrange("m (g t q k) -> m g t q k", g=S5_GROUPS, t=S5_STEPS, q=2)

        def take(eng, copy, mine):
            for j in range(mine, n, 2):
                eng.wait_ge(turned, 1 + j + 1)
                if j < len(first):
                    k, h = first[j]
                    for t in range(4):
                        last = copy(by_group[:, :, 4 * h + t, :, k],
                                    acc[j % 4][0:S5_CHUNKS, t, :].rearrange("m (g q) -> m g q", q=2))
                else:
                    g = 4 * (j - len(first))
                    last = copy(u[:, g:g + 4, :], acc[j % 4][:, :, 0:S5_CHUNKS])
                last.then_inc(taken[mine], 1)

        with ph.block() as block:
            @block.tensor
            def _(pe):
                for j in range(n):
                    if j == len(first):
                        for e in range(2):
                            pe.wait_ge(taken[e], 1 + len(first) // 2)
                    elif j >= 4:
                        pe.wait_ge(taken[j % 2], 1 + j // 2 - 1)
                    pe.nop(nofuse=True)
                    for t in range(4):
                        if j < len(first):
                            k, h = first[j]
                            last = nc.tensor.transpose(acc[j % 4][0:S5_CHUNKS, t, :], hn[:, k, 4 * h + t::S5_STEPS],
                                                       core.ident[:, :])
                        else:
                            g = 4 * (j - len(first)) + t
                            last = nc.tensor.transpose(acc[j % 4][:, t, 0:S5_CHUNKS], rows[:, g * P:(g + 1) * P],
                                                       core.ident[0:S5_CHUNKS, 0:S5_CHUNKS])
                    last.then_inc(turned, 1)

            @block.scalar
            def _(act):
                take(act, nc.scalar.copy, 0)

            @block.vector
            def _(dve):
                take(dve, nc.vector.tensor_copy, 1)


def output_rows(rows, g):
    view = rows[:, :].rearrange("m (k t p) -> m t p k", k=SLOTS, t=S5_STEPS)
    return view[:, :, bass.ds(2 * g, 2), :]


def group_rows(acc, g2):
    return acc[0:S5_CHUNKS, g2, :].rearrange("m (t q k) -> m t q k", t=S5_STEPS, q=2)


def factored(v, out, tmp, one, two, x1, x2):
    yield v.tensor_tensor(out, one, x1, ALU.mult)
    yield v.tensor_tensor(tmp, two, x2, ALU.mult)
    yield v.tensor_tensor(out, out, tmp, ALU.subtract)


def state_factor(tables, slot, c, n):
    shape = [P, 4, S5_STEPS, S5_CH]

    def tab(part):
        view = tables[:, slot, part, bass.ds(2 * n, 2)].rearrange("p g d t -> p (g d) t")
        return view.unsqueeze(3).to_broadcast(shape)

    def weight(part):
        return c[:, part, bass.ds(2 * n, 2)].rearrange("p g d i -> p (g d) i").unsqueeze(2).to_broadcast(shape)

    return tab(0), tab(1), weight(0), weight(1)


def s5_local_phase(core, u, tables, b, c, rows, state):
    nc = core.nc
    with Phase(core, "s5l") as ph:
        g_mat = [ph.sb(f"g_mat{x}", [P, 4, P]) for x in range(2)]
        f_mat = [ph.sb(f"f_mat{x}", [P, 4, P]) for x in range(2)]
        g_tmp, f_tmp = ph.sb("g_tmp", [P, 4, P]), ph.sb("f_tmp", [P, 4, P])
        g_turned = [ph.sb(f"g_turned{x}", [P, 4, P]) for x in range(2)]
        own = [ph.sb(f"own{x}", [P, 4, P]) for x in range(2)]
        inputs = [ph.sb(f"inputs{x}", [P, 2, S5_CHUNKS]) for x in range(2)]
        masks = ph.sb("masks", [P, 2 * P])
        ps_g, ps_own, ps_add, ps_y = ([ph.ps(f"{k}{x}", [P, 4, P]) for x in range(2)] for k in ("psg", "psown", "psadd", "psy"))
        names = ("masks_loaded", "g_ready", "f_ready", "g_transposed", "g_copied", "own_summed", "own_masked",
                 "inputs_ready", "added", "added_taken", "y_made", "y_taken", "g_chain", "f_chain", "edges")
        s = {k: ph.sem(k) for k in names}
        with ph.block() as block:
            @block.sync
            def _(sp):
                sp.dma_start(masks[:], core.dram["s5_masks"]).then_inc(s["masks_loaded"], 16)

            @block.gpsimd
            def _(pool):
                nc.gpsimd.memset(state[:, :, 0, :, 0:1], 0.0).then_inc(s["edges"], 1)
                nc.gpsimd.memset(state[:, :, 1, :, S5_CHUNKS:], 0.0).then_inc(s["edges"], 1)
                pool.wait_ge(s["edges"], 1 + 2)
                link = Chain(pool, s["f_chain"])
                with pool.Fori(0, S5_GP // 2) as i:
                    pool.nop(nofuse=True)
                    link.restart()
                    for x in range(2):
                        n = 2 * i + x
                        pool.wait_ge(s["own_summed"], 1 + (n - 1 if x else n))
                        pool.nop(nofuse=True)
                        one, two, x1, x2 = state_factor(tables, 1, c, n)
                        f4 = f_mat[x][:].rearrange("p a (t i) -> p a t i", i=S5_CH)
                        t4 = f_tmp[:].rearrange("p a (t i) -> p a t i", i=S5_CH)
                        link(nc.gpsimd.tensor_tensor(f4, one, x1, ALU.mult))
                        link(nc.gpsimd.tensor_tensor(t4, two, x2, ALU.mult))
                        link(nc.gpsimd.tensor_tensor(f4, f4, t4, ALU.subtract))
                        nc.gpsimd.nop(nofuse=True).then_inc(s["f_ready"], 1)

            @block.vector
            def _(dve):
                dve.wait_ge(s["masks_loaded"], 1 + 16)
                link = Chain(dve, s["g_chain"])
                with dve.Fori(0, S5_GP // 2) as i:
                    dve.nop(nofuse=True)
                    link.restart()
                    for x in range(2):
                        n = 2 * i + x
                        dve.wait_ge(s["own_summed"], 1 + (n - 1 if x else n))
                        shape = [P, 2, 16, S5_CH]

                        def tab(part):
                            return tables[:, 0, part, bass.ds(2 * n, 2)].rearrange("p g d t -> p g (d t)")\
                                .unsqueeze(3).to_broadcast(shape)

                        def weight(part):
                            return b[:, part, bass.ds(2 * n, 2)].unsqueeze(2).to_broadcast(shape)

                        g4 = g_mat[x][:].rearrange("p (g d) (t i) -> p g (d t) i", g=2, i=S5_CH)
                        t4 = g_tmp[:].rearrange("p (g d) (t i) -> p g (d t) i", g=2, i=S5_CH)
                        link(nc.vector.tensor_tensor(g4, tab(0), weight(0), ALU.mult))
                        link(nc.vector.tensor_tensor(t4, tab(1), weight(1), ALU.mult))
                        link(nc.vector.tensor_tensor(g4, g4, t4, ALU.subtract))
                        nc.vector.nop(nofuse=True).then_inc(s["g_ready"], 1)
                    for x in range(2):
                        n = 2 * i + x
                        dve.wait_ge(s["own_summed"], 1 + n + 1)
                        dve.wait_ge(s["y_made"], 1 + (n - 1 if x else n))
                        nc.vector.tensor_tensor(own[x][:].rearrange("p (g d) n -> p g (d n)", g=2),
                                                ps_own[x][:].rearrange("p (g d) n -> p g (d n)", g=2),
                                                masks[:, :].unsqueeze(1).to_broadcast([P, 2, 2 * P]), ALU.mult)\
                          .then_inc(s["own_masked"], 1)

            @block.scalar
            def _(act):
                with act.Fori(0, S5_GP // 2) as i:
                    for x in range(2):
                        n = 2 * i + x
                        act.wait_ge(s["y_made"], 1 + (n - 1 if x else n))
                        nc.scalar.copy(inputs[x][:], u[:, bass.ds(2 * n, 2), :]).then_inc(s["inputs_ready"], 1)
                        act.wait_ge(s["g_transposed"], 1 + n + 1)
                        act.wait_ge(s["added"], 1 + (n - 1 if x else n))
                        nc.scalar.copy(g_turned[x][:], ps_g[x][:]).then_inc(s["g_copied"], 1)
                    for x in range(2):
                        n = 2 * i + x
                        act.wait_ge(s["added"], 1 + n + 1)
                        for d in range(2):
                            last = nc.scalar.copy(
                                state[:, :, d, bass.ds(n, 1), 1 - d:1 - d + S5_CHUNKS].rearrange("p r a m -> p (r a) m"),
                                ps_add[x][:].rearrange("p (r d) n -> p r d n", r=2)[:, :, d, 0:S5_CHUNKS])
                        last.then_inc(s["added_taken"], 1)
                        act.wait_ge(s["y_made"], 1 + n + 1)
                        for g2 in range(2):
                            last = nc.scalar.copy(output_rows(rows, 2 * n + g2), group_rows(ps_y[x], g2))
                        last.then_inc(s["y_taken"], 1)

            @block.tensor
            def _(pe):
                with pe.Fori(0, S5_GP // 2) as i:
                    for x in range(2):
                        n = 2 * i + x
                        pe.wait_ge(s["g_ready"], 1 + n + 1)
                        pe.wait_ge(s["g_copied"], 1 + (n - 1 if x else n))
                        for a in range(4):
                            last = nc.tensor.transpose(ps_g[x][:, a, :], g_mat[x][:, a, :], core.ident[:, :])
                        last.then_inc(s["g_transposed"], 1)
                        pe.wait_ge(s["f_ready"], 1 + n + 1)
                        pe.wait_ge(s["own_masked"], 1 + (n - 1 if x else n))
                        for a in range(4):
                            last = nc.tensor.matmul(ps_own[x][:, a, :], g_mat[x][:, a, :], f_mat[x][:, a, :],
                                                    start=True, stop=True)
                        last.then_inc(s["own_summed"], 1)
                    for x in range(2):
                        n = 2 * i + x
                        pe.wait_ge(s["g_copied"], 1 + n + 1)
                        pe.wait_ge(s["inputs_ready"], 1 + n + 1)
                        pe.wait_ge(s["added_taken"], 1 + (n - 1 if x else n))
                        pe.nop(nofuse=True)
                        for g2 in range(2):
                            for d in range(2):
                                for r in range(2):
                                    last = nc.tensor.matmul(
                                        ps_add[x][S5_P * g2:S5_P * (g2 + 1), 2 * r + d, 0:S5_CHUNKS],
                                        g_turned[x][:, 2 * g2 + d, S5_P * r:S5_P * (r + 1)], inputs[x][:, g2, :],
                                        start=True, stop=True)
                        last.then_inc(s["added"], 1)
                        pe.wait_ge(s["own_masked"], 1 + n + 1)
                        pe.wait_ge(s["y_taken"], 1 + (n - 1 if x else n))
                        pe.nop(nofuse=True)
                        for g2 in range(2):
                            for d in range(2):
                                last = nc.tensor.matmul(ps_y[x][0:S5_CHUNKS, g2, :], inputs[x][:, g2, :],
                                                        own[x][:, 2 * g2 + d, :], start=(d == 0), stop=(d == 1))
                        last.then_inc(s["y_made"], 1)


def s5_scan_phase(core, state, a8):
    nc = core.nc
    with Phase(core, "s5s") as ph:
        matrix = ph.sb("matrix", [P, 2, 2, 2, S5_GP])
        products = [ph.sb(f"products{d}", [P, 2, 2, S5_GP]) for d in range(2)]
        ready, multiplied, summed, stepped = ([ph.sem(f"{k}{d}") for d in range(2)]
                                              for k in ("ready", "multiplied", "summed", "stepped"))

        def scan(eng, ops, d):
            for out, part, which in ((0, 0, 0), (0, 1, 2), (1, 0, 1), (1, 1, 0)):
                last = ops.tensor_copy(matrix[:, d, out, part], a8[:, which, d])
            last.then_inc(ready[d], 1)
            eng.wait_ge(ready[d], 1 + 1)
            with eng.Fori(0, S5_CHUNKS) as m:

                def at(place):
                    return state[:, :, d, :, bass.ds(place, 1)].rearrange("p r g a -> p r (g a)")

                before, now = (m, m + 1) if d == 0 else (S5_CHUNKS - m, S5_CHUNKS - 1 - m)
                eng.wait_ge(stepped[d], 1 + m)
                eng.nop(nofuse=True)
                ops.tensor_tensor(products[d][:], at(before).unsqueeze(1).to_broadcast([P, 2, 2, S5_GP]), matrix[:, d],
                                  ALU.mult).then_inc(multiplied[d], 1)
                eng.wait_ge(multiplied[d], 1 + m + 1)
                eng.nop(nofuse=True)
                ops.tensor_tensor(products[d][:, :, 0], products[d][:, :, 0], products[d][:, :, 1], ALU.add)\
                   .then_inc(summed[d], 1)
                eng.wait_ge(summed[d], 1 + m + 1)
                eng.nop(nofuse=True)
                ops.tensor_tensor(at(now), at(now), products[d][:, :, 0], ALU.add).then_inc(stepped[d], 1)

        with ph.block() as block:
            @block.vector
            def _(dve):
                scan(dve, nc.vector, 0)

            @block.gpsimd
            def _(pool):
                scan(pool, nc.gpsimd, 1)


def s5_swap_phase(core, state, swapped):
    nc = core.nc
    with Phase(core, "s5w") as ph:
        moved = ph.sem("moved")
        with ph.block() as block:
            @block.sync
            def _(sp):
                for g2 in range(2):
                    for r in range(2):
                        sp.dma_start(swapped[S5_P * r:S5_P * (r + 1), g2], state[S5_P * g2:S5_P * (g2 + 1), r])\
                          .then_inc(moved, 16)
                sp.wait_ge(moved, 1 + 4 * 16)


def s5_entering_phase(core, swapped, tables, c, rows):
    nc = core.nc
    with Phase(core, "s5e") as ph:
        f_mat = [ph.sb(f"f_mat{x}", [P, 4, P]) for x in range(2)]
        f_tmp = [ph.sb(f"f_tmp{x}", [P, 4, P]) for x in range(2)]
        entering = [ph.sb(f"entering{x}", [P, 2, 2, S5_CHUNKS]) for x in range(2)]
        ps_y = [ph.ps(f"psy{x}", [P, 4, P]) for x in range(2)]
        f_ready = [ph.sem(f"f_ready{x}") for x in range(2)]
        chain = [ph.sem(f"chain{x}") for x in range(2)]
        s = {k: ph.sem(k) for k in ("entering_ready", "y_made", "y_added")}

        def make_f(eng, ops, link, x, i):
            one, two, x1, x2 = state_factor(tables, 2, c, 2 * i + x)
            f4 = f_mat[x][:].rearrange("p a (t i) -> p a t i", i=S5_CH)
            t4 = f_tmp[x][:].rearrange("p a (t i) -> p a t i", i=S5_CH)
            link(ops.tensor_tensor(f4, one, x1, ALU.mult))
            link(ops.tensor_tensor(t4, two, x2, ALU.mult))
            ops.tensor_tensor(f4, f4, t4, ALU.subtract).then_inc(f_ready[x], 1)

        with ph.block() as block:
            @block.gpsimd
            def _(pool):
                link = Chain(pool, chain[1])
                with pool.Fori(0, S5_GP // 2) as i:
                    pool.wait_ge(s["y_made"], 1 + 2 * i)
                    pool.nop(nofuse=True)
                    link.restart()
                    make_f(pool, nc.gpsimd, link, 1, i)

            @block.vector
            def _(dve):
                link = Chain(dve, chain[0])
                with dve.Fori(0, S5_GP // 2) as i:
                    dve.nop(nofuse=True)
                    link.restart()
                    make_f(dve, nc.vector, link, 0, i)
                    for x in range(2):
                        n = 2 * i + x
                        dve.wait_ge(s["y_made"], 1 + n + 1)
                        for g2 in range(2):
                            dst = output_rows(rows, 2 * n + g2)
                            last = nc.vector.tensor_tensor(dst, group_rows(ps_y[x], g2), dst, ALU.add)
                        last.then_inc(s["y_added"], 1)

            @block.scalar
            def _(act):
                with act.Fori(0, S5_GP // 2) as i:
                    for x in range(2):
                        n = 2 * i + x
                        act.wait_ge(s["y_made"], 1 + (n - 1 if x else n))
                        for d in range(2):
                            last = nc.scalar.copy(
                                entering[x][:, :, d, :],
                                swapped[:, :, d, bass.ds(n, 1), d:d + S5_CHUNKS].rearrange("p g a m -> p (g a) m"))
                        last.then_inc(s["entering_ready"], 1)

            @block.tensor
            def _(pe):
                with pe.Fori(0, S5_GP // 2) as i:
                    for x in range(2):
                        n = 2 * i + x
                        pe.wait_ge(f_ready[x], 1 + i + 1)
                        pe.wait_ge(s["entering_ready"], 1 + n + 1)
                        pe.wait_ge(s["y_added"], 1 + (n - 1 if x else n))
                        pe.nop(nofuse=True)
                        for g2 in range(2):
                            for d in range(2):
                                last = nc.tensor.matmul(ps_y[x][0:S5_CHUNKS, g2, :], entering[x][:, g2, d, :],
                                                        f_mat[x][:, 2 * g2 + d, :], start=(d == 0), stop=(d == 1))
                        last.then_inc(s["y_made"], 1)


def s5_outputs_phase(core, rows, hn):
    nc = core.nc
    with Phase(core, "s5o") as ph:
        d_gain = ph.sb("d_gain", [P, SLOTS])
        acc = [ph.ps(f"acc{j}", [P, 4, P]) for j in range(4)]
        loaded, turned, added, slot_done = (ph.sem(k) for k in ("loaded", "turned", "added", "slot_done"))
        tiles = [(k, h) for k in range(SLOTS) for h in range(2)]
        with ph.block() as block:
            @block.sync
            def _(sp):
                sp.dma_start(d_gain[:], core.dram["s5_d"]).then_inc(loaded, 16)

            @block.tensor
            def _(pe):
                for j, (k, h) in enumerate(tiles):
                    if j >= 4:
                        pe.wait_ge(added, 1 + j - 3)
                    for t in range(4):
                        at = (k * S5_STEPS + 4 * h + t) * P
                        last = nc.tensor.transpose(acc[j % 4][:, t, 0:S5_CHUNKS], rows[:, at:at + P],
                                                   core.ident[0:S5_CHUNKS, 0:S5_CHUNKS])
                    last.then_inc(turned, 1)

            @block.vector
            def _(dve):
                dve.wait_ge(loaded, 1 + 16)
                for j, (k, h) in enumerate(tiles):
                    dve.wait_ge(turned, 1 + j + 1)
                    x = hn[:, k, :].rearrange("p (m t) -> p t m", t=S5_STEPS)[:, 4 * h:4 * h + 4]
                    nc.vector.scalar_tensor_tensor(out=x, in0=x, scalar=d_gain[:, k:k + 1],
                                                   in1=acc[j % 4][:, :, 0:S5_CHUNKS], op0=ALU.mult, op1=ALU.add)\
                      .then_inc(added, 1)

            @block.scalar
            def _(act):
                for k in range(SLOTS):
                    act.wait_ge(added, 1 + 2 * k + 2)
                    nc.scalar.activation(hn[:, k], hn[:, k], ACT.Gelu_apprx_tanh).then_inc(slot_done, 1)


def glu_phase(core, hn):
    nc = core.nc

    def outcome(ph, acc, multiplied, drained):
        gate = ph.sb("gate", [P, N_TOK])
        gated, product_made = ph.sem("gated"), ph.sem("product_made")

        def two(ap):
            return ap.rearrange("p (h n) -> p h n", h=2)

        def takers(block):
            @block.scalar
            def _(act):
                with act.Fori(0, SLOTS) as i:
                    act.wait_ge(multiplied[1], 1 + i + 1)
                    act.wait_ge(drained[0], 1 + i)
                    act.nop(nofuse=True)
                    nc.scalar.activation(two(gate[:, :]), acc[1][:, :, 0:HALF], ACT.Sigmoid).then_inc(drained[1], 1)

            @block.vector
            def _(dve):
                with dve.Fori(0, SLOTS) as i:
                    dve.wait_ge(multiplied[0], 1 + i + 1)
                    dve.wait_ge(drained[1], 1 + i + 1)
                    nc.vector.tensor_tensor(two(gate[:, :]), acc[0][:, :, 0:HALF], two(gate[:, :]), ALU.mult)\
                      .then_inc(product_made, 1)
                    dve.wait_ge(product_made, 1 + i + 1)
                    h = core.hT[:, bass.ds(i, 1), :].rearrange("p a n -> p (a n)")
                    nc.vector.tensor_tensor(h, h, gate[:, :], ALU.add).then_inc(drained[0], 1)
        return takers

    dense_phase(core, "glu", core.dram["w_glu"], SLOTS, hn, outcome)


def store_phase(core, result, stored):
    nc = core.nc
    with nc.Block() as block:
        @block.sync
        def _(sp):
            sp.dma_start(core.dram["out"], result[:, :, N_META:]).then_inc(stored, 16)
            sp.wait_ge(stored, 16)



def features(a):
    return a.reshape(P, SLOTS, *a.shape[1:])


def column_tiles(w, columns, rows_are_features=True):
    rows = features(w) if rows_are_features else w.reshape(SLOTS, P, -1).transpose(1, 0, 2)
    return np.stack([rows[:, :, c] for c in columns])


def in_pairs(tiles):
    return np.ascontiguousarray(tiles.reshape(-1, 2, P, SLOTS, P).transpose(0, 2, 1, 3, 4))


def attention_bias(rpb):
    ci = np.arange(16)[:, None, None, None]
    r = np.arange(8)[None, :, None, None]
    cj = np.arange(32)[None, None, :, None]
    rk = np.arange(8)[None, None, None, :]
    out = np.zeros((8, 3, P, N_META + 2 * P), rpb.dtype)
    for kind, block in enumerate((0, 1, 3)):
        base = 8 * WIN_FIRST[block]
        c, ck = 16 * block + ci, base + cj
        start = np.clip(c - 8, 0, GRID_W - 16)
        inside = np.broadcast_to((ck >= start) & (ck < start + 16), (16, 8, 32, 8))
        dc = np.clip(ck - c + 15, 0, 30)
        dr = rk - r + 7
        spread = rpb[:, np.broadcast_to(dr, inside.shape), np.broadcast_to(dc, inside.shape)]
        spread = np.where(inside[None], spread, rpb.dtype.type(-1e30))
        out[:, kind, :, N_META:] = spread.reshape(8, P, 2 * P)
    return np.ascontiguousarray(out.reshape(N_PAIRS, 2, 3, P, -1).transpose(0, 3, 2, 1, 4))


def rwkv_layout(w):
    pairs = lambda a: a.reshape(N_PAIRS, P).T
    up = np.stack([np.concatenate([w["rwkv_w_up"][d], w["rwkv_a_up"][d]], axis=0) for d in range(2)]
                  + [w["rwkv_g_up"]])
    vec = [w["rwkv_w0"][0], w["rwkv_w0"][1], w["rwkv_a0"][0], w["rwkv_a0"][1], w["rwkv_k_k"], w["rwkv_k_a"],
           w["rwkv_r_k"].reshape(-1)]
    return {"mu": np.ascontiguousarray(w["rwkv_mu"].reshape(N_SHIFT, P).T),
            "rw_up": np.ascontiguousarray(up.reshape(3, P, N_PAIRS, P).transpose(2, 1, 0, 3)),
            "rw_vec": np.ascontiguousarray(np.stack([pairs(a) for a in vec], axis=-1)),
            "rw_ln": np.ascontiguousarray(np.stack([pairs(w["rwkv_lnx_g"]), pairs(w["rwkv_lnx_b"])], axis=-1))}


def route_consts():
    row = np.concatenate([np.arange(8, 0, -1), np.arange(N_EXPERTS) * CAP, np.arange(MAX_ROUNDS) * CAP])
    token = np.arange(P)[:, None] + P * np.arange(N_TILES)[None, :]
    consts = np.concatenate([np.tile(row, (P, 1)), token < N_TOK], axis=1).astype(np.float32)
    return {"route_consts": consts, "token_order": np.triu(np.ones((P, P), np.float32), 1),
            "token_numbers": token.astype(np.float32),
            "places": np.tile(np.arange(CAP, dtype=np.float32), (P, 1))}


def route_layout(w_group, b_group, w_expert, b_expert):
    w = np.concatenate([w_group, w_expert.transpose(1, 0, 2).reshape(D, N_EXPERTS)], axis=1)
    b = np.concatenate([b_group, b_expert.reshape(-1)])
    return np.ascontiguousarray(features(w)), np.ascontiguousarray(np.tile(b, (P, 1)))


def s5_layout(w):
    twice = lambda a: np.concatenate([a, a], axis=0)
    lam = [w["s5_lambda_re"], w["s5_lambda_im"], np.broadcast_to(w["s5_log_step"][..., None], (2, S5_GROUPS, S5_P))]
    lam = np.stack([twice(a.transpose(2, 0, 1).reshape(S5_P, -1)) for a in lam], axis=1)
    b = [w["s5_b_re"].transpose(1, 0, 2), w["s5_b_im"].transpose(1, 0, 2)]
    c = [w["s5_c_re"].transpose(3, 1, 0, 2), w["s5_c_im"].transpose(3, 1, 0, 2)]
    both = lambda x: np.ascontiguousarray(np.stack([np.concatenate([x[0], x[1]]), np.concatenate([x[1], x[0]])], axis=1))
    step = np.arange(P) // S5_CH
    masks = np.concatenate([step[:, None] <= step[None, :], step[:, None] >= step[None, :]], axis=1)
    return {"s5_lam": np.ascontiguousarray(lam), "s5_b": both(b), "s5_c": both(c),
            "s5_masks": masks.astype(np.float32), "s5_d": np.ascontiguousarray(w["s5_d"].reshape(P, SLOTS))}



def build_program(nc, dram):
    core = Core(nc, dram)

    def keep(name, shape):
        return nc.alloc_sbuf_tensor(name, shape, F32)

    core.hT = keep("hT", [P, SLOTS, N_TOK])
    core.gains = keep("gains", [P, N_GAINS, SLOTS])
    core.ones, core.ones_head, core.ident = (keep(name, [P, P]) for name in ("ones", "ones_head", "ident"))
    core.scratch = nc.dram_tensor("expert_rows", [N_EXPERTS * CAP, D], F32, kind="Internal").ap()
    core.hn_rows = nc.dram_tensor("token_rows", [N_TOK, D], F32, kind="Internal").ap()
    stored = nc.alloc_semaphore("result_stored")
    states = [P, SLOTS, N_TOK]
    setup_phase(core)
    with nc.sbuf_tensor("mix", states, F32) as mix:
        projected = ExitStack()
        raw = projected.enter_context(nc.sbuf_tensor("raw", [P, N_SHIFT, N_TOK + 2], F32, side="right"))
        with nc.sbuf_tensor("hn0", states, F32) as hn:
            norm_phase(core, 0, hn)
            with nc.sbuf_tensor("queries_keys", [P, 2 * N_PAIRS, N_TOK], F32) as qk, \
                    nc.sbuf_tensor("values", [P, 8, NA_WIDTH], F32) as values:
                query_key_phase(core, hn, qk)
                value_phase(core, hn, values)
                attention_phase(core, qk, values, mix)
            rwkv_projection_phase(core, hn, raw)
        rwkv(core, raw, projected.close, mix)
        output_projection_phase(core, mix)
    with nc.sbuf_tensor("hn1", states, F32) as hn:
        norm_phase(core, 1, hn)
        moe(core, 0, hn)
    with nc.sbuf_tensor("hn2", states, F32) as hn:
        norm_phase(core, 2, hn)
        s5(core, hn)
        glu_phase(core, hn)
    with nc.sbuf_tensor("hn3", states, F32) as hn:
        norm_phase(core, 3, hn)
        moe(core, 1, hn)
    with nc.sbuf_tensor("result", states, F32) as result:
        norm_phase(core, 4, result)
        store_phase(core, result, stored)


def lay_out(w):
    h = np.concatenate([w["meta_tokens"], w["x"][0]], axis=0)
    gains = [w["norm_mix"][0], w["norm_ffn"][0], w["norm_mix"][1], w["norm_ffn"][1], w["norm_final"]]
    w_in = w["mix_w_in"][0]
    run = lambda at: np.arange(at, at + P)
    qk = [run(part * NA_WIDTH + P * j) for j in range(N_PAIRS) for part in range(2)]
    slot = lambda m: SLOTS * np.arange(P) + m
    glu = [slot(m) + part * D for m in range(SLOTS) for part in range(2)]
    out = {"hT": np.ascontiguousarray(h.T.reshape(P, SLOTS, N_TOK)),
           "gains": np.ascontiguousarray(np.stack([g.reshape(P, SLOTS) for g in gains], axis=1)),
           "w_qk": in_pairs(column_tiles(w_in, qk)),
           "w_v": np.ascontiguousarray(features(w_in)[:, :, 2 * NA_WIDTH:3 * NA_WIDTH]),
           "w_rw": in_pairs(column_tiles(w_in, [run(3 * NA_WIDTH + P * j) for j in range(N_SHIFT)])),
           "bias": attention_bias(w["na_rpb"][0]),
           "w_out": in_pairs(column_tiles(w["mix_w_out"][0], [slot(m) for m in range(SLOTS)], rows_are_features=False)),
           "w_glu": in_pairs(column_tiles(w["s5_w_glu"][0], glu))}
    out.update(chunk_masks())
    out.update(rwkv_layout({k: a[0] for k, a in w.items() if k.startswith("rwkv")}))
    out.update(s5_layout({k: a[0] for k, a in w.items() if k.startswith("s5")}))
    out.update(route_consts())
    for layer in range(2):
        out[f"route_w{layer}"], out[f"route_b{layer}"] = route_layout(
            *[w[f"moe_{name}"][layer] for name in ("w_group", "b_group", "w_expert", "b_expert")])
    for name in ("moe_w1", "moe_w3", "moe_w2"):
        out[name] = w[name]
    return out


def kernel(**inputs):
    import concourse.bacc as bacc
    from concourse.bass_utils import run_bass_kernel_spmd

    nc = bacc.Bacc("TRN2", target_bir_lowering=False, num_devices=1)
    arrays, dram = {}, {}
    for name, a in lay_out({k: np.asarray(v) for k, v in inputs.items()}).items():
        a = np.ascontiguousarray(a)
        arrays[f"in_{name}"] = a
        dram[name] = nc.dram_tensor(f"in_{name}", a.shape, mybir.dt.from_np(a.dtype), kind="ExternalInput").ap()
    dram["out"] = nc.dram_tensor("out_states", [P, SLOTS, SEQ], F32, kind="ExternalOutput").ap()
    build_program(nc, dram)
    result = run_bass_kernel_spmd(nc, [arrays], core_ids=[0]).results[0]["out_states"]
    return np.ascontiguousarray(result.reshape(D, SEQ).T[None])
```
